# Optimizing a Trainium2 kernel written in Bass

```python
import jax, jax.numpy as jnp
from jax import lax
import numpy as np
import math

D_MODEL = 1024
BATCH = 1
SEQ = 256
DEPTH = 1

PLE_DIM = 256
MLA_HEADS = 8
QK_NOPE_DIM = 64
QK_ROPE_DIM = 32
V_HEAD_DIM = 64
Q_LORA_RANK = 384
KV_LORA_RANK = 256
ROPE_THETA = 10000.0
Q_BLOCK = 128
CONV_CHANNELS = 512
CONV_WIDTH = 31
MLA_WIDTH = MLA_HEADS * V_HEAD_DIM
D_MIX = MLA_WIDTH + CONV_CHANNELS
IN_PROJ_DIM = Q_LORA_RANK + KV_LORA_RANK + QK_ROPE_DIM + 2 * CONV_CHANNELS
D_FF = 2816
FFN_CONV_WIDTH = 3
NORM_EPS = 1e-6


def rms_norm(x, g):
    xf = x.astype(jnp.float32)
    y = xf * lax.rsqrt(jnp.mean(xf * xf, axis=-1, keepdims=True) + NORM_EPS)
    return (y * g.astype(jnp.float32)).astype(x.dtype)

def layer_norm(x, g, b):
    xf = x.astype(jnp.float32)
    mu = jnp.mean(xf, axis=-1, keepdims=True)
    xc = xf - mu
    y = xc * lax.rsqrt(jnp.mean(xc * xc, axis=-1, keepdims=True) + NORM_EPS)
    return (y * g.astype(jnp.float32) + b.astype(jnp.float32)).astype(x.dtype)

def causal_depthwise_conv(x, w, b):
    k = w.shape[0]
    out = lax.conv_general_dilated(
        x, w[:, None, :].astype(x.dtype), window_strides=(1,), padding=((k - 1, 0),),
        dimension_numbers=('NWC', 'WIO', 'NWC'), feature_group_count=x.shape[-1])
    return out + b.astype(x.dtype)

def apply_rope(x, cos, sin):
    x1, x2 = jnp.split(x, 2, axis=-1)
    return jnp.concatenate([x1 * cos - x2 * sin, x1 * sin + x2 * cos], axis=-1)

def causal_mla_attention(q_nope, q_rope, k_nope, k_rope, v):
    b, s, h, _ = q_nope.shape
    nb = s // Q_BLOCK
    scale = (QK_NOPE_DIM + QK_ROPE_DIM) ** -0.5
    k_idx = jnp.arange(s)

    def to_blocks(t):
        return jnp.moveaxis(t.reshape(b, nb, Q_BLOCK, *t.shape[2:]), 1, 0)

    def block(args):
        qn, qr, start = args
        sc = (jnp.einsum('bqhd,bkhd->bhqk', qn, k_nope, preferred_element_type=jnp.float32)
              + jnp.einsum('bqhr,bkr->bhqk', qr, k_rope, preferred_element_type=jnp.float32)) * scale
        q_idx = start + jnp.arange(Q_BLOCK)
        sc = jnp.where(k_idx[None, :] <= q_idx[:, None], sc, -jnp.inf)
        pr = jax.nn.softmax(sc, axis=-1).astype(v.dtype)
        return jnp.einsum('bhqk,bkhd->bqhd', pr, v)

    starts = jnp.arange(nb) * Q_BLOCK
    out = lax.map(block, (to_blocks(q_nope), to_blocks(q_rope), starts))
    return jnp.moveaxis(out, 0, 1).reshape(b, s, h * V_HEAD_DIM)

def hybrid_mixer(xn, cos, sin, w_in, g_q_a, w_q_b, g_kv_a, w_kv_b,
                 conv_w, conv_b, conv_ln_g, conv_ln_b, w_o):
    b, s, _ = xn.shape
    proj = xn @ w_in
    o1 = Q_LORA_RANK
    o2 = o1 + KV_LORA_RANK
    o3 = o2 + QK_ROPE_DIM
    q_a, kv_a, k_rope, conv_in = jnp.split(proj, [o1, o2, o3], axis=-1)
    q = (rms_norm(q_a, g_q_a) @ w_q_b).reshape(b, s, MLA_HEADS, QK_NOPE_DIM + QK_ROPE_DIM)
    q_nope, q_rope = jnp.split(q, [QK_NOPE_DIM], axis=-1)
    kv = (rms_norm(kv_a, g_kv_a) @ w_kv_b).reshape(b, s, MLA_HEADS, QK_NOPE_DIM + V_HEAD_DIM)
    k_nope, v = jnp.split(kv, [QK_NOPE_DIM], axis=-1)
    q_rope = apply_rope(q_rope, cos[:, :, None, :], sin[:, :, None, :])
    k_rope = apply_rope(k_rope, cos, sin)
    attn = causal_mla_attention(q_nope, q_rope, k_nope, k_rope, v)
    a, gate = jnp.split(conv_in, 2, axis=-1)
    c = a * jax.nn.sigmoid(gate)
    c = causal_depthwise_conv(c, conv_w, conv_b)
    c = jax.nn.silu(layer_norm(c, conv_ln_g, conv_ln_b))
    return jnp.concatenate([attn, c], axis=-1) @ w_o

def conv_gated_ffn(xn, w_gate, w_up, dw_w, dw_b, w_down):
    g = causal_depthwise_conv(xn @ w_gate, dw_w, dw_b)
    return (jax.nn.gelu(g, approximate=True) * (xn @ w_up)) @ w_down

def first_inputs(seed: int = 0) -> dict:
    key = jax.random.key(seed)
    ks = iter(jax.random.split(key, 40))

    def w(shape, fan_in):
        return jax.random.normal(next(ks), shape, jnp.float32) * fan_in ** -0.5

    def gain(shape):
        return 1.0 + 0.05 * jax.random.normal(next(ks), shape, jnp.float32)

    def bias(shape):
        return 0.01 * jax.random.normal(next(ks), shape, jnp.float32)

    L = DEPTH
    x = jax.random.normal(next(ks), (BATCH, SEQ, D_MODEL), jnp.float32)
    p = jax.random.normal(next(ks), (DEPTH, BATCH, SEQ, PLE_DIM), jnp.float32)
    positions = jnp.broadcast_to(jnp.arange(SEQ, dtype=jnp.int32)[None, :], (BATCH, SEQ))
    return {
        "x": x,
        "p": p,
        "positions": positions,
        "g_mix_pre": gain((L, D_MODEL)),
        "w_in": w((L, D_MODEL, IN_PROJ_DIM), D_MODEL),
        "g_q_a": gain((L, Q_LORA_RANK)),
        "w_q_b": w((L, Q_LORA_RANK, MLA_HEADS * (QK_NOPE_DIM + QK_ROPE_DIM)), Q_LORA_RANK),
        "g_kv_a": gain((L, KV_LORA_RANK)),
        "w_kv_b": w((L, KV_LORA_RANK, MLA_HEADS * (QK_NOPE_DIM + V_HEAD_DIM)), KV_LORA_RANK),
        "conv_w": w((L, CONV_WIDTH, CONV_CHANNELS), CONV_WIDTH),
        "conv_b": bias((L, CONV_CHANNELS)),
        "conv_ln_g": gain((L, CONV_CHANNELS)),
        "conv_ln_b": bias((L, CONV_CHANNELS)),
        "w_o": w((L, D_MIX, D_MODEL), D_MIX),
        "g_mix_post": gain((L, D_MODEL)),
        "g_ffn_pre": gain((L, D_MODEL)),
        "w_ffn_gate": w((L, D_MODEL, D_FF), D_MODEL),
        "w_ffn_up": w((L, D_MODEL, D_FF), D_MODEL),
        "ffn_dw_w": w((L, FFN_CONV_WIDTH, D_FF), FFN_CONV_WIDTH),
        "ffn_dw_b": bias((L, D_FF)),
        "w_ffn_down": w((L, D_FF, D_MODEL), D_FF),
        "g_ffn_post": gain((L, D_MODEL)),
        "w_ple_proj": w((L, PLE_DIM, D_MODEL), PLE_DIM),
        "g_ple": gain((L, D_MODEL)),
        "w_ple_gate": w((L, D_MODEL, D_MODEL), D_MODEL),
    }

def first_block(x, p, positions, g_mix_pre, w_in, g_q_a, w_q_b, g_kv_a, w_kv_b,
              conv_w, conv_b, conv_ln_g, conv_ln_b, w_o, g_mix_post, g_ffn_pre,
              w_ffn_gate, w_ffn_up, ffn_dw_w, ffn_dw_b, w_ffn_down, g_ffn_post,
              w_ple_proj, g_ple, w_ple_gate):
    inv_freq = ROPE_THETA ** (-jnp.arange(0, QK_ROPE_DIM, 2, dtype=jnp.float32) / QK_ROPE_DIM)
    ang = positions.astype(jnp.float32)[..., None] * inv_freq
    cos = jnp.cos(ang).astype(x.dtype)
    sin = jnp.sin(ang).astype(x.dtype)

    h = x
    for i in range(DEPTH):
        mix = hybrid_mixer(rms_norm(h, g_mix_pre[i]), cos, sin, w_in[i], g_q_a[i], w_q_b[i],
                           g_kv_a[i], w_kv_b[i], conv_w[i], conv_b[i], conv_ln_g[i],
                           conv_ln_b[i], w_o[i])
        h = h + rms_norm(mix, g_mix_post[i])
        ffn = conv_gated_ffn(rms_norm(h, g_ffn_pre[i]), w_ffn_gate[i], w_ffn_up[i],
                             ffn_dw_w[i], ffn_dw_b[i], w_ffn_down[i])
        h = h + rms_norm(ffn, g_ffn_post[i])
        e = rms_norm(p[i] @ w_ple_proj[i], g_ple[i])
        h = h + jax.nn.sigmoid(h @ w_ple_gate[i]) * e
    return h


DEPTH_2 = 2

CHUNK = 64
N_META = 16
DIFF_HEADS = 4
DIFF_HEAD_DIM = 64
DIFF_V_DIM = 2 * DIFF_HEAD_DIM
FOX_HEADS = 8
FOX_HEAD_DIM = 64
DIFF_QK_W = DIFF_HEADS * 2 * DIFF_HEAD_DIM
DIFF_V_W = DIFF_HEADS * DIFF_V_DIM
FOX_W = FOX_HEADS * FOX_HEAD_DIM
EVEN_IN_W = 2 * DIFF_QK_W + DIFF_V_W + 3 * FOX_W + FOX_HEADS
EVEN_MIX_W = DIFF_V_W + FOX_W
RET_HEADS = 4
RET_QK_DIM = D_MODEL // RET_HEADS
RET_V_DIM = 2 * RET_QK_DIM
RET_QK_W = RET_HEADS * RET_QK_DIM
RET_V_W = RET_HEADS * RET_V_DIM
RET_IN_W = 2 * RET_QK_W + 2 * RET_V_W
D_FF_2 = 4 * D_MODEL
N_EVEN = (DEPTH_2 + 1) // 2
N_ODD = DEPTH_2 // 2
DEEPNORM_ALPHA = (2 * DEPTH_2) ** 0.25
DEEPNORM_BETA = (8 * DEPTH_2) ** -0.25
LN_EPS = 1e-5
RMS_EPS = 1e-6


F32 = jnp.float32

def _chunk_id(pos):
    return (pos + CHUNK - N_META) // CHUNK

def _layer_norm(x, g, b):
    xf = x.astype(F32)
    mu = jnp.mean(xf, axis=-1, keepdims=True)
    var = jnp.mean(jnp.square(xf - mu), axis=-1, keepdims=True)
    y = (xf - mu) * lax.rsqrt(var + LN_EPS)
    return (y * g.astype(F32) + b.astype(F32)).astype(x.dtype)

def _rms_norm(x):
    xf = x.astype(F32)
    return xf * lax.rsqrt(jnp.mean(jnp.square(xf), axis=-1, keepdims=True) + RMS_EPS)

def _even_mixer(h, w_in, f_bias, lam_vecs, subln_g, w_out, layer_idx):
    B, L, _ = h.shape
    Lp = -(-L // Q_BLOCK) * Q_BLOCK
    nblk = Lp // Q_BLOCK
    proj = h @ w_in
    offs = [int(o) for o in np.cumsum([DIFF_QK_W, DIFF_QK_W, DIFF_V_W, FOX_W, FOX_W, FOX_W])]
    qa, ka, va, qb, kb, vb, fb = jnp.split(proj, offs, axis=-1)
    pad = ((0, 0), (0, Lp - L), (0, 0))
    qa, ka, va, qb, kb, vb = (jnp.pad(t, pad) for t in (qa, ka, va, qb, kb, vb))
    log_f = jnp.pad(jax.nn.log_sigmoid((fb + f_bias).astype(F32)), pad)
    cum_f = jnp.cumsum(log_f, axis=1).transpose(0, 2, 1)

    qa = qa.reshape(B, nblk, Q_BLOCK, DIFF_HEADS, 2, DIFF_HEAD_DIM).transpose(1, 0, 3, 4, 2, 5)
    ka = ka.reshape(B, Lp, DIFF_HEADS, 2, DIFF_HEAD_DIM).transpose(0, 2, 3, 1, 4)
    va = va.reshape(B, Lp, DIFF_HEADS, DIFF_V_DIM).transpose(0, 2, 1, 3)
    qb = qb.reshape(B, nblk, Q_BLOCK, FOX_HEADS, FOX_HEAD_DIM).transpose(1, 0, 3, 2, 4)
    kb = kb.reshape(B, Lp, FOX_HEADS, FOX_HEAD_DIM).transpose(0, 2, 1, 3)
    vb = vb.reshape(B, Lp, FOX_HEADS, FOX_HEAD_DIM).transpose(0, 2, 1, 3)
    cq = cum_f.reshape(B, FOX_HEADS, nblk, Q_BLOCK).transpose(2, 0, 1, 3)

    lam_init = 0.8 - 0.6 * math.exp(-0.3 * layer_idx)
    lv = lam_vecs.astype(F32)
    lam = jnp.exp(jnp.sum(lv[0] * lv[1])) - jnp.exp(jnp.sum(lv[2] * lv[3])) + lam_init
    slopes = 2.0 ** (-8.0 * jnp.arange(1, DIFF_HEADS + 1, dtype=F32) / DIFF_HEADS)
    scale_a = DIFF_HEAD_DIM ** -0.5
    scale_b = FOX_HEAD_DIM ** -0.5
    k_pos = jnp.arange(Lp)
    k_chunk = _chunk_id(k_pos)
    q_pos_blk = k_pos.reshape(nblk, Q_BLOCK)

    def one_block(args):
        qa_i, qb_i, cq_i, q_pos = args
        dist = jnp.abs(q_pos[:, None] - k_pos[None, :]).astype(F32)
        chunk_vis = k_chunk[None, :] <= _chunk_id(q_pos)[:, None]
        frame_vis = k_pos[None, :] <= q_pos[:, None]
        s_a = jnp.einsum('bhmqd,bhmkd->bhmqk', qa_i, ka).astype(F32) * scale_a \
            - slopes[:, None, None, None] * dist
        p_a = jax.nn.softmax(jnp.where(chunk_vis, s_a, -jnp.inf), axis=-1)
        p_diff = p_a[:, :, 0] - lam * p_a[:, :, 1]
        o_a = jnp.einsum('bhqk,bhkd->bhqd', p_diff.astype(va.dtype), va)
        s_b = jnp.einsum('bhqd,bhkd->bhqk', qb_i, kb).astype(F32) * scale_b \
            + cq_i[..., :, None] - cum_f[:, :, None, :]
        p_b = jax.nn.softmax(jnp.where(frame_vis, s_b, -jnp.inf), axis=-1)
        o_b = jnp.einsum('bhqk,bhkd->bhqd', p_b.astype(vb.dtype), vb)
        return o_a, o_b

    o_a, o_b = lax.map(one_block, (qa, qb, cq, q_pos_blk))
    o_a = o_a.transpose(1, 0, 3, 2, 4).reshape(B, Lp, DIFF_HEADS, DIFF_V_DIM)[:, :L]
    o_a = (_rms_norm(o_a) * subln_g.astype(F32) * (1.0 - lam_init)).astype(h.dtype)
    o_b = o_b.transpose(1, 0, 3, 2, 4).reshape(B, Lp, FOX_W)[:, :L]
    o = jnp.concatenate([o_a.reshape(B, L, DIFF_V_W), o_b.astype(h.dtype)], axis=-1)
    return o @ w_out

def _retention(h, w_in, w_out):
    B, L, _ = h.shape
    proj = h @ w_in
    q, k, v, g = jnp.split(proj, [RET_QK_W, 2 * RET_QK_W, 2 * RET_QK_W + RET_V_W], axis=-1)
    k = k * RET_QK_DIM ** -0.5
    lpad = (-N_META) % CHUNK
    Lr = L + lpad
    nc = Lr // CHUNK

    def to_chunks(t, d):
        t = jnp.pad(t, ((0, 0), (lpad, 0), (0, 0)))
        return t.reshape(B, nc, CHUNK, RET_HEADS, d).transpose(1, 0, 3, 2, 4)

    qc, kc, vc = to_chunks(q, RET_QK_DIM), to_chunks(k, RET_QK_DIM), to_chunks(v, RET_V_DIM)
    log_gamma = jnp.log1p(-(2.0 ** (-5.0 - jnp.arange(RET_HEADS, dtype=F32))))
    idx = jnp.arange(CHUNK, dtype=F32)
    intra = jnp.exp(log_gamma[:, None, None] * jnp.abs(idx[:, None] - idx[None, :]))
    q_dec = jnp.exp(log_gamma[:, None] * (idx + 1.0))[:, :, None]
    k_dec = jnp.exp(log_gamma[:, None] * (CHUNK - 1.0 - idx))[:, :, None]
    c_dec = jnp.exp(log_gamma * CHUNK)[:, None, None]

    def step(state, inp):
        q_i, k_i, v_i = inp
        scores = jnp.einsum('bhid,bhjd->bhij', q_i, k_i) * intra
        o = jnp.einsum('bhij,bhje->bhie', scores, v_i) \
            + jnp.einsum('bhid,bhde->bhie', q_i * q_dec, state)
        state = c_dec * state + jnp.einsum('bhjd,bhje->bhde', k_i * k_dec, v_i)
        return state, o

    s0 = jnp.zeros((B, RET_HEADS, RET_QK_DIM, RET_V_DIM), F32)
    _, o = lax.scan(step, s0, (qc, kc, vc))
    o = o.transpose(1, 0, 3, 2, 4).reshape(B, Lr, RET_HEADS, RET_V_DIM)[:, lpad:]
    o = _rms_norm(o).reshape(B, L, RET_V_W).astype(h.dtype)
    y = jax.nn.silu(g) * o
    return y @ w_out

def _sq_relu_mlp(h, w1, w2):
    return jnp.square(jax.nn.relu(h @ w1)) @ w2

def second_inputs(seed: int = 0) -> dict:
    key = jax.random.key(seed)
    ks = jax.random.split(key, 13)

    def nrm(k, shape, scale):
        return jax.random.normal(k, shape, F32) * scale

    beta = DEEPNORM_BETA
    x = nrm(ks[0], (BATCH, SEQ, D_MODEL), 1.0)
    meta_tokens = nrm(ks[1], (N_META, D_MODEL), 1.0)
    even_col_scale = jnp.concatenate([
        jnp.ones((2 * DIFF_QK_W,), F32), jnp.full((DIFF_V_W,), beta, F32),
        jnp.ones((2 * FOX_W,), F32), jnp.full((FOX_W,), beta, F32),
        jnp.ones((FOX_HEADS,), F32)])
    even_w_in = nrm(ks[2], (N_EVEN, D_MODEL, EVEN_IN_W), D_MODEL ** -0.5) * even_col_scale
    even_f_bias = jnp.linspace(1.0, 6.0, FOX_HEADS, dtype=F32) + nrm(ks[3], (N_EVEN, FOX_HEADS), 0.1)
    diff_lambda = nrm(ks[4], (N_EVEN, 4, DIFF_HEAD_DIM), 0.1)
    diff_subln_g = 1.0 + nrm(ks[5], (N_EVEN, DIFF_V_DIM), 0.02)
    even_w_out = nrm(ks[6], (N_EVEN, EVEN_MIX_W, D_MODEL), EVEN_MIX_W ** -0.5 * beta)
    ret_col_scale = jnp.concatenate([
        jnp.ones((2 * RET_QK_W,), F32), jnp.full((RET_V_W,), beta, F32), jnp.ones((RET_V_W,), F32)])
    ret_w_in = nrm(ks[7], (N_ODD, D_MODEL, RET_IN_W), D_MODEL ** -0.5) * ret_col_scale
    ret_w_out = nrm(ks[8], (N_ODD, RET_V_W, D_MODEL), RET_V_W ** -0.5 * beta)
    ln_g = 1.0 + nrm(ks[9], (DEPTH_2, 2, D_MODEL), 0.02)
    ln_b = nrm(ks[10], (DEPTH_2, 2, D_MODEL), 0.02)
    ffn_w1 = nrm(ks[11], (DEPTH_2, D_MODEL, D_FF_2), D_MODEL ** -0.5 * beta)
    ffn_w2 = nrm(ks[12], (DEPTH_2, D_FF_2, D_MODEL), D_FF_2 ** -0.5 * beta)
    return {"x": x, "meta_tokens": meta_tokens, "even_w_in": even_w_in, "even_f_bias": even_f_bias,
            "diff_lambda": diff_lambda, "diff_subln_g": diff_subln_g, "even_w_out": even_w_out,
            "ret_w_in": ret_w_in, "ret_w_out": ret_w_out, "ln_g": ln_g, "ln_b": ln_b,
            "ffn_w1": ffn_w1, "ffn_w2": ffn_w2}

def second_block(x, meta_tokens, even_w_in, even_f_bias, diff_lambda, diff_subln_g, even_w_out,
              ret_w_in, ret_w_out, ln_g, ln_b, ffn_w1, ffn_w2):
    B = x.shape[0]
    meta = jnp.broadcast_to(meta_tokens[None].astype(x.dtype), (B, N_META, D_MODEL))
    h = jnp.concatenate([meta, x], axis=1)
    for layer in range(DEPTH_2):
        i = layer // 2
        if layer % 2 == 0:
            mix = _even_mixer(h, even_w_in[i], even_f_bias[i], diff_lambda[i], diff_subln_g[i],
                              even_w_out[i], layer)
        else:
            mix = _retention(h, ret_w_in[i], ret_w_out[i])
        h = _layer_norm(DEEPNORM_ALPHA * h + mix, ln_g[layer, 0], ln_b[layer, 0])
        h = _layer_norm(DEEPNORM_ALPHA * h + _sq_relu_mlp(h, ffn_w1[layer], ffn_w2[layer]),
                        ln_g[layer, 1], ln_b[layer, 1])
    return h[:, N_META:, :]


def setup_inputs(seed=0):
    out = dict(first_inputs(seed))
    for name, value in second_inputs(seed + 1).items():
        if name != "x":
            out[name + "_2"] = value
    return out


def reference(
    x, p, positions, g_mix_pre, w_in, g_q_a, w_q_b, g_kv_a, w_kv_b, conv_w, conv_b, conv_ln_g,
    conv_ln_b, w_o, g_mix_post, g_ffn_pre, w_ffn_gate, w_ffn_up, ffn_dw_w, ffn_dw_b, w_ffn_down,
    g_ffn_post, w_ple_proj, g_ple, w_ple_gate, meta_tokens_2, even_w_in_2, even_f_bias_2,
    diff_lambda_2, diff_subln_g_2, even_w_out_2, ret_w_in_2, ret_w_out_2, ln_g_2, ln_b_2,
    ffn_w1_2, ffn_w2_2,
):
    x = first_block(
        x, p, positions, g_mix_pre, w_in, g_q_a, w_q_b, g_kv_a, w_kv_b, conv_w, conv_b,
        conv_ln_g, conv_ln_b, w_o, g_mix_post, g_ffn_pre, w_ffn_gate, w_ffn_up, ffn_dw_w,
        ffn_dw_b, w_ffn_down, g_ffn_post, w_ple_proj, g_ple, w_ple_gate,
    )
    return second_block(
        x, meta_tokens_2, even_w_in_2, even_f_bias_2, diff_lambda_2, diff_subln_g_2,
        even_w_out_2, ret_w_in_2, ret_w_out_2, ln_g_2, ln_b_2, ffn_w1_2, ffn_w2_2,
    )


_drawn_inputs = setup_inputs


def setup_inputs(seed=0):
    import zlib

    import numpy as np

    out = dict(_drawn_inputs(seed))
    spreads = {}
    factors = {'g_q_a': 4.571,
     'g_kv_a': 3.035,
     'conv_b': 3.192,
     'conv_ln_b': 17.382,
     'ffn_dw_b': 8.0,
     'g_ple': 3.215,
     'diff_lambda_2': 5.55,
     'diff_subln_g_2': 35.53,
     'conv_ln_g': 2.726}
    for name, (base, spread) in spreads.items():
        noise = np.random.default_rng([zlib.crc32(name.encode()), seed]).standard_normal(out[name].shape)
        drawn = base * np.exp(spread * noise) if base else spread * noise
        out[name] = __import__('jax').numpy.asarray(drawn.astype(out[name].dtype))
    for name, factor in factors.items():
        out[name] = (out[name] * factor).astype(out[name].dtype)
    return out
```

```python
from contextlib import ExitStack

import numpy as np

import concourse.bass as bass
from concourse import mybir

F32 = mybir.dt.float32
F32R = mybir.dt.float32r
I32 = mybir.dt.int32
ALU = mybir.AluOpType
ACT = mybir.ActivationFunctionType
AX = mybir.AxisListType

P = 128
D = 1024
KD = D // P
N1 = 256
META = 16
N2 = N1 + META
HEADS, NOPE, ROPE, VDIM = 8, 64, 32, 64
QHEAD = NOPE + ROPE
QLORA, KVLORA = 384, 256
CONV_C, TAPS = 512, 31
POOL_TAPS = 16
CT = CONV_C // P
FF, FT = 2816, 2816 // P
PLE = 256
FF2, FT2 = 4096, 4096 // P
RH, RQK, RV = 4, 256, 512
CHUNK = 64
EPS1, LN_EPS, RMS_EPS = 1e-6, 1e-5, 1e-6
ALPHA = 4.0 ** 0.25
LAM_INIT = 0.2
SC1 = QHEAD ** -0.5
SC2 = 64 ** -0.5
NEG = -1.0e30
TOK = [(0, 80), (80, 128), (208, 64)]
SEEN = [80, 208, 272]
CH = 2048

STAGES = [("qkv_in", 3, 3), ("conv_in", 4, 4), ("q", 2, 4), ("kv", 1, 5), ("mix_out", 4, 4), ("ple", 1, 4),
          ("gate_up", 22, 22), ("down", 12, 4), ("ple_gate", 4, 4), ("even_qk", 8, 8), ("even_v", 4, 4),
          ("even_out", 4, 4), ("ffn_up0", 16, 16), ("ffn_down0", 16, 4), ("ret_qk", 8, 8), ("ret_v", 8, 8),
          ("ret_g", 8, 8), ("ret_out", 8, 4), ("ffn_up1", 16, 16), ("ffn_down1", 16, 4)]
C0, P0, E0, PER = {}, {}, {}, {}
CHUNK_END = []
_p = _e = 0
for _name, _nc, _np in STAGES:
    C0[_name], P0[_name], E0[_name], PER[_name] = len(CHUNK_END), _p, _e, max(1, _nc // _np)
    _n = max(_nc, _np)
    CHUNK_END += [_e + (_n * (j + 1)) // _nc if _name != "kv" else _e + _n for j in range(_nc)]
    _p, _e = _p + _np, _e + _n
CHUNKS = len(CHUNK_END)

ROWS1 = [("g_mix_post", 8), ("g_ffn_pre", 8), ("g_ffn_post", 8), ("g_ple", 8), ("ln_g_2", 32), ("ln_b_2", 32)]
ROWS2 = [("ffn_dw_w", 66), ("ffn_dw_b", 22), ("conv_b", 4), ("conv_ln_g", 4), ("conv_ln_b", 4), ("g_q_a", 3), ("g_kv_a", 2),
         ("diff_subln_g_2", 1)]


def starts(rows):
    at, out = 0, {}
    for name, n in rows:
        out[name] = at
        at += n
    return out, at


R1AT, R1N = starts(ROWS1)
R2AT, R2N = starts(ROWS2)

UNITS = [(t, True, h, m) for t in range(3) for h in range(4) for m in range(2)] + \
        [(t, False, h, 0) for t in range(3) for h in range(8)]
OUTS = [i for i, (t, d, h, m) in enumerate(UNITS) if not d or m == 1]
ORDER = {i: n for n, i in enumerate(OUTS)}


class Count:

    def __init__(self, n=0):
        self.n = n

    def up(self, by=1):
        self.n = self.n + by
        return self.n


def wait(eng, sem, value):
    if not isinstance(value, int) or value > 0:
        eng.wait_ge(sem, value)


def repeat(eng, turns, body):
    body(0)
    with eng.Fori(1, turns) as i:
        body(i)


def is_first(i):
    return isinstance(i, int) and i == 0


def at(i, n=1):
    return bass.ds(i, n)


def build(nc, a, out):
    with ExitStack() as ctx:
        def sb(name, shape, dt=F32):
            return ctx.enter_context(nc.sbuf_tensor(name, shape, dt))

        def sem(name):
            return ctx.enter_context(nc.semaphore(name))

        raw = sb("raw", [P, 2, CH])
        whi = sb("whi", [P, 2, CH], F32R)
        wlo = sb("wlo", [P, 2, CH], F32R)
        xh = sb("xh", [P, KD, N2], F32R)
        xl = sb("xl", [P, KD, N2], F32R)
        h = sb("h", [P, KD, N2])
        y = sb("y", [P, KD, N2])
        e_mem = sb("e_mem", [P, KD * N1])
        e = e_mem[:, :].rearrange("p (k n) -> p k n", k=KD)
        rw = e_mem[:, 0:4 * N2].rearrange("p (k n) -> p k n", k=4)
        sq = sb("sq", [P, 2, N2])
        acc1 = sb("acc1", [P, N2])
        acc2 = sb("acc2", [P, N2])
        rstd = sb("rstd", [P, 3, N2])
        lnv = sb("lnv", [P, N2])
        mu = sb("mu", [P, N2])
        musq = sb("musq", [P, N2])
        var = sb("var", [P, N2])
        ta = sb("ta", [P, 2, N2])
        tb = sb("tb", [P, 2, N2])
        b_col = sb("b_col", [P, 4])
        ra = sb("ra", [P, 4, N2])
        fa = sb("fa", [P, 4, N2])
        ident = sb("ident", [P, P])
        ones = sb("ones", [P, P])
        rot = sb("rot", [QHEAD, QHEAD])
        ones_row = sb("ones_row", [8, N2])
        eps = sb("eps", [P, 3])
        g_col = sb("g_col", [P, KD])
        col1 = sb("col1", [P, R1N])
        col2 = sb("col2", [P, R2N])
        lam_rows = sb("lam_rows", [1, 4 * 64])
        lam_s = sb("lam_s", [1, 8])
        neg_lam = sb("neg_lam", [P, 1])
        wf = sb("wf", [P, KD, 8])
        f_bias = sb("f_bias", [8, 1])
        small = sb("small", [P, 64, 4])
        arena0 = 512 * ((nc.sbuf_base + 511) // 512)

        class Arena:
            def __init__(self):
                self.at = arena0

            def __call__(self, name, shape, dt=F32):
                size = 4 * int(np.prod(shape[1:]))
                t = nc.alloc_sbuf_tensor_at(name, shape, dt, offset=self.at)
                self.at += 32 * ((size + 31) // 32)
                return t

        m1 = Arena()
        xt = m1("xt", [P, 2, D])
        qt = nc.alloc_sbuf_tensor_at("qt", [P, HEADS, N1], F32, offset=arena0)
        g_rows = m1("g_rows", [KD, P])
        rows1 = m1("rows1", [R1N, P])
        rows2 = m1("rows2", [R2N, P])
        meta_rows = m1("meta_rows", [META, D])
        pt = m1("pt", [P, 2, PLE])
        ph = m1("ph", [P, 2, N1], F32R)
        pl = m1("pl", [P, 2, N1], F32R)
        qkv = m1("qkv", [P, 6, N1])
        sq6 = m1("sq6", [P, 5, N1])
        conv_in = m1("conv_in", [P, CT, TAPS - 1 + N1])
        cv = m1("cv", [P, CT, N1])
        conv_t = m1("conv_t", [P, 2, N1])
        qxh = m1("qxh", [P, 5, N1], F32R)
        qxl = m1("qxl", [P, 5, N1], F32R)
        cw_rows = m1("cw_rows", [TAPS, CONV_C])
        cw = m1("cw", [P, CT, TAPS])
        pos_i = m1("pos_i", [QHEAD, N1], I32)
        ang = m1("ang", [QHEAD, 6, N1])
        freq = m1("freq", [QHEAD, 1])
        mask1 = m1("mask1", [P, N1])
        kt_ = m1("kt", [P, HEADS, N1])
        v1 = m1("v1", [P, 2, HEADS * VDIM])
        lr = nc.alloc_sbuf_tensor_at("lr", [P, 2, N1], F32, offset=m1.at)
        s1 = m1("s1", [P, 2, N1])
        p1 = m1("p1", [P, 4, N1])
        pt1 = m1("pt1", [P, 2, 2, P])
        rope_t = m1("rope_t", [QHEAD, 2, 2 * N1])
        f1 = Arena()
        fh = f1("fh", [P, FT2, N2], F32R)
        fl = f1("fl", [P, FT2, N2], F32R)
        xr_at = f1.at
        xrh = f1("xrh", [P, KD, N2 + 2], F32R)
        xrl = f1("xrl", [P, KD, N2 + 2], F32R)
        gt = nc.alloc_sbuf_tensor_at("gt", [P, 2, 2 + N1], F32, offset=xr_at)
        e1 = Arena()
        qk = e1("qk", [P, 16, N2])
        ve = e1("ve", [P, 3, 1024])
        fg = e1("fg", [8, 4, N2])
        pt2 = e1("pt2", [P, 2, 3, P])
        alibi = e1("alibi", [P, 4, 3, N2])
        mask2 = e1("mask2", [P, 3, N2])
        s2 = e1("s2", [P, 2, N2])
        p2 = e1("p2", [P, 4, N2])
        oa = e1("oa", [P, 4, N2])
        oasq = e1("oasq", [P, 4, N2])
        r1 = Arena()
        rqk = r1("rqk", [P, RH, 4, N2])
        r2_at = r1.at
        rv = r1("rv", [P, 3, RH * RV])
        rs = r1("rs", [P, 2, 3, N2])
        rsq = r1("rsq", [P, 2, N2])
        r_rstd = r1("r_rstd", [P, N2])
        decay = r1("decay", [P, 4, 3, N2])
        r2 = Arena()
        r2.at = r2_at
        gh = r2("gh", [P, 16, N2], F32R)
        gl = r2("gl", [P, 16, N2], F32R)
        otok = nc.alloc_sbuf_tensor_at("otok", [P, 2, D], F32, offset=arena0)
        for area in (m1, f1):
            assert area.at <= nc.sbuf_usable_end, (area.at, nc.sbuf_usable_end)
        for area in (e1, r1, r2):
            assert area.at <= xr_at, (area.at, xr_at)

        ps = [ctx.enter_context(nc.psum_tensor(f"ps{b}", [P, 512], F32)) for b in range(8)]

        raw_landed = [sem("raw_landed0"), sem("raw_landed1")]
        w_hi_ready, w_lo_ready = sem("w_hi_ready"), sem("w_lo_ready")
        mm_done = sem("mm_done")
        ident_in, g_in, rows1_in, x_in, small_in, const_in, table_in, decay_in, pos_in = sem("ident_in"), sem("g_in"), sem("rows1_in"), sem("x_in"), sem("small_in"), sem("const_in"), sem("table_in"), sem("decay_in"), sem("pos_in")
        set_up, cols_t, cols_ready = sem("set_up"), sem("cols_t"), sem("cols_ready")
        xt_done, meta_done, meta_ready, pt_done, p_hi, p_ready = sem("xt_done"), sem("meta_done"), sem("meta_ready"), sem("pt_done"), sem("p_hi"), sem("p_ready")
        tile_ready, sq_ready, acc_ready, stat_ready, rstd_ready = sem("tile_ready"), sem("sq_ready"), sem("acc_ready"), sem("stat_ready"), sem("rstd_ready")
        mu_ready, var_ready, sub_ready, norm_ready, hn_ready, post_ready, h_ready = (sem(n) for n in ("mu_ready", "var_ready", "sub_ready", "norm_ready", "hn_ready", "post_ready", "h_ready"))
        gb_hi, raw_sub, raw_out, raw_ready = sem("gb_hi"), sem("raw_sub"), sem("raw_out"), sem("raw_ready")
        xh_ready, x_ready = sem("xh_ready"), sem("x_ready")
        dve_chain, act_chain, pool_chain = sem("dve_chain"), sem("act_chain"), sem("pool_chain")
        ang_ready, trig_ready = sem("ang_ready"), sem("trig_ready")
        g_scaled, g_sig, conv_in_ready = sem("g_scaled"), sem("g_sig"), sem("conv_in_ready")
        e_copied, e_ready, conv_step2 = sem("e_copied"), sem("e_ready"), sem("conv_step2")
        conv_step, csq_ready, cstat_ready, cmu_ready, cvar_ready, crstd_ready = sem("conv_step"), sem("csq_ready"), sem("cstat_ready"), sem("cmu_ready"), sem("cvar_ready"), sem("crstd_ready")
        cn_ready, silu_ready, c_hi, c_ready = sem("cn_ready"), sem("silu_ready"), sem("c_hi"), sem("c_ready")
        qkv_ready, sq6_ready, lstat_ready, lrstd_ready, ln_ready, krot_done, krope_ready = sem("qkv_ready"), sem("sq6_ready"), sem("lstat_ready"), sem("lrstd_ready"), sem("ln_ready"), sem("krot_done"), sem("krope_ready")
        q_ready, qrot_done, qrope_ready, k_ready, v_ready = sem("q_ready"), sem("qrot_done"), sem("qrope_ready"), sem("k_ready"), sem("v_ready")
        s_done, max_ready, bias_ready, p_exp, pn_ready, t_done, pT_ready, pv_done, o_hi, o_ready = (sem(n) for n in ("s_done", "max_ready", "bias_ready", "p_exp", "pn_ready", "t_done", "pT_ready", "pv_done", "o_hi", "o_ready"))
        u_s_done, u_max, u_bias, u_exp, u_pn, u_t_done, u_pT, u_pv, u_ohi, u_o = (sem(n) for n in ("u_s_done", "u_max", "u_bias", "u_exp", "u_pn", "u_t_done", "u_pT", "u_pv", "u_ohi", "u_o"))
        gv_scaled, t0_ready, t1_ready, taps_ready, ge_ready, f_mul, f_hi, f_ready = (sem(n) for n in ("gv_scaled", "t0_ready", "t1_ready", "taps_ready", "ge_ready", "f_mul", "f_hi", "f_ready"))
        sig_ready = sem("sig_ready")
        qk_ready, ve_ready, fb_done, fz_ready, fl_ready, cum_ready = (sem(n) for n in ("qk_ready", "ve_ready", "fb_done", "fz_ready", "fl_ready", "cum_ready"))
        lam_sum, lam_exp, lam_one, lam_done, lam_ready = (sem(n) for n in ("lam_sum", "lam_exp", "lam_one", "lam_done", "lam_ready"))
        oasq_ready, oastat, oarstd, oan, oa_hi, oa_lo = (sem(n) for n in ("oasq_ready", "oastat", "oarstd", "oan", "oa_hi", "oa_lo"))
        relu_ready = sem("relu_ready")
        rqk_ready, rv_ready, rs_done, rs_ready, ro_done, ro_ready, rsq_ready, rstat, r_rstd_ready, ron_ready = (sem(n) for n in ("rqk_ready", "rv_ready", "rs_done", "rs_ready", "ro_done", "ro_ready", "rsq_ready", "rstat", "r_rstd_ready", "ron_ready"))
        silu2_ready, y_mul, y_hi, y_ready = (sem(n) for n in ("silu2_ready", "y_mul", "y_hi", "y_ready"))
        ot_done, ot_ready, stored = sem("ot_done"), sem("ot_ready"), sem("stored")

        def c1(name, k):
            return col1[:, R1AT[name] + k:R1AT[name] + k + 1]

        def c2(name, k):
            return col2[:, R2AT[name] + k:R2AT[name] + k + 1]

        def f32(ap):
            return ap.bitcast(F32)


        S_X, S_MIX, S_PRE, S_E, S_FFN, S_LN = 0, 1, 2, 3, 4, 5
        TILES = {S_X: 0, S_MIX: KD, S_PRE: 2 * KD, S_FFN: 3 * KD}
        TILES.update({S_LN + j: (4 + j) * KD for j in range(4)})
        X_A, X_QKV, X_FFN, X_PLE, X_B, X_LN0, X_LN1, X_RET, X_LN2 = 0, 8, 13, 21, 29, 37, 45, 53, 61
        ALL, LAST = slice(0, N2), slice(META, N2)

        RET_TILES = [(0,), (1, 2), (3,), (4, 5), (6,), (7,), (), ()]

        def size(cols):
            return cols.stop - cols.start

        block = ctx.enter_context(nc.Block())

        @block.sync
        def _(sp):
            sp.dma_start(ident[:], a["c_ident"]).then_inc(ident_in, 16)
            sp.dma_start(xt[:, 0, :], a["x"][0, 0:P, :]).then_inc(x_in, 16)
            sp.dma_start(xt[:, 1, :], a["x"][0, P:2 * P, :]).then_inc(x_in, 16)

            def load(c, slot, first, second):
                wait(sp, w_lo_ready, 2 * (c - 1))
                for dst, src in (first, second):
                    sp.dma_start(dst, src).then_inc(raw_landed[slot], 16)

            def view(slot, kt, n):
                return raw[:, slot, 0:kt * n].rearrange("p (k n) -> p k n", k=kt)

            def rows(w, kt):
                return w.rearrange("(k p) n -> p k n", k=kt)

            def columns(c, slot, w, kt, col, n=256):
                half = (kt + 1) // 2
                d, s = view(slot, kt, n), rows(w, kt)[:, :, at(col, n)]
                load(c, slot, (d[:, 0:half], s[:, 0:half]), (d[:, half:kt], s[:, half:kt]))

            def loop(name, count, w, kt):
                c = C0[name]

                def turn(i):
                    for u in range(2):
                        columns(c + 2 * i + u, (c + u) % 2, w, kt, 256 * (2 * i + u))

                repeat(sp, count // 2, turn)

            def deep(name, w, depth):
                c = C0[name]
                kts = [min(8, depth - 8 * j) for j in range((depth + 7) // 8)]
                n = len(kts)

                def turn(i):
                    for u in range(2):
                        for j, kt in enumerate(kts):
                            k = n * u + j
                            columns(c + 2 * n * i + k, (c + k) % 2, w[8 * j * P:(8 * j + kt) * P, :], kt, 256 * (2 * i + u))

                repeat(sp, 2, turn)

            w_in = a["w_in"][0]
            o3 = QLORA + KVLORA + ROPE
            for j in range(3):
                c = C0["qkv_in"] + j
                columns(c, c % 2, w_in, KD, 256 * j, 256 if j < 2 else o3 - 512)
            for m in range(CT):
                c = C0["conv_in"] + m
                d, s = view(c % 2, KD, 256), rows(w_in, KD)
                load(c, c % 2, (d[:, :, 0:P], s[:, :, o3 + P * m:o3 + P * m + P]),
                     (d[:, :, P:2 * P], s[:, :, o3 + CONV_C + P * m:o3 + CONV_C + P * m + P]))
            for j in range(2):
                c = C0["q"] + j
                columns(c, c % 2, a["w_q_b"][0], 3, 4 * QHEAD * j, 4 * QHEAD)
            columns(C0["kv"], C0["kv"] % 2, a["w_kv_b"][0], 2, 0, D)
            loop("mix_out", 4, a["w_o"][0], KD)
            columns(C0["ple"], C0["ple"] % 2, a["w_ple_proj"][0], 2, 0, D)

            def gate_up(i):
                for u in range(2):
                    c = C0["gate_up"] + u
                    d, col = view(c % 2, KD, 256), at(P * (2 * i + u), P)
                    load(c + 2 * i, c % 2, (d[:, :, 0:P], rows(a["w_ffn_gate"][0], KD)[:, :, col]),
                         (d[:, :, P:2 * P], rows(a["w_ffn_up"][0], KD)[:, :, col]))

            repeat(sp, FT // 2, gate_up)
            deep("down", a["w_ffn_down"][0], FT)
            loop("ple_gate", 4, a["w_ple_gate"][0], KD)
            ew = a["even_w_in_2"][0]
            for j, col in enumerate([0, 256, 512, 768, 1536, 1792, 2048, 2304]):
                c = C0["even_qk"] + j
                columns(c, c % 2, ew, KD, col)
            for j, col in enumerate([1024, 1280, 2560, 2816]):
                c = C0["even_v"] + j
                columns(c, c % 2, ew, KD, col)
            loop("even_out", 4, a["even_w_out_2"][0], KD)
            loop("ffn_up0", 16, a["ffn_w1_2"][0], KD)
            deep("ffn_down0", a["ffn_w2_2"][0], FT2)
            rw = a["ret_w_in_2"][0]
            loop("ret_qk", 8, rw[:, 0:2048], KD)
            loop("ret_v", 8, rw[:, 2048:4096], KD)
            loop("ret_g", 8, rw[:, 4096:6144], KD)
            deep("ret_out", a["ret_w_out_2"][0], 16)
            loop("ffn_up1", 16, a["ffn_w1_2"][1], KD)
            deep("ffn_down1", a["ffn_w2_2"][1], FT2)
            for n in range(4):
                half, t = n // 2, n % 2
                cols = slice(512 * half, 512 * half + 512)
                sp.wait_ge(ot_ready, n + 1)
                sp.dma_start(out[0, P * t:P * t + P, cols], otok[:, t, cols]).then_inc(stored, 16)
            sp.wait_ge(stored, 64)

        @block.gpsimd
        def _(pool):
            chain = Count()

            def link(ins):
                ins.then_inc(pool_chain, 1)
                pool.wait_ge(pool_chain, chain.up())

            nc.gpsimd.memset(ones[:], 1.0).then_inc(set_up, 1)
            nc.gpsimd.memset(ones_row[:], 1.0).then_inc(set_up, 1)
            nc.gpsimd.memset(eps[:, 0:1], EPS1).then_inc(set_up, 1)
            nc.gpsimd.memset(eps[:, 1:2], LN_EPS).then_inc(set_up, 1)
            nc.gpsimd.memset(eps[:, 2:3], 1.0).then_inc(set_up, 1)
            nc.gpsimd.memset(conv_in[:, :, 0:TAPS - 1], 0.0).then_inc(set_up, 1)
            for name, n in ROWS2:
                src = a[name]
                src = src.rearrange({2: "a (t c) -> (a t) c", 3: "a b (t c) -> (a b t) c"}[len(src.shape)], c=P)
                pool.dma_start(rows2[R2AT[name]:R2AT[name] + n, :], src).then_inc(small_in, 16)
            pool.dma_start(cw_rows[:], a["conv_w"][0]).then_inc(small_in, 16)
            pool.dma_start(meta_rows[:], a["meta_tokens_2"]).then_inc(small_in, 16)
            pool.dma_start(lam_rows[:], a["diff_lambda_2"].rearrange("a b c -> a (b c)")).then_inc(small_in, 16)
            pool.dma_start(f_bias[:], a["even_f_bias_2"].rearrange("a b -> b a")).then_inc(small_in, 16)
            pool.dma_start(wf[:], a["even_w_in_2"][0].rearrange("(k p) n -> p k n", p=P)[:, :, 3072:3080]).then_inc(small_in, 16)

            pool.dma_start(rot[:], a["c_rot"]).then_inc(const_in, 16)
            pool.dma_start(mask1[:], a["c_mask1"]).then_inc(const_in, 16)

            def sums(n, values=None, cols=slice(0, N1)):
                for k in range(KD):
                    pool.wait_ge(sq_ready, KD * n + k + 1)
                    if k == 0:
                        wait(pool, stat_ready, n)
                        if values is not None:
                            nc.gpsimd.tensor_copy(acc1[:, cols], values[:, k, cols])
                        nc.gpsimd.tensor_copy(acc2[:, cols], sq[:, k % 2, cols]).then_inc(acc_ready, 1)
                    else:
                        pool.wait_ge(acc_ready, KD * n + k)
                        if values is not None:
                            nc.gpsimd.tensor_tensor(acc1[:, cols], acc1[:, cols], values[:, k, cols], ALU.add)
                        nc.gpsimd.tensor_tensor(acc2[:, cols], acc2[:, cols], sq[:, k % 2, cols], ALU.add).then_inc(acc_ready, 1)

            sums(S_X)
            for m in range(CT):
                pool.wait_ge(g_sig, m + 1)
                nc.gpsimd.tensor_tensor(conv_in[:, m, TAPS - 1:], ta[:, m % 2, 0:N1], ra[:, m % 2, 0:N1], ALU.mult)\
                    .then_inc(conv_in_ready, 1)
            pool.wait_ge(conv_in_ready, CT)
            steps = [(2, tap) for tap in range(POOL_TAPS)] + [(3, tap) for tap in range(TAPS)]
            for n, (m, tap) in enumerate(steps):
                if tap == 0:
                    nc.gpsimd.tensor_scalar(cv[:, m, :], conv_in[:, m, 0:N1], cw[:, m, 0:1], c2("conv_b", m), ALU.mult, ALU.add).then_inc(conv_step2, 1)
                else:
                    t = conv_t[:, n % 2, :]
                    wait(pool, conv_step2, n - 1)
                    link(nc.gpsimd.tensor_scalar(t, conv_in[:, m, tap:tap + N1], cw[:, m, tap:tap + 1], None, ALU.mult))
                    pool.wait_ge(conv_step2, n)
                    nc.gpsimd.tensor_tensor(cv[:, m, :], cv[:, m, :], t, ALU.add).then_inc(conv_step2, 1)
            sums(S_MIX)
            sums(S_PRE)
            def gated(i):
                for u in range(2):
                    m = 2 * i + u
                    pool.wait_ge(ge_ready, m + 1)
                    wait(pool, f_ready, m - 1)
                    nc.gpsimd.tensor_tensor(fa[:, u, 0:N1], ra[:, 2 + u, 0:N1], ta[:, u, 0:N1], ALU.mult).then_inc(f_mul, 1)
                    if u == 1 or not is_first(i):
                        gated_low(m - 1, 1 - u)

            def gated_low(m, u):
                pool.wait_ge(f_hi, m + 1)
                nc.gpsimd.tensor_tensor(fl[:, at(m), 0:N1], fa[:, u, 0:N1], f32(fh[:, at(m), 0:N1]), ALU.subtract).then_inc(f_ready, 1)

            repeat(pool, FT // 2, gated)
            gated_low(FT - 1, (FT - 1) % 2)
            sums(S_E)
            sums(S_FFN)
            pool.wait_ge(stat_ready, S_FFN + 1)
            pool.dma_start(alibi[:], a["c_alibi"]).then_inc(table_in, 16)
            pool.dma_start(mask2[:], a["c_mask2"]).then_inc(table_in, 16)

            def hidden(base, cols):
                def low(m, slot):
                    pool.wait_ge(f_hi, base + m + 1)
                    nc.gpsimd.tensor_tensor(fl[:, at(m), cols], fa[:, slot, cols], f32(fh[:, at(m), cols]), ALU.subtract).then_inc(f_ready, 1)

                def turn(i):
                    for u in range(4):
                        m = 4 * i + u
                        pool.wait_ge(relu_ready, base - FT + m + 1)
                        pool.wait_ge(f_ready, base + m - 3)
                        nc.gpsimd.tensor_tensor(fa[:, u, cols], ra[:, u, cols], ra[:, u, cols], ALU.mult).then_inc(f_mul, 1)
                        if u % 2 == 1 and not (is_first(i) and u == 1):
                            for back in (3, 2):
                                low(m - back, (u - back) % 4)

                repeat(pool, FT2 // 4, turn)
                for m in (FT2 - 2, FT2 - 1):
                    low(m, m % 4)

            sums(S_LN, y, ALL)
            hidden(FT, ALL)
            sums(S_LN + 1, y, ALL)
            pool.wait_ge(stat_ready, S_LN + 2)
            pool.dma_start(decay[:], a["c_decay"]).then_inc(decay_in, 16)

            def y_low(i):
                for u in range(4):
                    m = 4 * i + u
                    pool.wait_ge(y_hi, m + 1)
                    nc.gpsimd.tensor_tensor(gl[:, at(m), LAST], fa[:, u, LAST], f32(gh[:, at(m), LAST]), ALU.subtract).then_inc(y_ready, 1)

            repeat(pool, 4, y_low)
            sums(S_LN + 2, y, LAST)
            hidden(FT + FT2, LAST)
            sums(S_LN + 3, y, LAST)

        @block.scalar
        def _(act):
            chain = Count()

            def link(ins):
                ins.then_inc(act_chain, 1)
                act.wait_ge(act_chain, chain.up())

            A = nc.scalar.activation
            act.dma_start(g_rows[:], a["g_mix_pre"].rearrange("a (t c) -> (a t) c", c=P)).then_inc(g_in, 16)
            for name, n in ROWS1:
                src = a[name]
                src = src.rearrange({2: "a (t c) -> (a t) c", 3: "a b (t c) -> (a b t) c"}[len(src.shape)], c=P)
                act.dma_start(rows1[R1AT[name]:R1AT[name] + n, :], src).then_inc(rows1_in, 16)
            act.dma_start(pt[:, :, :], a["p"][0, 0].rearrange("(t p) n -> p t n", p=P)).then_inc(pos_in, 16)
            act.dma_start(pos_i[NOPE:QHEAD, :], a["positions"].broadcast_to([ROPE, N1])).then_inc(pos_in, 16)
            act.dma_start(freq[NOPE:QHEAD, :], a["c_freq"]).then_inc(pos_in, 16)

            def split_hi(slot, use, used):
                act.wait_ge(raw_landed[slot], 32 * (use + 1))
                wait(act, mm_done, used)
                for s in range(2):
                    A(whi[:, slot, s * 1024:s * 1024 + 1024], raw[:, slot, s * 1024:s * 1024 + 1024], ACT.Copy).then_inc(w_hi_ready, 1)

            def split_at(c):
                if c < CHUNKS:
                    split_hi(c % 2, c // 2, CHUNK_END[c - 2] if c >= 2 else 0)

            def split_in(name, i, per, k):
                c = C0[name] + 2 + k
                split_hi(c % 2, c // 2 + per // 2 * i, CHUNK_END[c - 2] + per * i)

            def squares(n, k, src, cols=slice(0, N1)):
                act.wait_ge(*((e_copied, k // 2 + 1) if n == S_E else (tile_ready, TILES[n] + k + 1)))
                wait(act, acc_ready, KD * n + k - 1)
                A(sq[:, k % 2, cols], src, ACT.Square).then_inc(sq_ready, 1)

            def rms(n, width=N1):
                act.wait_ge(stat_ready, n + 1)
                nc.scalar.preload_act_table_set("natural_log_exp_and_others")
                link(A(lnv[:, 0:width], ps[4][:, 0:width], ACT.Ln, bias=eps[:, 0:1], scale=1.0 / D))
                A(rstd[:, n % 3, 0:width], lnv[:, 0:width], ACT.Exp, scale=-0.5).then_inc(rstd_ready, 1)

            def layer_stats(n, j, cols):
                w = size(cols)
                act.wait_ge(stat_ready, n + 1)
                link(A(mu[:, cols], ps[5][:, 0:w], ACT.Copy, scale=-1.0 / D))
                A(musq[:, cols], mu[:, cols], ACT.Square).then_inc(mu_ready, 1)
                nc.scalar.preload_act_table_set("natural_log_exp_and_others")
                act.wait_ge(var_ready, j + 1)
                link(A(lnv[:, cols], var[:, cols], ACT.Ln, bias=eps[:, 1:2]))
                A(rstd[:, n % 3, cols], lnv[:, cols], ACT.Exp, scale=-0.5).then_inc(rstd_ready, 1)

            def layer_apply(j, k, cols, dst=None):
                g, b = (col1[:, at(R1AT[name] + KD * j + k)] for name in ("ln_g_2", "ln_b_2"))
                act.wait_ge(norm_ready, KD * j + k + 1)
                A(h[:, at(k), cols], y[:, at(k), cols], ACT.Identity, bias=b, scale=g).then_inc(hn_ready, 1)
                if dst is not None:
                    A(dst[:, at(k), cols], y[:, at(k), cols], ACT.Identity, bias=b, scale=g).then_inc(xh_ready, 1)

            def raw_columns(j):
                for n, name in enumerate(("ln_g_2", "ln_b_2")):
                    r0 = R1AT[name] + KD * j
                    ins = A(xrh[:, :, N2 + n], col1[:, r0:r0 + KD], ACT.Copy)
                ins.then_inc(gb_hi, 1)

            act.wait_ge(set_up, 6)
            act.wait_ge(cols_ready, 1)
            for k in range(KD):
                act.wait_ge(tile_ready, k + 1)
                A(xh[:, k, 0:N1], h[:, k, META:], ACT.Copy, scale=g_col[:, k:k + 1]).then_inc(xh_ready, 1)
                squares(S_X, k, h[:, k, META:])
            split_at(0)
            split_at(1)
            act.wait_ge(pt_done, 1)
            A(ph[:, :, :], ps[6][:, :].rearrange("p (k n) -> p k n", k=2), ACT.Copy).then_inc(p_hi, 1)
            rms(S_X)
            act.wait_ge(lam_sum, 2)
            A(lam_s[:, 2:4], lam_s[:, 0:2], ACT.Exp).then_inc(lam_exp, 1)
            for j in range(3):
                for m in range(2):
                    t = 2 * j + m
                    if t < 5:
                        act.wait_ge(qkv_ready, t + 1)
                        A(sq6[:, t, :], qkv[:, t, :], ACT.Square).then_inc(sq6_ready, 1)
                split_at(C0["qkv_in"] + j + 2)
            nc.scalar.preload_act_table(ACT.Sin)
            act.wait_ge(ang_ready, 2)
            for j in range(2):
                A(ang[NOPE:QHEAD, 4 + j, :], ang[NOPE:QHEAD, 2 + j, :], ACT.Sin).then_inc(trig_ready, 1)
            nc.scalar.preload_act_table_set("natural_log_exp_and_others")
            split_at(C0["conv_in"] + 2)
            for j, width in enumerate((QLORA, KVLORA)):
                act.wait_ge(lstat_ready, j + 1)
                wait(act, lrstd_ready, j)
                link(A(lnv[:, 0:N1], ps[6 + j][:, 0:N1], ACT.Ln, bias=eps[:, 0:1], scale=1.0 / width))
                A(lr[:, j, :], lnv[:, 0:N1], ACT.Exp, scale=-0.5).then_inc(lrstd_ready, 1)
            nc.scalar.preload_act_table(ACT.Sigmoid)
            for t in range(5):
                act.wait_ge(ln_ready, t + 1)
                A(qxh[:, t, :], qkv[:, t, :], ACT.Copy).then_inc(xh_ready, 1)
            for m in range(CT):
                if m >= 1:
                    split_at(C0["conv_in"] + m + 2)
                act.wait_ge(g_scaled, m + 1)
                wait(act, conv_in_ready, m - 1)
                A(ra[:, m % 2, 0:N1], tb[:, m % 2, 0:N1], ACT.Sigmoid).then_inc(g_sig, 1)
            for j in range(4):
                act.wait_ge(mm_done, E0["q"] + j + 1)
                for m in range(2):
                    ins = A(qt[0:QHEAD, 2 * j + m, :], ps[2 * ((P0["q"] + j) % 2) + m][0:QHEAD, 0:N1], ACT.Copy)
                ins.then_inc(q_ready, 1)
                if j % 2 == 1:
                    split_at(C0["q"] + j // 2 + 2)
            for j in range(4):
                act.wait_ge(mm_done, E0["kv"] + j + 1)
                for m in range(2):
                    ins = A(kt_[0:NOPE, 2 * j + m, :], ps[2 * ((P0["kv"] + j) % 2) + m][0:NOPE, 0:N1], ACT.Copy)
                ins.then_inc(k_ready, 1)
            split_at(C0["kv"] + 2)
            nc.scalar.preload_act_table_set("natural_log_exp_and_others")
            for i in range(16 + 4):
                if i < 16:
                    w = P * (i // 8 + 1)
                    act.wait_ge(bias_ready, i + 1)
                    wait(act, t_done, i - 3)
                    A(p1[:, i % 4, 0:w], s1[:, i % 2, 0:w], ACT.Exp, bias=small[:, i, 1:2], scale=SC1,
                      accum_out=small[:, i, 2:3]).then_inc(p_exp, 1)
                if 3 <= i < 19:
                    u = i - 3
                    n = u // 8 + 1
                    act.wait_ge(t_done, u + 1)
                    wait(act, pv_done, u - 1)
                    A(pt1[:, u % 2, 0:n, :], ps[6 + u % 2][:, 0:n * P].rearrange("p (k n) -> p k n", k=n), ACT.Copy).then_inc(pT_ready, 1)
                if i >= 5 and i % 2 == 1:
                    g = (i - 5) // 2
                    act.wait_ge(pv_done, 2 * g + 2)
                    A(xh[:, g % 4, P * (g // 4):P * (g // 4) + P], ps[2 + g % 2][:, 0:P], ACT.Copy).then_inc(o_hi, 1)
            for m in range(CT):
                act.wait_ge(*((conv_step, 3 * TAPS - POOL_TAPS) if m < 3 else (conv_step2, TAPS + POOL_TAPS)))
                A(sq6[:, m, :], cv[:, m, :], ACT.Square).then_inc(csq_ready, 1)
            act.wait_ge(cstat_ready, 1)
            link(A(mu[:, 0:N1], ps[4][:, 0:N1], ACT.Copy, scale=1.0 / CONV_C))
            A(musq[:, 0:N1], mu[:, 0:N1], ACT.Square).then_inc(cmu_ready, 1)
            act.wait_ge(cvar_ready, 1)
            link(A(lnv[:, 0:N1], var[:, 0:N1], ACT.Ln, bias=eps[:, 0:1]))
            A(musq[:, 0:N1], lnv[:, 0:N1], ACT.Exp, scale=-0.5).then_inc(crstd_ready, 1)
            nc.scalar.preload_act_table(ACT.Silu)
            for m in range(CT):
                act.wait_ge(cn_ready, m + 1)
                A(sq6[:, m, :], cv[:, m, :], ACT.Silu, bias=c2("conv_ln_b", m), scale=c2("conv_ln_g", m)).then_inc(silu_ready, 1)
                act.wait_ge(silu_ready, m + 1)
                A(xh[:, 4 + m, 0:N1], sq6[:, m, :], ACT.Copy).then_inc(c_hi, 1)
            for j in range(4):
                for m in range(2):
                    squares(S_MIX, 2 * j + m, y[:, 2 * j + m, 0:N1])
                split_at(C0["mix_out"] + j + 2)
            rms(S_MIX)
            for k in range(KD):
                act.wait_ge(tile_ready, TILES[S_PRE] + k + 1)
                A(xh[:, k, 0:N1], h[:, k, META:], ACT.Copy, scale=c1("g_ffn_pre", k)).then_inc(xh_ready, 1)
                squares(S_PRE, k, h[:, k, META:])
            split_at(C0["ple"] + 2)
            rms(S_PRE)
            nc.scalar.preload_act_table(ACT.Gelu_apprx_tanh)

            def gelu_at(m, u):
                act.wait_ge(taps_ready, m + 1)
                A(ra[:, 2 + u, 0:N1], tb[:, u, 0:N1], ACT.Gelu_apprx_tanh, bias=col2[:, at(3 * FT + m)]).then_inc(ge_ready, 1)

            def gated_high(m, u):
                act.wait_ge(f_mul, m + 1)
                A(fh[:, at(m), 0:N1], fa[:, u, 0:N1], ACT.Copy).then_inc(f_hi, 1)

            def gelu(i):
                for u in range(2):
                    m = 2 * i + u
                    split_in("gate_up", i, 2, u)
                    act.wait_ge(gv_scaled, m + 1)
                    A(ra[:, u, 0:N1], gt[:, u, 0:N1], ACT.Copy, scale=col2[:, at(m)]).then_inc(t0_ready, 1)
                    later = not is_first(i)
                    if later or u == 1:
                        gelu_at(m - 1, 1 - u)
                    if later:
                        gated_high(m - 2, u)

            repeat(act, FT // 2, gelu)
            gelu_at(FT - 1, (FT - 1) % 2)
            for m in (FT - 2, FT - 1):
                gated_high(m, m % 2)
            for j in range(4):
                split_at(C0["down"] + 3 * j + 2)
                split_at(C0["down"] + 3 * j + 3)
                if j == 0:
                    for k in range(KD):
                        squares(S_E, k, e[:, k, :])
                if j == 2:
                    rms(S_E)
                for m in range(2):
                    squares(S_FFN, 2 * j + m, y[:, 2 * j + m, 0:N1])
                split_at(C0["down"] + 3 * j + 4)
            rms(S_FFN)
            for k in range(KD):
                act.wait_ge(h_ready, k + 1)
                A(xh[:, k, 0:N1], h[:, k, META:], ACT.Copy).then_inc(xh_ready, 1)
            nc.scalar.preload_act_table(ACT.Sigmoid)
            for j in range(4):
                p = P0["ple_gate"] + j
                act.wait_ge(mm_done, E0["ple_gate"] + j + 1)
                for m in range(2):
                    k = 2 * j + m
                    wait(act, h_ready, KD + k - 3 if k >= 4 else 0)
                    ins = A(ra[:, k % 4, 0:N1], ps[2 * (p % 2) + m][:, 0:N1], ACT.Sigmoid)
                    ins.then_inc(sig_ready, 1)
                split_at(C0["ple_gate"] + j + 2)
                for m in range(2):
                    k = 2 * j + m
                    act.wait_ge(h_ready, KD + k + 1)
                    A(xrh[:, k, 0:N2], h[:, k, :], ACT.Copy).then_inc(xh_ready, 1)
            def even_chunks(i):
                for u in range(2):
                    split_in("even_qk", i, 2, u)

            repeat(act, 6, even_chunks)
            nc.scalar.preload_act_table_set("natural_log_exp_and_others")
            act.wait_ge(fz_ready, 1)
            link(A(fg[:, 1, :], fg[:, 0, :], ACT.Abs))
            link(A(fg[:, 2, :], fg[:, 1, :], ACT.Exp, scale=-1.0))
            A(fg[:, 3, :], fg[:, 2, :], ACT.Ln, bias=eps[0:8, 2:3]).then_inc(fl_ready, 1)
            for i in range(len(UNITS) + 4):
                if i < len(UNITS):
                    t, diff, hd, m = UNITS[i]
                    n, w = TOK[t][1], SEEN[t]
                    act.wait_ge(u_bias, i + 1)
                    if i >= 4:
                        if i - 4 in ORDER:
                            act.wait_ge(u_t_done, ORDER[i - 4] + 1)
                        else:
                            act.wait_ge(u_pn, i - 2)
                    A(p2[0:n, i % 4, 0:w], s2[0:n, i % 2, 0:w], ACT.Exp, bias=small[0:n, i, 1:2], scale=SC2,
                      accum_out=small[0:n, i, 2:3]).then_inc(u_exp, 1)
                if i >= 3 and i - 3 in ORDER:
                    t, diff, hd, m = UNITS[i - 3]
                    o = ORDER[i - 3]
                    nq = TOK[t][1]
                    act.wait_ge(u_t_done, o + 1)
                    wait(act, u_pv, o - 1)
                    for b in range(t + 1):
                        kn = TOK[b][1]
                        ins = A(pt2[0:kn, o % 2, b, 0:nq], ps[6 + o % 2][0:kn, P * b:P * b + nq], ACT.Copy)
                    ins.then_inc(u_pT, 1)
                if i >= 4 and i - 4 in ORDER:
                    t, diff, hd, m = UNITS[i - 4]
                    o = ORDER[i - 4]
                    q0, nq = TOK[t]
                    if diff:
                        act.wait_ge(u_pv, o + 1)
                        A(oa[:, hd, q0:q0 + nq], ps[2 + o % 2][:, 0:nq], ACT.Copy).then_inc(u_ohi, 1)
                    elif hd % 2 == 1:
                        g = 12 + (o - 12) // 2
                        act.wait_ge(u_pv, o + 1)
                        A(xh[:, 4 + hd // 2, q0:q0 + nq], ps[2 + g % 2][:, 0:nq], ACT.Copy).then_inc(u_ohi, 1)
            act.wait_ge(u_ohi, 12)
            for hd in range(4):
                A(oasq[:, hd, :], oa[:, hd, :], ACT.Square).then_inc(oasq_ready, 1)
            for hd in range(4):
                act.wait_ge(oastat, hd + 1)
                wait(act, oarstd, hd)
                link(A(lnv[:, :], ps[4 + hd][:, 0:N2], ACT.Ln, bias=eps[:, 0:1], scale=1.0 / P))
                A(oasq[:, hd, :], lnv[:, :], ACT.Exp, scale=-0.5).then_inc(oarstd, 1)
            for hd in range(4):
                act.wait_ge(oan, hd + 1)
                A(xh[:, hd, :], oa[:, hd, :], ACT.Copy).then_inc(oa_hi, 1)

            def residual(n, name, per, j, cols):
                for i in range(4):
                    for q in range(per - 1):
                        split_at(C0[name] + per * i + q + 2)
                    if i == 0 and j < 3:
                        raw_columns(j)
                    if j < 3:
                        for k in (2 * i, 2 * i + 1):
                            act.wait_ge(tile_ready, TILES[n] + k + 1)
                            A(xrh[:, k, cols], y[:, k, cols], ACT.Copy, scale=c1("ln_g_2", KD * j + k)).then_inc(xh_ready, 1)
                    for k in (2 * i, 2 * i + 1):
                        squares(n, k, y[:, k, cols], cols)
                    split_at(C0[name] + per * i + per - 1 + 2)

            def ffn_up(name, base, j, cols):
                def turn(i):
                    for u in range(2):
                        split_in(name, i, 2, u)
                        if u == 0 and is_first(i):
                            layer_stats(S_LN + j, j, cols)
                        for m in range(2):
                            t = 4 * i + 2 * u + m
                            act.wait_ge(raw_ready, base - FT + (16 if j else 0) + t + 1)
                            A(ra[:, 2 * u + m, cols], rw[:, 2 * u + m, cols], ACT.Relu, bias=b_col[:, 2 * u + m:2 * u + m + 1]).then_inc(relu_ready, 1)
                        if not (is_first(i) and u == 0):
                            for m in range(2):
                                high(4 * i + 2 * u + m - 2, 2 - 2 * u + m)
                    layer_apply(j, i, cols)

                def high(t, slot):
                    act.wait_ge(f_mul, base + t + 1)
                    A(fh[:, at(t), cols], fa[:, slot, cols], ACT.Copy).then_inc(f_hi, 1)

                repeat(act, 8, turn)
                for t in (FT2 - 2, FT2 - 1):
                    high(t, t % 4)

            residual(S_LN, "even_out", 1, 0, ALL)
            ffn_up("ffn_up0", FT, 0, ALL)
            residual(S_LN + 1, "ffn_down0", 4, 1, ALL)
            for c in range(8):
                split_at(C0["ret_qk"] + c + 2)
                if c == 0:
                    layer_stats(S_LN + 1, 1, ALL)
                cols = LAST if c < 4 else ALL
                for m in range(2):
                    slot = 2 * (c % 2) + m
                    act.wait_ge(raw_ready, FT2 + 2 * c + m + 1)
                    A(rqk[:, c % 4, 2 * (c // 4) + m, cols], rw[:, slot, cols], ACT.Identity, bias=b_col[:, slot:slot + 1]).then_inc(rqk_ready, 1)
                for k in RET_TILES[c]:
                    layer_apply(1, k, ALL, xh)

            def ret_chunks(i):
                for u in range(2):
                    split_in("ret_v", i, 2, u)

            repeat(act, 4, ret_chunks)
            nc.scalar.preload_act_table_set("natural_log_exp_and_others")
            for hd in range(RH):
                for q in range(4):
                    n = 4 * hd + q
                    act.wait_ge(ro_done, n + 1)
                    A(rqk[:, hd, q, LAST], ps[6 + n % 2][:, 0:N1], ACT.Copy).then_inc(ro_ready, 1)
                    act.wait_ge(ro_ready, n + 1)
                    wait(act, rstat, n - 1)
                    A(rsq[:, n % 2, LAST], rqk[:, hd, q, LAST], ACT.Square).then_inc(rsq_ready, 1)
                act.wait_ge(rstat, 4 * hd + 4)
                wait(act, ron_ready, hd)
                link(A(lnv[:, LAST], ps[hd % 2][:, 0:N1], ACT.Ln, bias=eps[:, 0:1], scale=1.0 / RV))
                A(r_rstd[:, LAST], lnv[:, LAST], ACT.Exp, scale=-0.5).then_inc(r_rstd_ready, 1)
            nc.scalar.preload_act_table(ACT.Silu)

            def ret_gate(i):
                for u in range(2):
                    act.wait_ge(mm_done, E0["ret_g"] + 2 * i + u + 1)
                    for m in range(2):
                        A(ra[:, 2 * u + m, LAST], ps[2 * ((P0["ret_g"] + u) % 2) + m][:, 0:N1], ACT.Silu).then_inc(silu2_ready, 1)
                    split_in("ret_g", i, 2, u)
                    for m in range(2):
                        t = 4 * i + 2 * u + m
                        act.wait_ge(y_mul, t + 1)
                        A(gh[:, at(t), LAST], fa[:, 2 * u + m, LAST], ACT.Copy).then_inc(y_hi, 1)

            repeat(act, 4, ret_gate)
            residual(S_LN + 2, "ret_out", 2, 2, LAST)
            ffn_up("ffn_up1", FT + FT2, 2, LAST)
            residual(S_LN + 3, "ffn_down1", 4, 3, LAST)
            layer_stats(S_LN + 3, 3, LAST)
            for k in range(KD):
                layer_apply(3, k, LAST)

        @block.vector
        def _(dve):
            V = nc.vector
            chain = Count()

            def link(ins):
                ins.then_inc(dve_chain, 1)
                dve.wait_ge(dve_chain, chain.up())

            def split_lo(c, slot):
                for s in range(2):
                    dve.wait_ge(w_hi_ready, 2 * c + s + 1)
                    V.tensor_tensor(wlo[:, slot, s * 1024:s * 1024 + 1024], raw[:, slot, s * 1024:s * 1024 + 1024],
                                    f32(whi[:, slot, s * 1024:s * 1024 + 1024]), ALU.subtract).then_inc(w_lo_ready, 1)

            def split_at(c):
                if c < CHUNKS:
                    split_lo(c, c % 2)

            def split_in(name, i, per, k):
                c = C0[name] + 2 + k
                split_lo(c + per * i, c % 2)

            def x_low(done, k, src, gain=None, dst=(xh, xl), cols=None):
                hi, lo = (v[:, at(k), cols or slice(0, src.shape[-1])] for v in dst)
                dve.wait_ge(xh_ready, done + k + 1)
                if gain is None:
                    V.tensor_tensor(lo, src, f32(hi), ALU.subtract).then_inc(x_ready, 1)
                else:
                    V.scalar_tensor_tensor(lo, src, gain, f32(hi), ALU.mult, ALU.subtract).then_inc(x_ready, 1)

            dve.wait_ge(cols_t, 1)
            V.tensor_copy(g_col[:, :], ps[0][:, 0:KD]).then_inc(cols_ready, 1)
            for k in range(KD):
                dve.wait_ge(xt_done, k + 1)
                V.tensor_copy(h[:, k, META:], ps[4 + k % 4][:, 0:N1]).then_inc(tile_ready, 1)
                if k >= 1:
                    x_low(X_A, k - 1, h[:, k - 1, META:], g_col[:, k - 1:k])
            x_low(X_A, KD - 1, h[:, KD - 1, META:], g_col[:, KD - 1:KD])
            split_at(0)
            split_at(1)
            dve.wait_ge(cols_t, 2)
            V.tensor_copy(col1[:, :], ps[7][:, 2 * P:2 * P + R1N])
            V.tensor_copy(col2[:, :], ps[7][:, 0:R2N]).then_inc(cols_ready, 1)
            V.tensor_copy(cw[:, :, :], ps[7][:, P:P + CT * TAPS].rearrange("p (m n) -> p m n", m=CT)).then_inc(cols_ready, 1)
            for j in range(2):
                V.tensor_tensor_reduce(var[0:1, 64 * j:64 * j + 64], lam_rows[:, 128 * j:128 * j + 64], lam_rows[:, 128 * j + 64:128 * j + 128],
                                       1.0, 0.0, ALU.mult, ALU.add, lam_s[:, j:j + 1]).then_inc(lam_sum, 1)
            dve.wait_ge(meta_done, 1)
            V.tensor_copy(h[:, :, 0:META], ps[5][:, 0:KD * META].rearrange("p (k n) -> p k n", k=KD)).then_inc(meta_ready, 1)
            dve.wait_ge(p_hi, 1)
            V.tensor_tensor(pl[:, :, :], ps[6][:, :].rearrange("p (k n) -> p k n", k=2), f32(ph[:, :, :]), ALU.subtract).then_inc(p_ready, 1)
            R = slice(NOPE, QHEAD)
            cos, sin = ang[R, 4, :], ang[R, 5, :]

            def rotary_angles():
                dve.wait_ge(pos_in, 48)
                link(V.tensor_copy(ang[R, 0, :], pos_i[R, :]))
                link(V.tensor_scalar(ang[R, 0, :], ang[R, 0, :], freq[R, 0:1], None, ALU.mult))
                two_pi = 2 * np.pi
                p_1 = 6.28125
                p_2 = float(np.float32(np.floor((two_pi - p_1) * 2 ** 21) / 2 ** 21))
                p_3 = float(np.float32(two_pi - p_1 - p_2))
                magic = 1.5 * 2 ** 23
                for j, (turn, shift) in enumerate(((0.25, np.pi / 2), (0.0, 0.0))):
                    link(V.tensor_scalar(ang[R, 1, :], ang[R, 0, :], float(1 / two_pi), turn, ALU.mult, ALU.add))
                    link(V.tensor_scalar(ang[R, 1, :], ang[R, 1, :], magic, None, ALU.add))
                    link(V.tensor_scalar(ang[R, 1, :], ang[R, 1, :], magic, None, ALU.subtract))
                    link(V.scalar_tensor_tensor(ang[R, 2 + j, :], ang[R, 1, :], -p_1, ang[R, 0, :], ALU.mult, ALU.add))
                    link(V.scalar_tensor_tensor(ang[R, 2 + j, :], ang[R, 1, :], -p_2, ang[R, 2 + j, :], ALU.mult, ALU.add))
                    link(V.scalar_tensor_tensor(ang[R, 2 + j, :], ang[R, 1, :], -p_3, ang[R, 2 + j, :], ALU.mult, ALU.add))
                    link(V.tensor_scalar(ang[R, 2 + j, :], ang[R, 2 + j, :], float(shift), 3.1415925, ALU.add, ALU.min))
                    V.tensor_scalar(ang[R, 2 + j, :], ang[R, 2 + j, :], -3.1415925, None, ALU.max).then_inc(ang_ready, 1)

            steps = [(m, tap) for tap in range(POOL_TAPS) for m in (0, 1)]
            steps += [s for tap in range(POOL_TAPS, TAPS) for s in ((0, tap), (2, tap), (1, tap))]

            def conv_taps(first, last):
                for n, (m, tap) in list(enumerate(steps))[first:last]:
                    if tap == 0:
                        dve.wait_ge(conv_in_ready, m + 1)
                        V.tensor_scalar(cv[:, m, :], conv_in[:, m, 0:N1], cw[:, m, 0:1], c2("conv_b", m), ALU.mult, ALU.add).then_inc(conv_step, 1)
                    else:
                        if (m, tap) == (2, POOL_TAPS):
                            dve.wait_ge(conv_step2, POOL_TAPS)
                        else:
                            dve.wait_ge(conv_step, steps.index((m, tap - 1)) + 1)
                        V.scalar_tensor_tensor(cv[:, m, :], conv_in[:, m, tap:tap + N1], cw[:, m, tap:tap + 1], cv[:, m, :],
                                               ALU.mult, ALU.add).then_inc(conv_step, 1)

            r_x = rstd[:, S_X % 3, 0:N1]
            dve.wait_ge(rstd_ready, 1)
            for j in range(3):
                p = P0["qkv_in"] + j
                dve.wait_ge(mm_done, E0["qkv_in"] + j + 1)
                for m in range(2):
                    n = QHEAD if 2 * j + m == 5 else P
                    V.tensor_tensor(qkv[0:n, 2 * j + m, :], ps[2 * (p % 2) + m][0:n, 0:N1], r_x[0:n], ALU.mult).then_inc(qkv_ready, 1)
                split_at(C0["qkv_in"] + j + 2)
                if j == 1:
                    rotary_angles()

            def conv_input(m):
                p = P0["conv_in"] + m
                dve.wait_ge(mm_done, E0["conv_in"] + m + 1)
                wait(dve, conv_in_ready, m - 1)
                V.tensor_tensor(ta[:, m % 2, 0:N1], ps[2 * (p % 2)][:, 0:N1], r_x, ALU.mult)
                V.tensor_tensor(tb[:, m % 2, 0:N1], ps[2 * (p % 2) + 1][:, 0:N1], r_x, ALU.mult).then_inc(g_scaled, 1)
                split_at(C0["conv_in"] + m + 2)

            conv_input(0)
            dve.wait_ge(krot_done, 1)
            dve.wait_ge(trig_ready, 2)
            V.tensor_tensor(rope_t[R, 0, 0:N1], ps[5][R, 0:N1], sin, ALU.mult)
            link(V.tensor_tensor(rope_t[R, 1, 0:N1], qkv[R, 5, :], cos, ALU.mult))
            heads = [ROPE, HEADS, N1]
            V.tensor_tensor(kt_[R, :, :], rope_t[R, 0, 0:N1].unsqueeze(1).broadcast_to(heads),
                            rope_t[R, 1, 0:N1].unsqueeze(1).broadcast_to(heads), ALU.add).then_inc(krope_ready, 1)
            for t in range(5):
                j = 0 if t < 3 else 1
                dve.wait_ge(lrstd_ready, j + 1)
                V.scalar_tensor_tensor(qkv[:, t, :], qkv[:, t, :], c2("g_q_a", t) if t < 3 else c2("g_kv_a", t - 3), lr[:, j, :],
                                       ALU.mult, ALU.mult).then_inc(ln_ready, 1)
                if t >= 1:
                    x_low(X_QKV, t - 1, qkv[:, t - 1, :], dst=(qxh, qxl))
            x_low(X_QKV, 4, qkv[:, 4, :], dst=(qxh, qxl))
            for m in range(1, CT):
                conv_input(m)
                if m >= 2:
                    conv_taps(10 * (m - 2), 10 * (m - 1))
            dve.wait_ge(lam_exp, 1)
            link(V.tensor_tensor(lam_s[:, 5:6], lam_s[:, 2:3], lam_s[:, 3:4], ALU.subtract))
            V.tensor_scalar(lam_s[:, 4:5], lam_s[:, 5:6], LAM_INIT, None, ALU.add).then_inc(lam_one, 1)
            for j in range(2):
                split_at(C0["q"] + j + 2)
            pair = [ROPE, 2, N1]

            def query_rope(j):
                dve.wait_ge(qrot_done, j + 1)
                wait(dve, qrope_ready, j)
                t1, t2 = (rope_t[R, n, :].rearrange("p (h n) -> p h n", h=2) for n in range(2))
                V.tensor_tensor(t1, ps[4 + j][R, :].rearrange("p (h n) -> p h n", h=2), sin.unsqueeze(1).broadcast_to(pair), ALU.mult)
                link(V.tensor_tensor(t2, qt[R, 2 * j:2 * j + 2, :], cos.unsqueeze(1).broadcast_to(pair), ALU.mult))
                V.tensor_tensor(qt[R, 2 * j:2 * j + 2, :], t1, t2, ALU.add).then_inc(qrope_ready, 1)

            conv_taps(20, 32)
            for j in range(2):
                query_rope(j)
            for t in range(2):
                dve.wait_ge(mm_done, E0["kv"] + 5)
                V.tensor_copy(v1[:, t, :], ps[2 * ((P0["kv"] + 4) % 2) + t][:, :]).then_inc(v_ready, 1)
            split_at(C0["kv"] + 2)
            dve.wait_ge(const_in, 32)
            for i in range(16 + 4):
                if i < 16:
                    w = P * (i // 8 + 1)
                    dve.wait_ge(s_done, i + 1)
                    wait(dve, p_exp, i - 1)
                    V.tensor_tensor_reduce(s1[:, i % 2, 0:w], ps[4 + i % 2][:, 0:w], mask1[:, N1 - w:N1], 1.0, -3.0e38,
                                           ALU.add, ALU.max, small[:, i, 0:1]).then_inc(max_ready, 1)
                    dve.wait_ge(max_ready, i + 1)
                    V.tensor_scalar(small[:, i, 1:2], small[:, i, 0:1], -SC1, None, ALU.mult).then_inc(bias_ready, 1)
                if i < 2:
                    query_rope(2 + i)
                if 1 <= i < 17:
                    u = i - 1
                    w = P * (u // 8 + 1)
                    dve.wait_ge(p_exp, u + 1)
                    link(V.reciprocal(small[:, u, 3:4], small[:, u, 2:3]))
                    V.tensor_scalar(p1[:, u % 4, 0:w], p1[:, u % 4, 0:w], small[:, u, 3:4], None, ALU.mult).then_inc(pn_ready, 1)
                if i >= 5 and i % 2 == 1:
                    g = (i - 5) // 2
                    dve.wait_ge(o_hi, g + 1)
                    lo, hi = (x[:, g % 4, P * (g // 4):P * (g // 4) + P] for x in (xl, xh))
                    V.tensor_tensor(lo, ps[2 + g % 2][:, 0:P], f32(hi), ALU.subtract).then_inc(o_ready, 1)
                if i >= 2:
                    conv_taps(32 + 3 * (i - 2), 35 + 3 * (i - 2))
            dve.wait_ge(cstat_ready, 1)
            dve.wait_ge(cmu_ready, 1)
            V.scalar_tensor_tensor(var[:, 0:N1], ps[5][:, 0:N1], 1.0 / CONV_C, musq[:, 0:N1], ALU.mult, ALU.subtract).then_inc(cvar_ready, 1)
            for m in range(CT):
                ins = V.tensor_tensor(cv[:, m, :], cv[:, m, :], mu[:, 0:N1], ALU.subtract)
            link(ins)
            dve.wait_ge(crstd_ready, 1)
            for m in range(CT):
                V.tensor_tensor(cv[:, m, :], cv[:, m, :], musq[:, 0:N1], ALU.mult).then_inc(cn_ready, 1)
            for m in range(CT):
                dve.wait_ge(c_hi, m + 1)
                V.tensor_tensor(xl[:, 4 + m, 0:N1], sq6[:, m, :], f32(xh[:, 4 + m, 0:N1]), ALU.subtract).then_inc(c_ready, 1)

            dve.wait_ge(lam_done, 1)
            V.tensor_scalar(neg_lam[:, :], ps[6][:, 0:1], -1.0, None, ALU.mult).then_inc(lam_ready, 1)

            def post_norm(n, gain, done, signal, posts):
                base, gain_in, x0 = done
                dve.wait_ge(rstd_ready, n + 1)
                for k in range(KD + 2):
                    if k < KD:
                        if k >= 2:
                            dve.wait_ge(signal, base + k - 1)
                        V.scalar_tensor_tensor(ta[:, k % 2, 0:N1], y[:, k, 0:N1], c1(gain, k), rstd[:, n % 3, 0:N1],
                                               ALU.mult, ALU.mult).then_inc(post_ready, 1)
                    if 1 <= k <= KD:
                        dve.wait_ge(post_ready, posts + k)
                        V.tensor_tensor(h[:, k - 1, META:], h[:, k - 1, META:], ta[:, (k - 1) % 2, 0:N1], ALU.add).then_inc(signal, 1)
                    if k >= 2:
                        x_low(x0, k - 2, h[:, k - 2, META:], gain_in and c1(gain_in, k - 2))

            for j in range(4):
                dve.wait_ge(mm_done, E0["mix_out"] + j + 1)
                for m in range(2):
                    V.tensor_copy(y[:, 2 * j + m, 0:N1], ps[2 * ((P0["mix_out"] + j) % 2) + m][:, 0:N1]).then_inc(tile_ready, 1)
                split_at(C0["mix_out"] + j + 2)
            V.memset(gt[:, :, 0:2], 0.0)
            for j in range(4):
                dve.wait_ge(mm_done, E0["ple"] + j + 1)
                b = 2 * ((P0["ple"] + j) % 2)
                for m in range(2):
                    ins = V.tensor_copy(e[:, 2 * j + m, :], ps[b + m][:, 0:N1])
                ins.then_inc(e_copied, 1)
            post_norm(S_MIX, "g_mix_post", (TILES[S_PRE], "g_ffn_pre", X_FFN), tile_ready, 0)
            split_at(C0["ple"] + 2)
            r_pre = rstd[:, S_PRE % 3, 0:N1]
            dve.wait_ge(rstd_ready, S_PRE + 1)

            def gate_up(i):
                for u in range(2):
                    m = 2 * i + u
                    b = 2 * ((P0["gate_up"] + u) % 2)
                    dve.wait_ge(mm_done, E0["gate_up"] + m + 1)
                    wait(dve, f_mul, m - 1)
                    V.tensor_tensor(ta[:, u, 0:N1], ps[b + 1][:, 0:N1], r_pre, ALU.mult)
                    V.tensor_tensor(gt[:, u, 2:2 + N1], ps[b][:, 0:N1], r_pre, ALU.mult).then_inc(gv_scaled, 1)
                    split_in("gate_up", i, 2, u)
                    dve.wait_ge(t0_ready, m + 1)
                    V.scalar_tensor_tensor(fa[:, 2 + u, 0:N1], gt[:, u, 1:1 + N1], col2[:, at(FT + m)], ra[:, u, 0:N1],
                                           ALU.mult, ALU.add).then_inc(t1_ready, 1)
                    dve.wait_ge(t1_ready, m + 1)
                    V.scalar_tensor_tensor(tb[:, u, 0:N1], gt[:, u, 2:2 + N1], col2[:, at(2 * FT + m)], fa[:, 2 + u, 0:N1],
                                           ALU.mult, ALU.add).then_inc(taps_ready, 1)

            repeat(dve, FT // 2, gate_up)

            def branch(name, per, put, low=None, aside=None):
                for j in range(4):
                    for q in range(per - 1):
                        split_at(C0[name] + per * j + q + 2)
                    if aside is not None:
                        aside(j)
                    dve.wait_ge(mm_done, E0[name] + per * (j + 1))
                    for m in range(2):
                        put(2 * j + m, ps[2 * ((P0[name] + j) % 2) + m])
                    if low is not None:
                        for m in range(2):
                            low(2 * j + m)
                    split_at(C0[name] + per * j + per - 1 + 2)

            def plain(k, bank):
                V.tensor_copy(y[:, k, 0:N1], bank[:, 0:N1]).then_inc(tile_ready, 1)

            def finish_e(j):
                if j == 3:
                    dve.wait_ge(rstd_ready, S_E + 1)
                    for k in range(KD):
                        V.scalar_tensor_tensor(e[:, k, :], e[:, k, :], c1("g_ple", k), rstd[:, S_E % 3, 0:N1], ALU.mult, ALU.mult).then_inc(e_ready, 1)

            def residual(n, name, per, j, x0, cols):
                def columns(i):
                    if i > 0:
                        return
                    if j < 3:
                        dve.wait_ge(gb_hi, j + 1)
                        for c, gain in enumerate(("ln_g_2", "ln_b_2")):
                            r0 = R1AT[gain] + KD * j
                            V.tensor_tensor(xrl[:, :, N2 + c], col1[:, r0:r0 + KD], f32(xrh[:, :, N2 + c]), ALU.subtract)
                    if j > 0:
                        dve.wait_ge(hn_ready, KD * j)

                def put(k, bank):
                    V.scalar_tensor_tensor(y[:, k, cols], h[:, k, cols], ALPHA, bank[:, 0:size(cols)], ALU.mult, ALU.add).then_inc(tile_ready, 1)

                def low(k):
                    x_low(x0, k, y[:, k, cols], c1("ln_g_2", KD * j + k), (xrh, xrl), cols)

                branch(name, per, put, low if j < 3 else None, columns)

            branch("down", 3, plain, aside=finish_e)
            post_norm(S_FFN, "g_ffn_post", (0, None, X_PLE), h_ready, KD)
            dve.wait_ge(e_ready, KD)
            for j in range(4):
                for k in (2 * j, 2 * j + 1):
                    dve.wait_ge(sig_ready, k + 1)
                    V.tensor_tensor(ta[:, k % 2, 0:N1], ra[:, k % 4, 0:N1], e[:, k, :], ALU.mult).then_inc(post_ready, 1)
                    dve.wait_ge(post_ready, 2 * KD + k + 1)
                    V.tensor_tensor(h[:, k, META:], h[:, k, META:], ta[:, k % 2, 0:N1], ALU.add).then_inc(h_ready, 1)
                split_at(C0["ple_gate"] + j + 2)
                for k in (2 * j, 2 * j + 1):
                    x_low(X_B, k, h[:, k, :], dst=(xrh, xrl))
            def even_qk(i):
                for u in range(2):
                    dve.wait_ge(mm_done, E0["even_qk"] + 2 * i + u + 1)
                    for m in range(2):
                        V.tensor_copy(qk[:, at(4 * i + 2 * u + m), :], ps[2 * ((P0["even_qk"] + u) % 2) + m][:, 0:N2]).then_inc(qk_ready, 1)
                    split_in("even_qk", i, 2, u)

            def values(name, dst, ready):
                def turn(i):
                    for u in range(2):
                        b = 2 * ((P0[name] + u) % 2)
                        dve.wait_ge(mm_done, E0[name] + 2 * i + u + 1)
                        for t, (r0, bank, c) in enumerate([(0, b, 0), (0, b, 256), (64, b + 1, 0)]):
                            n = TOK[t][1]
                            V.tensor_copy(dst[0:n, t, at(256 * (2 * i + u), 256)], ps[bank][r0:r0 + n, c:c + 256]).then_inc(ready, 1)
                        split_in(name, i, 2, u)
                return turn

            repeat(dve, 4, even_qk)
            repeat(dve, 2, values("even_v", ve, ve_ready))
            dve.wait_ge(fb_done, 1)
            V.tensor_scalar(fg[:, 0, :], ps[7][0:8, 0:N2], f_bias[:, 0:1], None, ALU.add).then_inc(fz_ready, 1)
            dve.wait_ge(fl_ready, 1)
            link(V.scalar_tensor_tensor(fg[:, 1, :], fg[:, 0, :], 0.0, fg[:, 3, :], ALU.min, ALU.subtract))
            link(V.tensor_tensor_scan(fg[:, 2, :], ones_row[:, :], fg[:, 1, :], 0.0, ALU.mult, ALU.add))
            V.tensor_scalar(fg[:, 0, :], fg[:, 2, :], -1.0 / SC2, None, ALU.mult).then_inc(cum_ready, 1)
            dve.wait_ge(table_in, 32)
            for i in range(len(UNITS) + 4):
                if i < len(UNITS):
                    t, diff, hd, m = UNITS[i]
                    n, w = TOK[t][1], SEEN[t]
                    dve.wait_ge(u_s_done, i + 1)
                    wait(dve, u_exp, i - 1)
                    mask = alibi[0:n, hd, t, 0:w] if diff else mask2[0:n, t, 0:w]
                    V.tensor_tensor_reduce(s2[0:n, i % 2, 0:w], ps[4 + i % 2][0:n, 0:w], mask, 1.0, -3.0e38,
                                           ALU.add, ALU.max, small[0:n, i, 0:1]).then_inc(u_max, 1)
                    dve.wait_ge(u_max, i + 1)
                    V.tensor_scalar(small[0:n, i, 1:2], small[0:n, i, 0:1], -SC2, None, ALU.mult).then_inc(u_bias, 1)
                if 1 <= i <= len(UNITS):
                    u = i - 1
                    t, diff, hd, m = UNITS[u]
                    n, w = TOK[t][1], SEEN[t]
                    pu, inv = p2[0:n, u % 4, 0:w], small[0:n, u, 3:4]
                    dve.wait_ge(u_exp, u + 1)
                    link(V.reciprocal(inv, small[0:n, u, 2:3]))
                    if diff and m == 1:
                        link(V.tensor_tensor(inv, inv, neg_lam[0:n, :], ALU.mult))
                        dve.wait_ge(u_pn, u)
                        V.scalar_tensor_tensor(pu, pu, inv, p2[0:n, (u - 1) % 4, 0:w], ALU.mult, ALU.add).then_inc(u_pn, 1)
                    else:
                        V.tensor_scalar(pu, pu, inv, None, ALU.mult).then_inc(u_pn, 1)
                if i >= 4:
                    t, diff, hd, m = UNITS[i - 4]
                    if not diff and hd % 2 == 1:
                        g = 12 + (ORDER[i - 4] - 12) // 2
                        q0, nq = TOK[t]
                        dve.wait_ge(u_ohi, g + 1)
                        V.tensor_tensor(xl[:, 4 + hd // 2, q0:q0 + nq], ps[2 + g % 2][:, 0:nq], f32(xh[:, 4 + hd // 2, q0:q0 + nq]),
                                        ALU.subtract).then_inc(u_o, 1)
            sub_gain = small[:, 63, 0:1]
            link(V.tensor_scalar(sub_gain, c2("diff_subln_g_2", 0), 1.0 - LAM_INIT, None, ALU.mult))
            for hd in range(4):
                dve.wait_ge(oarstd, hd + 1)
                V.scalar_tensor_tensor(oa[:, hd, :], oa[:, hd, :], sub_gain, oasq[:, hd, :], ALU.mult, ALU.mult).then_inc(oan, 1)
            for hd in range(4):
                dve.wait_ge(oa_hi, hd + 1)
                V.tensor_tensor(xl[:, hd, :], oa[:, hd, :], f32(xh[:, hd, :]), ALU.subtract).then_inc(oa_lo, 1)

            def layer_var(n, j, cols):
                dve.wait_ge(mu_ready, j + 1)
                V.scalar_tensor_tensor(var[:, cols], ps[4][:, 0:size(cols)], 1.0 / D, musq[:, cols], ALU.mult, ALU.subtract).then_inc(var_ready, 1)
                dve.wait_ge(rstd_ready, n + 1)

            def layer_apply(n, j, k, cols):
                V.tensor_tensor(y[:, at(k), cols], y[:, at(k), cols], mu[:, cols], ALU.add).then_inc(sub_ready, 1)
                dve.wait_ge(sub_ready, KD * j + k + 1)
                V.tensor_tensor(y[:, at(k), cols], y[:, at(k), cols], rstd[:, n % 3, cols], ALU.mult).then_inc(norm_ready, 1)

            def raw_tiles(event, bank, slot, n, done, used, cols):
                w = size(cols)
                dve.wait_ge(mm_done, event)
                wait(dve, raw_ready, done)
                for m in range(2):
                    V.scalar_tensor_tensor(ta[:, m, cols], mu[:, cols], ps[bank + m][:, w:w + 1], ps[bank + m][:, 0:w], ALU.mult, ALU.add).then_inc(raw_sub, 1)
                wait(dve, *used)
                for m in range(2):
                    ins = V.tensor_copy(b_col[:, slot + m:slot + m + 1], ps[bank + m][:, w + 1:w + 2])
                ins.then_inc(raw_out, 1)
                for m in range(2):
                    dve.wait_ge(raw_sub, done + m + 1)
                    V.tensor_tensor(rw[:, slot + m, cols], ta[:, m, cols], rstd[:, n % 3, cols], ALU.mult).then_inc(raw_ready, 1)

            def ffn_up(name, base, j, cols):
                raw0 = base + (16 if j else 0)

                def turn(i):
                    for u in range(2):
                        if u == 0 and is_first(i):
                            layer_var(S_LN + j, j, cols)
                        t = 4 * i + 2 * u
                        raw_tiles(E0[name] + 2 * i + u + 1, 2 * ((P0[name] + u) % 2), 2 * u, S_LN + j, raw0 + t, (relu_ready, base + t - 2), cols)
                        split_in(name, i, 2, u)
                    layer_apply(S_LN + j, j, i, cols)

                repeat(dve, 8, turn)

            residual(S_LN, "even_out", 1, 0, X_LN0, ALL)
            ffn_up("ffn_up0", 0, 0, ALL)
            residual(S_LN + 1, "ffn_down0", 4, 1, X_LN1, ALL)
            low = 0
            for c in range(8):
                if c == 0:
                    layer_var(S_LN + 1, 1, ALL)
                raw_tiles(E0["ret_qk"] + c + 1, 2 * ((P0["ret_qk"] + c) % 2), 2 * (c % 2), S_LN + 1, FT2 + 2 * c, (rqk_ready, 2 * c - 2),
                          LAST if c < 4 else ALL)
                split_at(C0["ret_qk"] + c + 2)
                for k in RET_TILES[c]:
                    layer_apply(S_LN + 1, 1, k, ALL)
                for k in RET_TILES[c - 1] if c else ():
                    x_low(X_RET, k, h[:, k, :], cols=ALL)

            repeat(dve, 4, values("ret_v", rv, rv_ready))
            dve.wait_ge(decay_in, 16)
            for u in range(3 * RH + 6):
                if u < 3 * RH:
                    hd, st = u // 3, u % 3
                    t0, sn = TOK[st]
                    dve.wait_ge(rs_done, u + 1)
                    if st == 0 and hd >= 2:
                        dve.wait_ge(ro_done, 4 * (hd - 1))
                    t0 = max(t0, META)
                    V.tensor_tensor(rs[0:sn, hd % 2, st, t0:N2], ps[4 + u % 2][0:sn, t0:N2], decay[0:sn, hd, st, t0:N2], ALU.mult).then_inc(rs_ready, 1)
                if u % 3 == 2 and u >= 8:
                    hd = u // 3 - 2
                    dve.wait_ge(r_rstd_ready, hd + 1)
                    for q in range(4):
                        ins = V.tensor_tensor(rqk[:, hd, q, LAST], rqk[:, hd, q, LAST], r_rstd[:, LAST], ALU.mult)
                    ins.then_inc(ron_ready, 1)
            dve.wait_ge(ron_ready, RH)
            o_tiles = rqk[:, :, :, :].rearrange("p h q n -> p (h q) n")

            def ret_gate(i):
                for u in range(2):
                    for m in range(2):
                        t = 4 * i + 2 * u + m
                        dve.wait_ge(silu2_ready, t + 1)
                        if not is_first(i):
                            dve.wait_ge(y_ready, t - 3)
                        V.tensor_tensor(fa[:, 2 * u + m, LAST], ra[:, 2 * u + m, LAST], o_tiles[:, at(t), LAST], ALU.mult).then_inc(y_mul, 1)
                    split_in("ret_g", i, 2, u)

            repeat(dve, 4, ret_gate)
            residual(S_LN + 2, "ret_out", 2, 2, X_LN2, LAST)
            ffn_up("ffn_up1", FT2, 2, LAST)
            residual(S_LN + 3, "ffn_down1", 4, 3, 0, LAST)
            layer_var(S_LN + 3, 3, LAST)
            for k in range(KD):
                layer_apply(S_LN + 3, 3, k, LAST)
            for n in range(4):
                half, t = n // 2, n % 2
                dve.wait_ge(ot_done, n + 1)
                V.tensor_copy(otok[:, t, 512 * half:512 * half + 512], ps[2 * t + half][:, :]).then_inc(ot_ready, 1)

        @block.tensor
        def _(pe):
            T = nc.tensor
            rows_x, rows_q, rows_r, rows_f, rows_g = (xh, xl), (qxh, qxl), (xrh, xrl), (fh, fl), (gh, gl)

            def three(dst, w, x, first, last):
                T.matmul(dst, w[0], x[0], start=first, stop=False)
                T.matmul(dst, w[0], x[1], start=False, stop=False)
                return T.matmul(dst, w[1], x[0], start=False, stop=last)

            def tile(slot, at0, n):
                return whi[:, slot, at0:at0 + n], wlo[:, slot, at0:at0 + n]

            def product(c, slot, outs, x, at_x, cols, kt=KD, k0=0, first=True, last=True, ready=None, order=None):
                order = order or range(kt)
                halves = 0
                for n, k in enumerate(order):
                    half = 1 if (k + 1) * cols <= CH // 2 else 2
                    if half > halves:
                        pe.wait_ge(w_lo_ready, 2 * c + half)
                        halves = half
                    if ready is not None:
                        ready(k0 + k)
                    for dst, col, m in outs:
                        ins = three(dst, tile(slot, k * cols + col, m), [v[:, k0 + k, at_x] for v in x],
                                    first and n == 0, last and n == kt - 1)
                return ins

            def pair(name, u, width):
                b = 2 * ((P0[name] + u) % 2)
                return [(ps[b + m][:, 0:width], P * m, P) for m in range(2)]

            def x_from(base):
                return lambda k: pe.wait_ge(x_ready, base + k + 1)

            def f_from(base):
                return lambda k: pe.wait_ge(f_ready, base + k + 1)

            def outputs(name, turns, at_x, x, ready, free, per_pair, behind=None, first=0):
                def turn(i):
                    for u in range(2):
                        j = first + 2 * i + u
                        wait(pe, free, per_pair(j - 2))
                        start = u == 0 and is_first(i)
                        product(C0[name] + j, (C0[name] + u) % 2, pair(name, u, size(at_x)), x, at_x, 256,
                                ready=ready if start else None).then_inc(mm_done, 1)
                        if start and behind is not None:
                            behind()
                repeat(pe, turns, turn)

            def outputs_deep(name, n, at_x, x, depth, ready, behind=None):
                kts = [min(8, depth - 8 * j) for j in range((depth + 7) // 8)]
                with pe.Fori(0, 2) as i:
                    for u in range(2):
                        pe.wait_ge(tile_ready, TILES[n] + 4 * i + 2 * u - 2)
                        for q, kt in enumerate(kts):
                            k = len(kts) * u + q
                            product(C0[name] + 2 * len(kts) * i + k, (C0[name] + k) % 2, pair(name, u, size(at_x)), x, at_x, 256, kt=kt,
                                    k0=8 * q, first=q == 0, last=q == len(kts) - 1, ready=ready if u == 0 else None).then_inc(mm_done, 1)

            def stat(n, cols=None):
                pe.wait_ge(acc_ready, KD * n + KD)
                if cols is not None:
                    T.matmul(ps[5][:, 0:size(cols)], ones[:, :], acc1[:, cols], start=True, stop=True)
                cols = cols or TOK1
                T.matmul(ps[4][:, 0:size(cols)], ones[:, :], acc2[:, cols], start=True, stop=True).then_inc(stat_ready, 1)

            TOK1 = slice(0, N1)
            pe.wait_ge(ident_in, 16)
            pe.wait_ge(x_in, 32)
            for k in range(KD):
                if k == 1:
                    pe.wait_ge(g_in, 16)
                    T.transpose(ps[0][:, 0:KD], g_rows[:, :], ident[0:KD, 0:KD]).then_inc(cols_t, 1)
                wait(pe, tile_ready, k - 3)
                for t in range(2):
                    ins = T.transpose(ps[4 + k % 4][:, P * t:P * t + P], xt[:, t, P * k:P * k + P], ident[:, :])
                ins.then_inc(xt_done, 1)
            pe.wait_ge(cols_ready, 1)
            pe.wait_ge(tile_ready, KD)

            def others():
                pe.wait_ge(small_in, 16 * (len(ROWS2) + 5))
                T.transpose(ps[7][:, 0:R2N], rows2[:, :], ident[0:R2N, 0:R2N])
                pe.wait_ge(rows1_in, 16 * len(ROWS1))
                T.transpose(ps[7][:, 2 * P:2 * P + R1N], rows1[:, :], ident[0:R1N, 0:R1N])
                for m in range(CT):
                    ins = T.transpose(ps[7][:, P + TAPS * m:P + TAPS * m + TAPS], cw_rows[:, P * m:P * m + P], ident[0:TAPS, 0:TAPS])
                ins.then_inc(cols_t, 1)
                for k in range(KD):
                    ins = T.transpose(ps[5][:, META * k:META * k + META], meta_rows[:, P * k:P * k + P], ident[0:META, 0:META])
                ins.then_inc(meta_done, 1)
                pe.wait_ge(pos_in, 48)
                for kt in range(2):
                    for t in range(2):
                        ins = T.transpose(ps[6][:, N1 * kt + P * t:N1 * kt + P * t + P], pt[:, t, P * kt:P * kt + P], ident[:, :])
                ins.then_inc(pt_done, 1)

            for j in range(3):
                if j == 2:
                    pe.wait_ge(qkv_ready, 2)
                outs = pair("qkv_in", j, N1)
                if j == 2:
                    outs[1] = (outs[1][0][0:QHEAD], NOPE, QHEAD)
                product(C0["qkv_in"] + j, (C0["qkv_in"] + j) % 2, outs, rows_x, TOK1, 256 if j < 2 else P + ROPE,
                        ready=x_from(X_A) if j == 0 else None).then_inc(mm_done, 1)
                if j == 0:
                    stat(S_X)
                    others()
            for m in range(CT):
                pe.wait_ge(qkv_ready, 4 + 2 * m) if m < 2 else pe.wait_ge(g_scaled, m - 1)
                product(C0["conv_in"] + m, (C0["conv_in"] + m) % 2, pair("conv_in", m, N1), rows_x, TOK1, 256).then_inc(mm_done, 1)
                if m == 0:
                    pe.wait_ge(qkv_ready, 6)
                    pe.wait_ge(meta_ready, 1)
                    pe.wait_ge(const_in, 32)
                    T.matmul(ps[5][0:QHEAD, 0:N1], rot[:, :], qkv[0:QHEAD, 5, :], start=True, stop=True).then_inc(krot_done, 1)
                    pe.wait_ge(p_ready, 1)
                    pe.wait_ge(cols_ready, 3)
                    for t in range(5):
                        j, n = (0, t) if t < 3 else (1, t - 3)
                        pe.wait_ge(sq6_ready, t + 1)
                        ins = T.matmul(ps[6 + j][:, 0:N1], ones[:, :], sq6[:, t, :], start=n == 0, stop=n == (2, 1)[j])
                        if n == (2, 1)[j]:
                            ins.then_inc(lstat_ready, 1)
            for j in range(4):
                c = C0["q"] + j // 2
                pe.wait_ge(g_scaled, 3 + j) if j < 2 else pe.wait_ge(q_ready, j - 1)
                outs = [(ps[2 * ((P0["q"] + j) % 2) + m][0:QHEAD, 0:N1], QHEAD * (2 * (j % 2) + m), QHEAD) for m in range(2)]
                product(c, c % 2, outs, rows_q, TOK1, 4 * QHEAD, kt=3, ready=x_from(X_QKV) if j == 0 else None).then_inc(mm_done, 1)
            pe.wait_ge(lrstd_ready, 2)
            pe.wait_ge(krope_ready, 1)
            c = C0["kv"]
            for j in range(4):
                pe.wait_ge(q_ready, 3 + j) if j < 2 else pe.wait_ge(k_ready, j - 1)
                outs = [(ps[2 * ((P0["kv"] + j) % 2) + m][:, 0:N1], P * (2 * j + m), P) for m in range(2)]
                product(c, c % 2, outs, rows_q, TOK1, D, kt=2, k0=3, ready=x_from(X_QKV)).then_inc(mm_done, 1)
                pe.wait_ge(q_ready, j + 1)
                T.matmul(ps[4 + j][0:QHEAD, :], rot[:, :], qt[0:QHEAD, 2 * j:2 * j + 2, :], start=True, stop=True).then_inc(qrot_done, 1)
            pe.wait_ge(k_ready, 3)
            b = 2 * ((P0["kv"] + 4) % 2)
            for t in range(2):
                for k in range(2):
                    wv = [v[:, c % 2, D * k:D * k + D].rearrange("p (h c) -> p h c", c=P)[:, :, NOPE:] for v in (whi, wlo)]
                    xv = [v[:, 3 + k, P * t:P * t + P] for v in rows_q]
                    ins = three(ps[b + t][:, :], xv, wv, k == 0, k == 1)
            ins.then_inc(mm_done, 1)
            pe.wait_ge(k_ready, 4)
            pe.wait_ge(v_ready, 2)
            for i in range(16 + 4):
                if i < 16:
                    t, hd = i // 8, i % 8
                    wait(pe, max_ready, i - 1)
                    if i < 8:
                        pe.wait_ge(qrope_ready, max(2, i // 2 + 1))
                    T.matmul(ps[4 + i % 2][:, 0:P * (t + 1)], qt[0:QHEAD, hd, P * t:P * t + P], kt_[0:QHEAD, hd, 0:P * (t + 1)],
                             start=True, stop=True).then_inc(s_done, 1)
                if 3 <= i < 19:
                    u = i - 3
                    pe.wait_ge(pn_ready, u + 1)
                    wait(pe, pT_ready, u - 1)
                    pe.wait_ge(qrope_ready, 4)
                    for b in range(u // 8 + 1):
                        ins = T.transpose(ps[6 + u % 2][:, P * b:P * b + P], p1[:, u % 4, P * b:P * b + P], ident[:, :])
                    ins.then_inc(t_done, 1)
                if i >= 4:
                    u = i - 4
                    t, hd, g, s = u // 8, u % 8, u // 2, u % 2
                    pe.wait_ge(pT_ready, u + 1)
                    wait(pe, o_ready, g - 1)
                    for b in range(t + 1):
                        ins = T.matmul(ps[2 + g % 2][64 * s:64 * s + 64, 0:P], v1[:, b, VDIM * hd:VDIM * hd + VDIM], pt1[:, u % 2, b, :],
                                       start=b == 0, stop=b == t)
                    ins.then_inc(pv_done, 1)
            pe.wait_ge(max_ready, 16)
            for m in range(CT):
                pe.wait_ge(csq_ready, m + 1)
                T.matmul(ps[4][:, 0:N1], ones[:, :], cv[:, m, :], start=m == 0, stop=m == CT - 1)
                ins = T.matmul(ps[5][:, 0:N1], ones[:, :], sq6[:, m, :], start=m == 0, stop=m == CT - 1)
            ins.then_inc(cstat_ready, 1)
            def mixed(k):
                pe.wait_ge(o_ready, 4 + k + 1) if k < 4 else pe.wait_ge(c_ready, k - 3)

            pe.wait_ge(lam_one, 1)
            pe.wait_ge(pT_ready, 16)
            T.matmul(ps[6][:, 0:1], ones[0:1, :], lam_s[:, 4:5], start=True, stop=True).then_inc(lam_done, 1)
            outputs("mix_out", 2, TOK1, rows_x, mixed, tile_ready, lambda j: TILES[S_MIX] + 2 * j + 2 if not isinstance(j, int) or j >= 0 else 0)
            pe.wait_ge(p_ready, 1)
            pe.wait_ge(w_lo_ready, 2 * (C0["ple"] + 1))
            for j in range(4):
                pe.wait_ge(tile_ready, TILES[S_MIX] + 6 + 2 * j) if j < 2 else pe.wait_ge(e_copied, j - 1)
                b = 2 * ((P0["ple"] + j) % 2)
                for k in range(2):
                    for m in range(2):
                        ins = three(ps[b + m][:, 0:N1], tile(C0["ple"] % 2, D * k + N1 * j + P * m, P), (ph[:, k, :], pl[:, k, :]), k == 0, k == 1)
                ins.then_inc(mm_done, 1)
                if j == 1:
                    stat(S_MIX)
            pe.wait_ge(e_copied, 4)
            outputs("gate_up", FT // 2, TOK1, rows_x, x_from(X_FFN), gv_scaled, lambda j: j + 1, behind=lambda: stat(S_PRE))
            pe.wait_ge(gv_scaled, FT)
            kts = (8, 8, 6)
            for j in range(4):
                pe.wait_ge(tile_ready, TILES[S_FFN] + 2 * j - 2)
                for q, kt in enumerate(kts):
                    c = C0["down"] + 3 * j + q
                    product(c, c % 2, pair("down", j, N1), rows_f, TOK1, 256, kt=kt, k0=8 * q, first=q == 0, last=q == 2,
                            ready=f_from(0) if j == 0 else None).then_inc(mm_done, 1)
                if j == 1:
                    stat(S_E)
            stat(S_FFN)
            outputs("ple_gate", 2, TOK1, rows_x, x_from(X_PLE), sig_ready, lambda j: 2 * j + 2)
            outputs("even_qk", 4, ALL, rows_r, x_from(X_B), qk_ready, lambda j: 2 * j + 2)

            def values(name, turns, x, free):
                def turn(i):
                    for u in range(2):
                        j = 2 * i + u
                        slot, b = (C0[name] + u) % 2, 2 * ((P0[name] + u) % 2)
                        wait(pe, free, 3 * (j - 1))
                        pe.wait_ge(w_lo_ready, 2 * (C0[name] + j + 1))
                        for q0, bank, c in ((0, b, 0), (TOK[1][0], b, 256), (N2 - P, b + 1, 0)):
                            for k in range(KD):
                                ins = three(ps[bank][:, c:c + 256], [v[:, k, q0:q0 + P] for v in x], tile(slot, 256 * k, 256), k == 0, k == KD - 1)
                        ins.then_inc(mm_done, 1)
                repeat(pe, turns, turn)

            pe.wait_ge(qk_ready, 16)
            values("even_v", 2, rows_r, ve_ready)
            for k in range(KD):
                ins = T.matmul(ps[7][0:8, 0:N2], wf[:, k, :], h[:, k, :], start=k == 0, stop=k == KD - 1)
            ins.then_inc(fb_done, 1)
            pe.wait_ge(ve_ready, 12)
            pe.wait_ge(fz_ready, 1)
            for i in range(len(UNITS) + 4):
                if i < len(UNITS):
                    t, diff, hd, m = UNITS[i]
                    (q0, n), w = TOK[t], SEEN[t]
                    wait(pe, u_max, i - 1)
                    s = ps[4 + i % 2][0:n, 0:w]
                    if diff:
                        r = slice(64 * m, 64 * m + 64)
                        ins = T.matmul(s, qk[r, hd, q0:q0 + n], qk[r, 4 + hd, 0:w], start=True, stop=True)
                    else:
                        r = slice(64 * (hd % 2), 64 * (hd % 2) + 64)
                        T.matmul(s, qk[r, 8 + hd // 2, q0:q0 + n], qk[r, 12 + hd // 2, 0:w], start=True, stop=False)
                        pe.wait_ge(cum_ready, 1)
                        ins = T.matmul(s, ident[0:8, hd:hd + 1].broadcast_to([8, n]), fg[:, 0, 0:w], start=False, stop=True)
                    ins.then_inc(u_s_done, 1)
                if i >= 3 and i - 3 in ORDER:
                    t, o = UNITS[i - 3][0], ORDER[i - 3]
                    nq = TOK[t][1]
                    pe.wait_ge(u_pn, i - 2)
                    wait(pe, u_pT, o - 1)
                    for b in range(t + 1):
                        k0, kn = TOK[b]
                        ins = T.transpose(ps[6 + o % 2][0:kn, P * b:P * b + nq], p2[0:nq, (i - 3) % 4, k0:k0 + kn], ident[0:nq, 0:nq])
                    ins.then_inc(u_t_done, 1)
                if i >= 4 and i - 4 in ORDER:
                    t, diff, hd, m = UNITS[i - 4]
                    o, nq = ORDER[i - 4], TOK[UNITS[i - 4][0]][1]
                    pe.wait_ge(u_pT, o + 1)
                    if diff:
                        g, r, v0, vn = o, slice(0, P), P * hd, P
                        wait(pe, u_ohi, g - 1)
                    else:
                        g, r, v0, vn = 12 + (o - 12) // 2, slice(64 * (hd % 2), 64 * (hd % 2) + 64), 512 + 64 * hd, 64
                        pe.wait_ge(u_ohi, g - 1) if g < 14 else pe.wait_ge(u_o, g - 13)
                    for b in range(t + 1):
                        kn = TOK[b][1]
                        ins = T.matmul(ps[2 + g % 2][r, 0:nq], ve[0:kn, b, v0:v0 + vn], pt2[0:kn, o % 2, b, 0:nq], start=b == 0, stop=b == t)
                    ins.then_inc(u_pv, 1)
            pe.wait_ge(u_max, len(UNITS))
            pe.wait_ge(u_pT, len(OUTS))
            for hd in range(4):
                pe.wait_ge(oasq_ready, hd + 1)
                T.matmul(ps[4 + hd][:, 0:N2], ones[:, :], oasq[:, hd, :], start=True, stop=True).then_inc(oastat, 1)

            def even_mix(k):
                pe.wait_ge(oa_lo, k + 1) if k < 4 else pe.wait_ge(u_o, 12)

            for j in range(4):
                wait(pe, tile_ready, TILES[S_LN] + 2 * (j - 1) if j >= 2 else 0)
                product(C0["even_out"] + j, (C0["even_out"] + j) % 2, pair("even_out", j, N2), rows_x, ALL, 256,
                        ready=even_mix if j == 0 else None, order=[4, 5, 6, 7, 0, 1, 2, 3]).then_inc(mm_done, 1)

            def raw(cols):
                return slice(cols.start, N2 + 2)

            def mlp(j, layer, x0, raw0, hidden0, cols):
                outputs(f"ffn_up{layer}", FT2 // 4, raw(cols), rows_r, x_from(x0), raw_out,
                        lambda t: raw0 + t + 1 if not isinstance(t, int) or t >= 0 else 0, behind=lambda: stat(S_LN + j, cols))
                pe.wait_ge(raw_out, raw0 + FT2 // 2)
                outputs_deep(f"ffn_down{layer}", S_LN + j + 1, cols, rows_f, FT2, f_from(hidden0))

            mlp(0, 0, X_LN0, 0, FT, ALL)
            raw_from = lambda j: FT2 // 2 + j + 1
            outputs("ret_qk", 2, raw(LAST), rows_r, x_from(X_LN1), raw_out, raw_from, behind=lambda: stat(S_LN + 1, ALL))
            outputs("ret_qk", 2, raw(ALL), rows_r, None, raw_out, raw_from, first=4)
            pe.wait_ge(raw_out, FT2 // 2 + 8)
            pe.wait_ge(x_ready, X_RET + KD)
            values("ret_v", 4, rows_x, rv_ready)
            pe.wait_ge(rv_ready, 24)
            pe.wait_ge(rqk_ready, 16)

            def ret_scores(hd):
                for st in range(3):
                    u = 3 * hd + st
                    t0, sn = TOK[st]
                    wait(pe, rs_ready, u - 1)
                    tq = max(t0, META)
                    for kt in range(2):
                        ins = T.matmul(ps[4 + u % 2][0:sn, tq:N2], rqk[:, hd, 2 + kt, t0:t0 + sn], rqk[:, hd, kt, tq:N2], start=kt == 0, stop=kt == 1)
                    ins.then_inc(rs_done, 1)

            def ret_stat(n):
                hd = n // 4
                pe.wait_ge(rsq_ready, n + 1)
                wait(pe, r_rstd_ready, hd - 1)
                T.matmul(ps[hd % 2][:, 0:N1], ones[:, :], rsq[:, n % 2, LAST], start=n % 4 == 0, stop=n % 4 == 3).then_inc(rstat, 1)

            ret_scores(0)
            for hd in range(RH):
                if hd + 1 < RH:
                    ret_scores(hd + 1)
                pe.wait_ge(rs_ready, 3 * hd + 3)
                for q in range(4):
                    n = 4 * hd + q
                    wait(pe, ro_ready, n - 1)
                    for st in range(3):
                        t0, sn = max(TOK[st][0], META), TOK[st][1]
                        ins = T.matmul(ps[6 + n % 2][:, t0 - META:N1], rv[0:sn, st, RV * hd + P * q:RV * hd + P * q + P], rs[0:sn, hd % 2, st, t0:N2],
                                       start=st == 0, stop=st == 2)
                    ins.then_inc(ro_done, 1)
                    if n >= 1:
                        ret_stat(n - 1)
            ret_stat(4 * RH - 1)
            pe.wait_ge(r_rstd_ready, RH)
            outputs("ret_g", 4, LAST, rows_x, None, silu2_ready, lambda j: 2 * j + 2)
            pe.wait_ge(silu2_ready, 16)
            outputs_deep("ret_out", S_LN + 2, LAST, rows_g, 16, lambda k: pe.wait_ge(y_ready, k + 1))
            mlp(2, 1, X_LN2, FT2 // 2 + 8, FT + FT2, LAST)
            stat(S_LN + 3, LAST)
            for k in range(KD):
                pe.wait_ge(hn_ready, 3 * KD + k + 1)
                for t in range(2):
                    ins = T.transpose(ps[2 * t + k // 4][:, P * (k % 4):P * (k % 4) + P], h[:, k, META + P * t:META + P * t + P], ident[:, :])
                    if k % 4 == 3:
                        ins.then_inc(ot_done, 1)


INPUTS = ["x", "p", "positions", "g_mix_pre", "w_in", "g_q_a", "w_q_b", "g_kv_a", "w_kv_b", "conv_w", "conv_b", "conv_ln_g",
          "conv_ln_b", "w_o", "g_mix_post", "g_ffn_pre", "w_ffn_gate", "w_ffn_up", "ffn_dw_w", "ffn_dw_b", "w_ffn_down",
          "g_ffn_post", "w_ple_proj", "g_ple", "w_ple_gate", "meta_tokens_2", "even_w_in_2", "even_f_bias_2", "diff_lambda_2",
          "diff_subln_g_2", "even_w_out_2", "ret_w_in_2", "ret_w_out_2", "ln_g_2", "ln_b_2", "ffn_w1_2", "ffn_w2_2"]


def constants():
    c = {"c_ident": np.eye(P)}
    rot = np.zeros((QHEAD, QHEAD))
    half = ROPE // 2
    for m in range(half):
        rot[NOPE + half + m, NOPE + m] = -1.0
        rot[NOPE + m, NOPE + half + m] = 1.0
    c["c_rot"] = rot
    row, col = np.arange(P)[:, None], np.arange(P)[None, :]
    c["c_mask1"] = np.concatenate([np.zeros((P, P)), np.where(col <= row, 0.0, NEG)], axis=1)
    pos = np.arange(N2)
    chunk = (pos + CHUNK - META) // CHUNK
    mask2, alibi, decay = np.zeros((P, 3, N2)), np.zeros((P, 4, 3, N2)), np.zeros((P, 4, 3, N2))
    for t, (q0, n) in enumerate(TOK):
        q = pos[q0:q0 + n]
        mask2[0:n, t] = np.where(pos[None, :] <= q[:, None], 0.0, NEG)
        dist = np.abs(q[:, None] - pos[None, :])
        for hd in range(4):
            slope = 2.0 ** (-8.0 * (hd + 1) / 4)
            alibi[0:n, hd, t] = np.where(chunk[None, :] <= chunk[q][:, None], -slope * dist / SC2, NEG)
            gamma = 1.0 - 2.0 ** (-5.0 - hd)
            decay[0:n, hd, t] = np.where(chunk[q][:, None] <= chunk[None, :], gamma ** dist * RQK ** -0.5, 0.0)
    c["c_mask2"], c["c_alibi"], c["c_decay"] = mask2, alibi, decay
    c["c_freq"] = np.tile(10000.0 ** (-np.arange(0, ROPE, 2) / ROPE), 2)[:, None]
    return {name: np.ascontiguousarray(v.astype(np.float32)) for name, v in c.items()}


def kernel(**inputs):
    import concourse.bacc as bacc
    from concourse.bass_utils import run_bass_kernel_spmd

    nc = bacc.Bacc("TRN2", target_bir_lowering=False, num_devices=1)
    arrays = {name: np.ascontiguousarray(inputs[name]) for name in INPUTS}
    arrays.update(constants())
    a = {name: nc.dram_tensor(name, v.shape, mybir.dt.from_np(v.dtype), kind="ExternalInput").ap() for name, v in arrays.items()}
    out = nc.dram_tensor("result", (1, N1, D), F32, kind="ExternalOutput").ap()
    build(nc, a, out)
    r = run_bass_kernel_spmd(nc, [arrays], core_ids=[0])
    return r.results[0]["result"]
```

```python
from contextlib import ExitStack

import numpy as np

import concourse.bass as bass
from concourse import mybir

F32 = mybir.dt.float32
F32R = mybir.dt.float32r
I32 = mybir.dt.int32
ALU = mybir.AluOpType
ACT = mybir.ActivationFunctionType
AX = mybir.AxisListType

P = 128
D = 1024
KD = D // P
N1 = 256
META = 16
N2 = N1 + META
HEADS, NOPE, ROPE, VDIM = 8, 64, 32, 64
QHEAD = NOPE + ROPE
QLORA, KVLORA = 384, 256
CONV_C, TAPS = 512, 31
CT = CONV_C // P
FF, FT = 2816, 2816 // P
PLE = 256
FF2, FT2 = 4096, 4096 // P
RH, RQK, RV = 4, 256, 512
CHUNK = 64
EPS1, LN_EPS, RMS_EPS = 1e-6, 1e-5, 1e-6
ALPHA = 4.0 ** 0.25
LAM_INIT = 0.2
SC1 = QHEAD ** -0.5
SC2 = 64 ** -0.5
NEG = -1.0e30
TOK = [(0, 80), (80, 128), (208, 64)]
SEEN = [80, 208, 272]
CH = 2048

STAGES = [("qkv_in", 3, 3), ("conv_in", 4, 4), ("q", 2, 4), ("kv", 1, 5), ("mix_out", 4, 4), ("ple", 1, 4),
          ("gate_up", 22, 22), ("down", 12, 4), ("ple_gate", 4, 4), ("even_dqk", 4, 4), ("even_v0", 2, 2),
          ("even_fqk", 4, 4), ("even_v1", 2, 2),
          ("even_out", 4, 4), ("ffn_up0", 16, 16), ("ffn_down0", 16, 4), ("ret_qk", 8, 8), ("ret_v", 8, 8),
          ("ret_g", 8, 8), ("ret_out", 8, 4), ("ffn_up1", 16, 16), ("ffn_down1", 16, 4)]
C0, P0, E0, PER = {}, {}, {}, {}
CHUNK_END = []
_p = _e = 0
for _name, _nc, _np in STAGES:
    C0[_name], P0[_name], E0[_name], PER[_name] = len(CHUNK_END), _p, _e, max(1, _nc // _np)
    _n = max(_nc, _np)
    CHUNK_END += [_e + (_n * (j + 1)) // _nc if _name != "kv" else _e + _n for j in range(_nc)]
    _p, _e = _p + _np, _e + _n
CHUNKS = len(CHUNK_END)
assert P0["even_dqk"] % 2 == P0["even_v0"] % 2 == P0["even_fqk"] % 2 == 0

ROWS1 = [("g_mix_post", 8), ("g_ffn_pre", 8), ("g_ffn_post", 8), ("g_ple", 8), ("ln_g_2", 32), ("ln_b_2", 32)]
ROWS2 = [("ffn_dw_w", 66), ("ffn_dw_b", 22), ("conv_b", 4), ("conv_ln_g", 4), ("conv_ln_b", 4), ("g_q_a", 3), ("g_kv_a", 2),
         ("diff_subln_g_2", 1)]


def starts(rows):
    at, out = 0, {}
    for name, n in rows:
        out[name] = at
        at += n
    return out, at


R1AT, R1N = starts(ROWS1)
R2AT, R2N = starts(ROWS2)

UNITS = [(t, True, h, m) for t in (2, 1, 0) for h in range(4) for m in range(2)] + \
        [(t, False, h, 0) for h0 in (0, 4) for t in (2, 1, 0) for h in range(h0, h0 + 4)]
OUTS = [i for i, (t, d, h, m) in enumerate(UNITS) if not d or m == 1]
ORDER = {i: n for n, i in enumerate(OUTS)}
T_LAG, V_LAG = 4, 5
P2, PT2 = 4, 3
DIFF = 24
WITH = [range(4 * c, 4 * c + 4) for c in range(6)] + [range(24, 29), range(29, 34)]
ALONE = WITH[-1].stop
EVAC_AT, HI_AT, LO_AT = 0, (0, 1), (1, 2)
LEAD = (1, 2)
FORGET = DIFF + 11 + V_LAG
NORM = ALONE


def score_bank(i):
    return 4 + i % 2 if i < ALONE else (4 + ALONE % 2, 5 - ALONE % 2, 0)[(i - ALONE) % 3]


def out_bank(o):
    return (6 + o % 2, 3 * P) if OUTS[o] < ALONE else (2 + o % 2, 0)


class Count:

    def __init__(self, n=0):
        self.n = n

    def up(self, by=1):
        self.n = self.n + by
        return self.n


def wait(eng, sem, value):
    if not isinstance(value, int) or value > 0:
        eng.wait_ge(sem, value)


def repeat(eng, turns, body):
    body(0)
    with eng.Fori(1, turns) as i:
        body(i)


def is_first(i):
    return isinstance(i, int) and i == 0


def at(i, n=1):
    return bass.ds(i, n)


def build(nc, a, out):
    with ExitStack() as ctx:
        def sb(name, shape, dt=F32):
            return ctx.enter_context(nc.sbuf_tensor(name, shape, dt))

        def sem(name):
            return ctx.enter_context(nc.semaphore(name))

        raw = sb("raw", [P, 2, CH])
        whi = sb("whi", [P, 2, CH], F32R)
        wlo = sb("wlo", [P, 2, CH], F32R)
        xh = sb("xh", [P, KD, N2], F32R)
        xl = sb("xl", [P, KD, N2], F32R)
        h = sb("h", [P, KD, N2])
        y_at = 32 * ((nc.sbuf_base + 31) // 32)
        y = sb("y", [P, KD, N2])
        e_mem = sb("e_mem", [P, KD * N1])
        e = e_mem[:, :].rearrange("p (k n) -> p k n", k=KD)
        rw = e_mem[:, 0:4 * N2].rearrange("p (k n) -> p k n", k=4)
        sq = sb("sq", [P, 2, N2])
        acc1 = sb("acc1", [P, N2])
        acc2 = sb("acc2", [P, N2])
        rstd = sb("rstd", [P, 3, N2])
        lnv = sb("lnv", [P, N2])
        mu = sb("mu", [P, N2])
        musq = sb("musq", [P, N2])
        var = sb("var", [P, N2])
        ta = sb("ta", [P, 2, N2])
        tb = sb("tb", [P, 2, N2])
        b_col = sb("b_col", [P, 4])
        ra = sb("ra", [P, 4, N2])
        fa = sb("fa", [P, 4, N2])
        ident = sb("ident", [P, P])
        ones = sb("ones", [P, P])
        rot = sb("rot", [QHEAD, QHEAD])
        ones_row = sb("ones_row", [8, N2])
        eps = sb("eps", [P, 3])
        g_col = sb("g_col", [P, KD])
        col1 = sb("col1", [P, R1N])
        col2 = sb("col2", [P, R2N])
        lam_rows = sb("lam_rows", [1, 4 * 64])
        lam_s = sb("lam_s", [1, 8])
        neg_lam = sb("neg_lam", [P, 1])
        wf = sb("wf", [P, KD, 8])
        f_bias = sb("f_bias", [8, 1])
        small = sb("small", [P, 64, 4])
        arena0 = 512 * ((nc.sbuf_base + 511) // 512)

        class Arena:
            def __init__(self):
                self.at = arena0

            def __call__(self, name, shape, dt=F32):
                size = 4 * int(np.prod(shape[1:]))
                t = nc.alloc_sbuf_tensor_at(name, shape, dt, offset=self.at)
                self.at += 32 * ((size + 31) // 32)
                return t

        m1 = Arena()
        xt = m1("xt", [P, 2, D])
        qt = nc.alloc_sbuf_tensor_at("qt", [P, HEADS, N1], F32, offset=arena0)
        rows_at = m1.at
        g_rows = m1("g_rows", [KD, P])
        rows1 = m1("rows1", [R1N, P])
        rows2 = m1("rows2", [R2N, P])
        meta_rows = m1("meta_rows", [META, D])
        pt = m1("pt", [P, 2, PLE])
        rows_end = m1.at
        ph = m1("ph", [P, 2, N1], F32R)
        pl = m1("pl", [P, 2, N1], F32R)
        qkv = m1("qkv", [P, 6, N1])
        sq6 = m1("sq6", [P, 5, N1])
        conv_in = m1("conv_in", [P, CT, TAPS - 1 + N1])
        cv = m1("cv", [P, CT, N1])
        cv_part = m1("cv_part", [P, N1])
        qxh = m1("qxh", [P, 5, N1], F32R)
        qxl = m1("qxl", [P, 5, N1], F32R)
        cw_rows = m1("cw_rows", [TAPS, CONV_C])
        cw = m1("cw", [P, CT, TAPS])
        pos_i = m1("pos_i", [QHEAD, N1], I32)
        ang = m1("ang", [QHEAD, 6, N1])
        freq = m1("freq", [QHEAD, 1])
        mask1 = m1("mask1", [P, N1])
        kt_ = m1("kt", [P, HEADS, N1])
        v1 = m1("v1", [P, 2, HEADS * VDIM])
        lr = nc.alloc_sbuf_tensor_at("lr", [P, 2, N1], F32, offset=m1.at)
        s1 = m1("s1", [P, 2, N1])
        p1 = m1("p1", [P, 4, N1])
        pt1 = m1("pt1", [P, 2, 2, P])
        rope_t = m1("rope_t", [QHEAD, 2, 2 * N1])
        diag_low = nc.alloc_sbuf_tensor_at("diag_low", [P, TAPS - 16, P], F32, offset=rows_at)
        assert 4 * P * (TAPS - 16) <= rows_end - rows_at
        diag = [e_mem[:, P * n:P * n + P] for n in range(16)] + [diag_low[:, n, :] for n in range(TAPS - 16)]
        f1 = Arena()
        fh = f1("fh", [P, FT2, N2], F32R)
        fl = f1("fl", [P, FT2, N2], F32R)
        xr_at = f1.at
        xrh = f1("xrh", [P, KD, N2 + 2], F32R)
        xrl = f1("xrl", [P, KD, N2 + 2], F32R)
        gt = nc.alloc_sbuf_tensor_at("gt", [P, 2, 2 + N1], F32, offset=xr_at)
        e1 = Arena()
        qs = e1("qs", [P, 16, N2], F32R)
        ks = e1("ks", [P, 16, N2], F32R)
        ql = nc.alloc_sbuf_tensor_at("ql", [P, KD, N2], F32R, offset=y_at)
        ve = e1("ve", [P, 3, 1024])
        fg = e1("fg", [8, 4, N2])
        fgs = e1("fgs", [104, N2], F32R)
        sel = e1("sel", [104, 8], F32R)
        alibi = e1("alibi", [P, 4, 3, N2])
        mask2 = e1("mask2", [P, 3, N2])
        rsum = (acc1, acc2)
        s2, p2, oa = ta, ra, rw
        pt2 = [mem.rearrange("p (k n) -> p k n", k=3) for mem in
               (e_mem[:, 4 * N2:4 * N2 + 3 * P], e_mem[:, 4 * N2 + 3 * P:4 * N2 + 6 * P], sq[:, :, :].rearrange("p k n -> p (k n)")[:, 0:3 * P])]
        oasq, of = fa, y
        r1 = Arena()
        rqk = r1("rqk", [P, RH, 4, N2])
        r2_at = r1.at
        rv = r1("rv", [P, 3, RH * RV])
        rs = r1("rs", [P, 2, 3, N2])
        rsq = r1("rsq", [P, 2, N2])
        r_rstd = r1("r_rstd", [P, N2])
        decay = r1("decay", [P, 4, 3, N2])
        r2 = Arena()
        r2.at = r2_at
        gh = r2("gh", [P, 16, N2], F32R)
        gl = r2("gl", [P, 16, N2], F32R)
        otok = nc.alloc_sbuf_tensor_at("otok", [P, 2, D], F32, offset=arena0)
        for area in (m1, f1):
            assert area.at <= nc.sbuf_usable_end, (area.at, nc.sbuf_usable_end)
        for area in (e1, r1, r2):
            assert area.at <= xr_at, (area.at, xr_at)

        ps = [ctx.enter_context(nc.psum_tensor(f"ps{b}", [P, 512], F32)) for b in range(8)]

        raw_landed = [sem("raw_landed0"), sem("raw_landed1")]
        w_hi_ready, w_lo_ready = sem("w_hi_ready"), sem("w_lo_ready")
        mm_done = sem("mm_done")
        ident_in, g_in, gates_in, rows1_in, x_in, small_in, const_in, table_in, decay_in, pos_in = sem("ident_in"), sem("g_in"), sem("gates_in"), sem("rows1_in"), sem("x_in"), sem("small_in"), sem("const_in"), sem("table_in"), sem("decay_in"), sem("pos_in")
        set_up, cols_t, cols_ready = sem("set_up"), sem("cols_t"), sem("cols_ready")
        xt_done, meta_done, meta_ready, pt_done, p_hi, p_ready = sem("xt_done"), sem("meta_done"), sem("meta_ready"), sem("pt_done"), sem("p_hi"), sem("p_ready")
        tile_ready, sq_ready, acc_ready, stat_ready, rstd_ready = sem("tile_ready"), sem("sq_ready"), sem("acc_ready"), sem("stat_ready"), sem("rstd_ready")
        mu_ready, var_ready, sub_ready, norm_ready, hn_ready, post_ready, h_ready = (sem(n) for n in ("mu_ready", "var_ready", "sub_ready", "norm_ready", "hn_ready", "post_ready", "h_ready"))
        gb_hi, raw_sub, raw_out, raw_ready = sem("gb_hi"), sem("raw_sub"), sem("raw_out"), sem("raw_ready")
        xh_ready, x_ready = sem("xh_ready"), sem("x_ready")
        dve_chain, act_chain, pool_chain = sem("dve_chain"), sem("act_chain"), sem("pool_chain")
        ang_ready, trig_ready = sem("ang_ready"), sem("trig_ready")
        g_scaled, g_sig, conv_in_ready = sem("g_scaled"), sem("g_sig"), sem("conv_in_ready")
        e_late = sem("e_late")
        e_copied, e_ready, conv_step2, conv_mul = sem("e_copied"), sem("e_ready"), sem("conv_step2"), sem("conv_mul")
        diag_ready, conv_pe, krope_mul = sem("diag_ready"), sem("conv_pe"), sem("krope_mul")
        conv_step, csq_ready, cstat_ready, cmu_ready, cvar_ready, crstd_ready = sem("conv_step"), sem("csq_ready"), sem("cstat_ready"), sem("cmu_ready"), sem("cvar_ready"), sem("crstd_ready")
        cn_ready, silu_ready, c_hi, c_ready = sem("cn_ready"), sem("silu_ready"), sem("c_hi"), sem("c_ready")
        qkv_ready, sq6_ready, lstat_ready, lrstd_ready, ln_ready, krot_done, krope_ready = sem("qkv_ready"), sem("sq6_ready"), sem("lstat_ready"), sem("lrstd_ready"), sem("ln_ready"), sem("krot_done"), sem("krope_ready")
        q_ready, qrot_done, qrope_ready, k_ready, v_ready = sem("q_ready"), sem("qrot_done"), sem("qrope_ready"), sem("k_ready"), sem("v_ready")
        s_done, max_ready, p_exp, pn_ready, t_done, pT_ready, pv_done, o_hi, o_ready = (sem(n) for n in ("s_done", "max_ready", "p_exp", "pn_ready", "t_done", "pT_ready", "pv_done", "o_hi", "o_ready"))
        u_s_done, u_max, u_exp, u_alone, u_pn, u_t_done, u_pT, u_pv, u_out, u_fhi, u_flo = (sem(n) for n in ("u_s_done", "u_max", "u_exp", "u_alone", "u_pn", "u_t_done", "u_pT", "u_pv", "u_out", "u_fhi", "u_flo"))
        gv_scaled, t0_ready, t1_ready, taps_ready, ge_ready, f_mul, f_hi, f_ready = (sem(n) for n in ("gv_scaled", "t0_ready", "t1_ready", "taps_ready", "ge_ready", "f_mul", "f_hi", "f_ready"))
        sig_ready = sem("sig_ready")
        qk_hi, q_twice, qk_ready, ve_ready, fb_done, fz_ready, fl_ready = (sem(n) for n in ("qk_hi", "q_twice", "qk_ready", "ve_ready", "fb_done", "fz_ready", "fl_ready"))
        sel_ready, cum_ready, cum_hi, cum_lo = (sem(n) for n in ("sel_ready", "cum_ready", "cum_hi", "cum_lo"))
        lam_sum, lam_exp, lam_one, lam_done, lam_ready = (sem(n) for n in ("lam_sum", "lam_exp", "lam_one", "lam_done", "lam_ready"))
        oasq_ready, oastat, oarstd, oan, oa_hi, oa_lo, gain_ready, u_inv = (sem(n) for n in ("oasq_ready", "oastat", "oarstd", "oan", "oa_hi", "oa_lo", "gain_ready", "u_inv"))
        relu_ready = sem("relu_ready")
        rsum_ready = sem("rsum_ready")
        vt_ready, vt_done = sem("vt_ready"), sem("vt_done")
        rqk_ready, rv_ready, rs_done, rs_ready, ro_done, ro_ready, rsq_ready, rstat, r_rstd_ready, ron_ready = (sem(n) for n in ("rqk_ready", "rv_ready", "rs_done", "rs_ready", "ro_done", "ro_ready", "rsq_ready", "rstat", "r_rstd_ready", "ron_ready"))
        silu2_ready, y_mul, y_hi, y_ready = (sem(n) for n in ("silu2_ready", "y_mul", "y_hi", "y_ready"))
        ot_done, ot_ready, stored = sem("ot_done"), sem("ot_ready"), sem("stored")

        def c1(name, k):
            return col1[:, R1AT[name] + k:R1AT[name] + k + 1]

        def c2(name, k):
            return col2[:, R2AT[name] + k:R2AT[name] + k + 1]

        def f32(ap):
            return ap.bitcast(F32)


        S_X, S_MIX, S_PRE, S_E, S_FFN, S_LN = 0, 1, 2, 3, 4, 5
        TILES = {S_X: 0, S_MIX: KD, S_PRE: 2 * KD, S_FFN: 3 * KD}
        TILES.update({S_LN + j: (4 + j) * KD for j in range(4)})
        X_A, X_QKV, X_FFN, X_PLE, X_B, X_LN0, X_LN1, X_RET, X_LN2 = 0, 8, 13, 21, 29, 37, 45, 53, 61
        SUMMED = {n: KD - 2 if n in (S_FFN, S_LN + 3) else KD for n in range(S_LN + 4)}
        ACC0 = {n: sum(SUMMED[m] for m in range(n)) for n in SUMMED}
        ALL, LAST = slice(0, N2), slice(META, N2)

        RET_TILES = [(0,), (1, 2), (3,), (4, 5), (6,), (7,), (), ()]

        def size(cols):
            return cols.stop - cols.start

        CONV_SPLIT = 10
        DVE_TAPS = [(m, tap) for tap in range(TAPS) for m in (0, 1) if m == 0 or tap < CONV_SPLIT]
        POOL_TAPS = [(m, tap) for n in range(TAPS) for m, tap in ((2, n), (1, CONV_SPLIT + n)) if tap < TAPS]
        QROT = (4, 5, 6, 4)
        SCORES = (5, 6, 4)
        RSTAT = (2, 3, 2, 4)
        STAT_ORDER = (3, 2, 1, 0)

        block = ctx.enter_context(nc.Block())

        @block.sync
        def _(sp):
            sp.dma_start(ident[:], a["c_ident"]).then_inc(ident_in, 16)
            sp.dma_start(g_rows[:], a["g_mix_pre"].rearrange("a (t c) -> (a t) c", c=P)).then_inc(g_in, 16)
            sp.dma_start(xt[:, 0, :], a["x"][0, 0:P, :]).then_inc(x_in, 16)
            sp.dma_start(xt[:, 1, :], a["x"][0, P:2 * P, :]).then_inc(x_in, 16)

            def load(c, slot, first, second):
                wait(sp, w_lo_ready, 2 * (c - 1))
                for dst, src in (first, second):
                    sp.dma_start(dst, src).then_inc(raw_landed[slot], 16)

            def view(slot, kt, n):
                return raw[:, slot, 0:kt * n].rearrange("p (k n) -> p k n", k=kt)

            def rows(w, kt):
                return w.rearrange("(k p) n -> p k n", k=kt)

            def columns(c, slot, w, kt, col, n=256):
                half = (kt + 1) // 2
                d, s = view(slot, kt, n), rows(w, kt)[:, :, at(col, n)]
                load(c, slot, (d[:, 0:half], s[:, 0:half]), (d[:, half:kt], s[:, half:kt]))

            def loop(name, count, w, kt):
                c = C0[name]

                def turn(i):
                    for u in range(2):
                        columns(c + 2 * i + u, (c + u) % 2, w, kt, 256 * (2 * i + u))

                repeat(sp, count // 2, turn)

            def deep(name, w, depth):
                c = C0[name]
                kts = [min(8, depth - 8 * j) for j in range((depth + 7) // 8)]
                n = len(kts)

                def turn(i):
                    for u in range(2):
                        for j, kt in enumerate(kts):
                            k = n * u + j
                            columns(c + 2 * n * i + k, (c + k) % 2, w[8 * j * P:(8 * j + kt) * P, :], kt, 256 * (2 * i + u))

                repeat(sp, 2, turn)

            w_in = a["w_in"][0]
            o3 = QLORA + KVLORA + ROPE
            for j in range(3):
                c = C0["qkv_in"] + j
                columns(c, c % 2, w_in, KD, 256 * j, 256 if j < 2 else o3 - 512)
                if j == 1:
                    for rows_of, to, starts_at, landed in ((ROWS2, rows2, R2AT, small_in), (ROWS1, rows1, R1AT, rows1_in)):
                        for name, n in rows_of:
                            src = a[name]
                            src = src.rearrange({2: "a (t c) -> (a t) c", 3: "a b (t c) -> (a b t) c"}[len(src.shape)], c=P)
                            sp.dma_start(to[starts_at[name]:starts_at[name] + n, :], src).then_inc(landed, 16)
                    sp.dma_start(cw_rows[:], a["conv_w"][0]).then_inc(small_in, 16)
                    sp.dma_start(meta_rows[:], a["meta_tokens_2"]).then_inc(small_in, 16)
                    sp.dma_start(lam_rows[:], a["diff_lambda_2"].rearrange("a b c -> a (b c)")).then_inc(small_in, 16)
                    sp.dma_start(pt[:, :, :], a["p"][0, 0].rearrange("(t p) n -> p t n", p=P)).then_inc(pos_in, 16)
                    sp.dma_start(pos_i[NOPE:QHEAD, :], a["positions"].broadcast_to([ROPE, N1])).then_inc(pos_in, 16)
                    sp.dma_start(freq[NOPE:QHEAD, :], a["c_freq"]).then_inc(pos_in, 16)
            for m in range(CT):
                c = C0["conv_in"] + m
                d, s = view(c % 2, KD, 256), rows(w_in, KD)
                load(c, c % 2, (d[:, :, 0:P], s[:, :, o3 + P * m:o3 + P * m + P]),
                     (d[:, :, P:2 * P], s[:, :, o3 + CONV_C + P * m:o3 + CONV_C + P * m + P]))
            for j in range(2):
                c = C0["q"] + j
                columns(c, c % 2, a["w_q_b"][0], 3, 4 * QHEAD * j, 4 * QHEAD)
            columns(C0["kv"], C0["kv"] % 2, a["w_kv_b"][0], 2, 0, D)
            loop("mix_out", 4, a["w_o"][0], KD)
            columns(C0["ple"], C0["ple"] % 2, a["w_ple_proj"][0], 2, 0, D)

            def gate_up(i):
                for u in range(2):
                    c = C0["gate_up"] + u
                    d, col = view(c % 2, KD, 256), at(P * (2 * i + u), P)
                    load(c + 2 * i, c % 2, (d[:, :, 0:P], rows(a["w_ffn_gate"][0], KD)[:, :, col]),
                         (d[:, :, P:2 * P], rows(a["w_ffn_up"][0], KD)[:, :, col]))

            repeat(sp, FT // 2, gate_up)
            deep("down", a["w_ffn_down"][0], FT)
            loop("ple_gate", 4, a["w_ple_gate"][0], KD)
            ew = a["even_w_in_2"][0]
            for j, col in enumerate([0, 256, 512, 768, 1024, 1280, 1536, 1792, 2048, 2304, 2560, 2816]):
                c = C0["even_dqk"] + j
                columns(c, c % 2, ew, KD, col)
            loop("even_out", 4, a["even_w_out_2"][0], KD)
            loop("ffn_up0", 16, a["ffn_w1_2"][0], KD)
            deep("ffn_down0", a["ffn_w2_2"][0], FT2)
            rw = a["ret_w_in_2"][0]
            loop("ret_qk", 8, rw[:, 0:2048], KD)
            loop("ret_v", 8, rw[:, 2048:4096], KD)
            loop("ret_g", 8, rw[:, 4096:6144], KD)
            deep("ret_out", a["ret_w_out_2"][0], 16)
            loop("ffn_up1", 16, a["ffn_w1_2"][1], KD)
            deep("ffn_down1", a["ffn_w2_2"][1], FT2)
            for n in range(4):
                half, t = n // 2, n % 2
                cols = slice(512 * half, 512 * half + 512)
                sp.wait_ge(ot_ready, n + 1)
                sp.dma_start(out[0, P * t:P * t + P, cols], otok[:, t, cols]).then_inc(stored, 16)
            sp.wait_ge(stored, 64)

        @block.gpsimd
        def _(pool):
            chain = Count()

            def link(ins):
                ins.then_inc(pool_chain, 1)
                pool.wait_ge(pool_chain, chain.up())

            nc.gpsimd.memset(ones[:], 1.0).then_inc(set_up, 1)
            nc.gpsimd.memset(ones_row[:], 1.0).then_inc(set_up, 1)
            nc.gpsimd.memset(eps[:, 0:1], EPS1).then_inc(set_up, 1)
            nc.gpsimd.memset(eps[:, 1:2], LN_EPS).then_inc(set_up, 1)
            nc.gpsimd.memset(eps[:, 2:3], 1.0).then_inc(set_up, 1)
            nc.gpsimd.memset(conv_in[:, :, 0:TAPS - 1], 0.0).then_inc(set_up, 1)
            def sums(n, values=None, cols=slice(0, N1)):
                for k in range(SUMMED[n]):
                    pool.wait_ge(sq_ready, KD * n + k + 1)
                    if k == 0:
                        wait(pool, stat_ready, n)
                        if values is not None:
                            nc.gpsimd.tensor_copy(acc1[:, cols], values[:, k, cols])
                        nc.gpsimd.tensor_copy(acc2[:, cols], sq[:, k % 2, cols]).then_inc(acc_ready, 1)
                    else:
                        pool.wait_ge(acc_ready, ACC0[n] + k)
                        if values is not None:
                            nc.gpsimd.tensor_tensor(acc1[:, cols], acc1[:, cols], values[:, k, cols], ALU.add)
                        nc.gpsimd.tensor_tensor(acc2[:, cols], acc2[:, cols], sq[:, k % 2, cols], ALU.add).then_inc(acc_ready, 1)

            sums(S_X)
            pool.dma_start(rot[:], a["c_rot"]).then_inc(const_in, 16)
            pool.dma_start(mask1[:], a["c_mask1"]).then_inc(const_in, 16)
            pool.wait_ge(ident_in, 16)
            pool.wait_ge(cols_ready, 3)
            pool.wait_ge(pt_done, 1)
            for tap in range(TAPS):
                nc.gpsimd.tensor_scalar(diag[tap], ident[:, :], cw[:, CT - 1, tap:tap + 1], None, ALU.mult).then_inc(diag_ready, 1)
            for m in range(CT):
                pool.wait_ge(g_sig, m + 1)
                nc.gpsimd.tensor_tensor(conv_in[:, m, TAPS - 1:], ta[:, m % 2, 0:N1], ra[:, m % 2, 0:N1], ALU.mult)\
                    .then_inc(conv_in_ready, 1)
            pool.wait_ge(conv_in_ready, CT)
            heads = [ROPE, HEADS, N1]
            pool.wait_ge(krope_mul, 2)
            nc.gpsimd.tensor_tensor(kt_[NOPE:QHEAD, :, :], rope_t[NOPE:QHEAD, 0, 0:N1].unsqueeze(1).broadcast_to(heads),
                                    rope_t[NOPE:QHEAD, 1, 0:N1].unsqueeze(1).broadcast_to(heads), ALU.add).then_inc(krope_ready, 1)
            pool.wait_ge(krope_ready, 1)
            for n, (m, tap) in enumerate(POOL_TAPS):
                dst = cv[:, m, :] if m == 2 else cv_part[:, :]
                if n < 2:
                    src, w = conv_in[:, m, tap:tap + N1], cw[:, m, tap:tap + 1]
                    ins = nc.gpsimd.tensor_scalar(dst, src, w, c2("conv_b", m), ALU.mult, ALU.add) if m == 2 else \
                        nc.gpsimd.tensor_scalar(dst, src, w, None, ALU.mult)
                    ins.then_inc(conv_step2, 1)
                else:
                    pool.wait_ge(conv_mul, n - 1)
                    pool.wait_ge(conv_step2, POOL_TAPS.index((m, tap - 1)) + 1)
                    nc.gpsimd.tensor_tensor(dst, dst, y[:, n % KD, 0:N1], ALU.add).then_inc(conv_step2, 1)
            pool.dma_start(f_bias[:], a["even_f_bias_2"].rearrange("a b -> b a")).then_inc(gates_in, 16)
            pool.dma_start(wf[:], a["even_w_in_2"][0].rearrange("(k p) n -> p k n", p=P)[:, :, 3072:3080]).then_inc(gates_in, 16)
            sums(S_MIX)
            sums(S_PRE)
            def gated(i):
                for u in range(2):
                    m = 2 * i + u
                    pool.wait_ge(ge_ready, m + 1)
                    wait(pool, f_ready, m - 1)
                    nc.gpsimd.tensor_tensor(fa[:, u, 0:N1], ra[:, 2 + u, 0:N1], ta[:, u, 0:N1], ALU.mult).then_inc(f_mul, 1)
                    if u == 1 or not is_first(i):
                        gated_low(m - 1, 1 - u)

            def gated_low(m, u):
                pool.wait_ge(f_hi, m + 1)
                nc.gpsimd.tensor_tensor(fl[:, at(m), 0:N1], fa[:, u, 0:N1], f32(fh[:, at(m), 0:N1]), ALU.subtract).then_inc(f_ready, 1)

            repeat(pool, FT // 2, gated)
            gated_low(FT - 1, (FT - 1) % 2)
            sums(S_E)
            sums(S_FFN)
            for k in range(KD):
                pool.wait_ge(post_ready, KD + k + 1)
                nc.gpsimd.tensor_tensor(h[:, k, META:], h[:, k, META:], ta[:, k % 2, 0:N1], ALU.add).then_inc(h_ready, 1)
            pool.wait_ge(stat_ready, S_FFN + 1)
            pool.dma_start(alibi[:], a["c_alibi"]).then_inc(table_in, 16)
            pool.dma_start(mask2[:], a["c_mask2"]).then_inc(table_in, 16)
            pool.wait_ge(ident_in, 16)
            for n, r0 in enumerate((0, 64)):
                wait(pool, sel_ready, n)
                nc.gpsimd.tensor_tensor(sel[r0:r0 + 40, :], ident[r0:r0 + 40, r0:r0 + 8], ident[r0:r0 + 40, r0 + 32:r0 + 40], ALU.add).then_inc(sel_ready, 1)
            pool.wait_ge(sel_ready, 2)
            for n0 in range(0, N2, P):
                ins = nc.gpsimd.tensor_scalar(fgs[:, n0:min(n0 + P, N2)], ones[0:104, 0:min(P, N2 - n0)], 0.0, None, ALU.mult)
            ins.then_inc(sel_ready, 1)

            def twice(i):
                for n in range(4):
                    s0 = 8 * i + 2 * n
                    pool.wait_ge(qk_hi, 8 * i + n + 1)
                    if n == 0:
                        if not is_first(i):
                            pool.wait_ge(q_twice, 8 * i)
                        else:
                            pool.wait_ge(sel_ready, 3)
                    else:
                        pool.wait_ge(q_twice, 8 * i + 2 * n)
                    nc.gpsimd.tensor_copy(qs[64:P, at(s0), :], qs[0:64, at(s0), :]).then_inc(q_twice, 1)
                    pool.wait_ge(q_twice, 8 * i + 2 * n + 1)
                    nc.gpsimd.tensor_copy(qs[0:64, at(s0 + 1), :], qs[64:P, at(s0 + 1), :]).then_inc(q_twice, 1)

            repeat(pool, 2, twice)
            pool.wait_ge(q_twice, 16)
            pool.wait_ge(u_out, 12)
            for hd in range(4):
                nc.gpsimd.tensor_tensor(oasq[:, hd, :], oa[:, hd, :], oa[:, hd, :], ALU.mult).then_inc(oasq_ready, 1)

            def forget_low(j):
                for k in (2 * j, 2 * j + 1):
                    pool.wait_ge(u_fhi, k + 1)
                    nc.gpsimd.tensor_tensor(xl[:, 4 + k, :], of[:, k, :], f32(xh[:, 4 + k, :]), ALU.subtract).then_inc(u_flo, 1)

            forget_low(0)
            for hd in range(4):
                pool.wait_ge(oa_hi, hd + 1)
                nc.gpsimd.tensor_tensor(xl[:, hd, :], oa[:, hd, :], f32(xh[:, hd, :]), ALU.subtract).then_inc(oa_lo, 1)
            forget_low(1)

            def hidden(base, cols):
                def low(m, slot):
                    pool.wait_ge(f_hi, base + m + 1)
                    nc.gpsimd.tensor_tensor(fl[:, at(m), cols], fa[:, slot, cols], f32(fh[:, at(m), cols]), ALU.subtract).then_inc(f_ready, 1)

                def turn(i):
                    for u in range(4):
                        m = 4 * i + u
                        pool.wait_ge(relu_ready, base - FT + m + 1)
                        pool.wait_ge(f_ready, base + m - 3)
                        nc.gpsimd.tensor_tensor(fa[:, u, cols], ra[:, u, cols], ra[:, u, cols], ALU.mult).then_inc(f_mul, 1)
                        if u % 2 == 1 and not (is_first(i) and u == 1):
                            for back in (3, 2):
                                low(m - back, (u - back) % 4)

                repeat(pool, FT2 // 4, turn)
                for m in (FT2 - 2, FT2 - 1):
                    low(m, m % 4)

            sums(S_LN, y, ALL)
            hidden(FT, ALL)
            sums(S_LN + 1, y, ALL)
            pool.wait_ge(stat_ready, S_LN + 2)
            pool.dma_start(decay[:], a["c_decay"]).then_inc(decay_in, 16)

            for hd in range(RH):
                for q in range(1, 4):
                    n = 4 * hd + q
                    pool.wait_ge(rsq_ready, n + 1)
                    wait(pool, rsum_ready, 3 * hd + q - 1)
                    nc.gpsimd.tensor_tensor(rsum[hd % 2][:, LAST], rsum[hd % 2][:, LAST], rsq[:, n % 2, LAST], ALU.add).then_inc(rsum_ready, 1)
            pool.wait_ge(rstat, RH)

            def y_low(i):
                for u in range(4):
                    m = 4 * i + u
                    pool.wait_ge(y_hi, m + 1)
                    nc.gpsimd.tensor_tensor(gl[:, at(m), LAST], fa[:, u, LAST], f32(gh[:, at(m), LAST]), ALU.subtract).then_inc(y_ready, 1)

            repeat(pool, 4, y_low)
            sums(S_LN + 2, y, LAST)
            hidden(FT + FT2, LAST)
            sums(S_LN + 3, y, LAST)

        @block.scalar
        def _(act):
            chain = Count()

            def link(ins):
                ins.then_inc(act_chain, 1)
                act.wait_ge(act_chain, chain.up())

            A = nc.scalar.activation
            def split_hi(slot, use, used, halves=(0, 1)):
                act.wait_ge(raw_landed[slot], 32 * (use + 1))
                wait(act, mm_done, used)
                for s in halves:
                    A(whi[:, slot, s * 1024:s * 1024 + 1024], raw[:, slot, s * 1024:s * 1024 + 1024], ACT.Copy).then_inc(w_hi_ready, 1)

            def split_at(c, halves=(0, 1)):
                if c < CHUNKS:
                    split_hi(c % 2, c // 2, CHUNK_END[c - 2] if c >= 2 else 0, halves)

            def split_in(name, i, per, k):
                c = C0[name] + 2 + k
                split_hi(c % 2, c // 2 + per // 2 * i, CHUNK_END[c - 2] + per * i)

            def squares(n, k, src, cols=slice(0, N1)):
                act.wait_ge(*((e_copied, k // 2 + 1) if n == S_E and k < 4 else (e_late, k // 2 - 1) if n == S_E else (tile_ready, TILES[n] + k + 1)))
                wait(act, acc_ready, ACC0[n] + k - 1)
                A(sq[:, k % 2, cols], src, ACT.Square).then_inc(sq_ready, 1)

            def rms(n, width=N1):
                act.wait_ge(stat_ready, n + 1)
                link(A(lnv[:, 0:width], ps[4][:, 0:width], ACT.Ln, bias=eps[:, 0:1], scale=1.0 / D))
                A(rstd[:, n % 3, 0:width], lnv[:, 0:width], ACT.Exp, scale=-0.5).then_inc(rstd_ready, 1)

            def layer_stats(n, j, cols, between=None):
                w = size(cols)
                act.wait_ge(stat_ready, n + 1)
                link(A(mu[:, cols], ps[5][:, 0:w], ACT.Copy, scale=-1.0 / D))
                A(musq[:, cols], mu[:, cols], ACT.Square).then_inc(mu_ready, 1)
                if between is not None:
                    between()
                act.wait_ge(var_ready, j + 1)
                link(A(lnv[:, cols], var[:, cols], ACT.Ln, bias=eps[:, 1:2]))
                A(rstd[:, n % 3, cols], lnv[:, cols], ACT.Exp, scale=-0.5).then_inc(rstd_ready, 1)

            def layer_apply(j, k, cols, dst=None):
                g, b = (col1[:, at(R1AT[name] + KD * j + k)] for name in ("ln_g_2", "ln_b_2"))
                act.wait_ge(norm_ready, KD * j + k + 1)
                A(h[:, at(k), cols], y[:, at(k), cols], ACT.Identity, bias=b, scale=g).then_inc(hn_ready, 1)
                if dst is not None:
                    A(dst[:, at(k), cols], y[:, at(k), cols], ACT.Identity, bias=b, scale=g).then_inc(xh_ready, 1)

            def raw_columns(j):
                for n, name in enumerate(("ln_g_2", "ln_b_2")):
                    r0 = R1AT[name] + KD * j
                    ins = A(xrh[:, :, N2 + n], col1[:, r0:r0 + KD], ACT.Copy)
                ins.then_inc(gb_hi, 1)

            nc.scalar.preload_act_table_set("natural_log_exp_and_others")
            act.wait_ge(set_up, 6)
            act.wait_ge(cols_ready, 1)
            for k in range(KD):
                act.wait_ge(tile_ready, k + 1)
                A(xh[:, k, 0:N1], h[:, k, META:], ACT.Copy, scale=g_col[:, k:k + 1]).then_inc(xh_ready, 1)
                if k in (3, 5):
                    split_at(0, (k // 2 - 1,))
                if k >= 1:
                    squares(S_X, k - 1, h[:, k - 1, META:])
            split_at(1)
            squares(S_X, KD - 1, h[:, KD - 1, META:])
            act.wait_ge(pt_done, 1)
            A(ph[:, :, :], ps[6][:, :].rearrange("p (k n) -> p k n", k=2), ACT.Copy).then_inc(p_hi, 1)
            rms(S_X)
            act.wait_ge(lam_sum, 2)
            A(lam_s[:, 2:4], lam_s[:, 0:2], ACT.Exp).then_inc(lam_exp, 1)
            for j in range(3):
                for m in range(2):
                    t = 2 * j + m
                    if t < 5:
                        act.wait_ge(qkv_ready, t + 1)
                        A(sq6[:, t, :], qkv[:, t, :], ACT.Square).then_inc(sq6_ready, 1)
                split_at(C0["qkv_in"] + j + 2)
            split_at(C0["conv_in"] + 2)
            for j, width in enumerate((QLORA, KVLORA)):
                act.wait_ge(lstat_ready, j + 1)
                wait(act, lrstd_ready, j)
                link(A(lnv[:, 0:N1], ps[6 + j][:, 0:N1], ACT.Ln, bias=eps[:, 0:1], scale=1.0 / width))
                A(lr[:, j, :], lnv[:, 0:N1], ACT.Exp, scale=-0.5).then_inc(lrstd_ready, 1)
            nc.scalar.preload_act_table(ACT.Sin)
            act.wait_ge(ang_ready, 2)
            for j in range(2):
                A(ang[NOPE:QHEAD, 4 + j, :], ang[NOPE:QHEAD, 2 + j, :], ACT.Sin).then_inc(trig_ready, 1)
            nc.scalar.preload_act_table(ACT.Sigmoid)
            for t in range(5):
                act.wait_ge(ln_ready, t + 1)
                A(qxh[:, t, :], qkv[:, t, :], ACT.Copy).then_inc(xh_ready, 1)
            split_at(C0["conv_in"] + 3)
            def conv_products(first, last):
                for n in range(max(2, first), min(len(POOL_TAPS), last)):
                    m, tap = POOL_TAPS[n]
                    if n < 4:
                        act.wait_ge(conv_in_ready, m + 1)
                    wait(act, conv_step2, n - 7)
                    A(y[:, n % KD, 0:N1], conv_in[:, m, tap:tap + N1], ACT.Copy, scale=cw[:, m, tap:tap + 1]).then_inc(conv_mul, 1)

            for m in range(CT):
                if m >= 2:
                    split_at(C0["conv_in"] + m + 2)
                act.wait_ge(g_scaled, m + 1)
                wait(act, conv_in_ready, m - 1)
                A(ra[:, m % 2, 0:N1], tb[:, m % 2, 0:N1], ACT.Sigmoid).then_inc(g_sig, 1)
            for j in range(4):
                act.wait_ge(mm_done, E0["q"] + j + 1)
                for m in range(2):
                    ins = A(qt[0:QHEAD, 2 * j + m, :], ps[2 * ((P0["q"] + j) % 2) + m][0:QHEAD, 0:N1], ACT.Copy)
                ins.then_inc(q_ready, 1)
                if j == 1:
                    split_at(C0["q"] + 2)
                conv_products(3 * j, 3 * j + 3)
            for j in range(4):
                act.wait_ge(mm_done, E0["kv"] + j + 1)
                for m in range(2):
                    ins = A(kt_[0:NOPE, 2 * j + m, :], ps[2 * ((P0["kv"] + j) % 2) + m][0:NOPE, 0:N1], ACT.Copy)
                ins.then_inc(k_ready, 1)
                conv_products(12 + 3 * j, 15 + 3 * j)
                if j == 1:
                    split_at(C0["q"] + 3)
            nc.scalar.preload_act_table_set("natural_log_exp_and_others")
            act.wait_ge(mm_done, E0["kv"] + 5)
            for t in range(2):
                A(v1[:, t, :], ps[2 * ((P0["kv"] + 4) % 2) + t][:, :], ACT.Copy).then_inc(v_ready, 1)
            def conv_square(m):
                if m == 2:
                    act.wait_ge(conv_step2, POOL_TAPS.index((2, TAPS - 1)) + 1)
                elif m == 3:
                    act.wait_ge(conv_pe, 2)
                else:
                    act.wait_ge(conv_step, len(DVE_TAPS) + m)
                A(sq6[:, m, :], cv[:, m, :], ACT.Square).then_inc(csq_ready, 1)
            for i in range(16 + 4):
                if 3 <= i < 19:
                    u = i - 3
                    n = u // 8 + 1
                    act.wait_ge(t_done, u + 1)
                    wait(act, pv_done, u - 1)
                    A(pt1[:, u % 2, 0:n, :], ps[u % 2][:, 0:n * P].rearrange("p (k n) -> p k n", k=n), ACT.Copy).then_inc(pT_ready, 1)
                if i < 16:
                    w = P * (i // 8 + 1)
                    act.wait_ge(max_ready, i + 1)
                    wait(act, t_done, i - 3)
                    A(p1[:, i % 4, 0:w], s1[:, i % 2, 0:w], ACT.Exp, bias=small[:, i, 1:2], scale=-1.0,
                      accum_out=small[:, i, 2:3]).then_inc(p_exp, 1)
                if i >= 5 and i % 2 == 1:
                    g = (i - 5) // 2
                    act.wait_ge(pv_done, 2 * g + 2)
                    A(xh[:, g % 4, P * (g // 4):P * (g // 4) + P], ps[2 + g % 2][:, 0:P], ACT.Copy).then_inc(o_hi, 1)
                conv_products(24 + 4 * i // 2, 24 + 4 * (i + 1) // 2)
                if i in (7, 9):
                    split_at(C0["kv"] + 2, (i // 2 - 3,))
                if i >= 18:
                    conv_square(STAT_ORDER[i - 18])
            for m in STAT_ORDER[2:]:
                conv_square(m)
            act.wait_ge(cstat_ready, 1)
            link(A(mu[:, 0:N1], ps[4][:, 0:N1], ACT.Copy, scale=1.0 / CONV_C))
            A(musq[:, 0:N1], mu[:, 0:N1], ACT.Square).then_inc(cmu_ready, 1)
            act.wait_ge(cvar_ready, 1)
            link(A(lnv[:, 0:N1], var[:, 0:N1], ACT.Ln, bias=eps[:, 0:1]))
            A(musq[:, 0:N1], lnv[:, 0:N1], ACT.Exp, scale=-0.5).then_inc(crstd_ready, 1)
            nc.scalar.preload_act_table(ACT.Silu)
            for m in range(CT + 1):
                if m < CT:
                    act.wait_ge(cn_ready, m + 1)
                    A(sq6[:, m, :], cv[:, m, :], ACT.Silu, bias=c2("conv_ln_b", m), scale=c2("conv_ln_g", m)).then_inc(silu_ready, 1)
                if m >= 1:
                    act.wait_ge(silu_ready, m)
                    A(xh[:, 3 + m, 0:N1], sq6[:, m - 1, :], ACT.Copy).then_inc(c_hi, 1)
            nc.scalar.preload_act_table_set("natural_log_exp_and_others")
            for j in range(4):
                for m in range(2):
                    squares(S_MIX, 2 * j + m, y[:, 2 * j + m, 0:N1])
                split_at(C0["mix_out"] + j + 2)
            rms(S_MIX)
            for j in (2, 3):
                act.wait_ge(mm_done, E0["ple"] + j + 1)
                for m in range(2):
                    ins = A(e[:, 2 * j + m, :], ps[2 * ((P0["ple"] + j) % 2) + m][:, 0:N1], ACT.Copy)
                ins.then_inc(e_late, 1)
            for k in range(KD):
                act.wait_ge(tile_ready, TILES[S_PRE] + k + 1)
                A(xh[:, k, 0:N1], h[:, k, META:], ACT.Copy, scale=c1("g_ffn_pre", k)).then_inc(xh_ready, 1)
                squares(S_PRE, k, h[:, k, META:])
            split_at(C0["ple"] + 2)
            rms(S_PRE)
            nc.scalar.preload_act_table(ACT.Gelu_apprx_tanh)

            def gelu_at(m, u):
                act.wait_ge(taps_ready, m + 1)
                A(ra[:, 2 + u, 0:N1], tb[:, u, 0:N1], ACT.Gelu_apprx_tanh, bias=col2[:, at(3 * FT + m)]).then_inc(ge_ready, 1)

            def gated_high(m, u):
                act.wait_ge(f_mul, m + 1)
                A(fh[:, at(m), 0:N1], fa[:, u, 0:N1], ACT.Copy).then_inc(f_hi, 1)

            def gelu(i):
                for u in range(2):
                    m = 2 * i + u
                    split_in("gate_up", i, 2, u)
                    act.wait_ge(gv_scaled, m + 1)
                    A(ra[:, u, 0:N1], gt[:, u, 0:N1], ACT.Copy, scale=col2[:, at(m)]).then_inc(t0_ready, 1)
                    later = not is_first(i)
                    if later or u == 1:
                        gelu_at(m - 1, 1 - u)
                    if later:
                        gated_high(m - 2, u)

            repeat(act, FT // 2, gelu)
            gelu_at(FT - 1, (FT - 1) % 2)
            for m in (FT - 2, FT - 1):
                gated_high(m, m % 2)
            nc.scalar.preload_act_table_set("natural_log_exp_and_others")
            for j in range(4):
                split_at(C0["down"] + 3 * j + 2)
                if j == 0:
                    for k in range(3):
                        squares(S_E, k, e[:, k, :])
                split_at(C0["down"] + 3 * j + 3)
                if j == 0:
                    for k in range(3, KD):
                        squares(S_E, k, e[:, k, :])
                if j == 2:
                    rms(S_E)
                for m in range(2):
                    squares(S_FFN, 2 * j + m, y[:, 2 * j + m, 0:N1])
                if j < 3:
                    split_at(C0["down"] + 3 * j + 4)
            rms(S_FFN)
            for k in range(KD):
                act.wait_ge(h_ready, k + 1)
                A(xh[:, k, 0:N1], h[:, k, META:], ACT.Copy).then_inc(xh_ready, 1)
                if k in (3, 5):
                    split_at(C0["ple_gate"] + 1, (k // 2 - 1,))
            nc.scalar.preload_act_table(ACT.Sigmoid)
            for j in range(4):
                p = P0["ple_gate"] + j
                act.wait_ge(mm_done, E0["ple_gate"] + j + 1)
                for m in range(2):
                    k = 2 * j + m
                    wait(act, h_ready, KD + k - 3 if k >= 4 else 0)
                    ins = A(ra[:, k % 4, 0:N1], ps[2 * (p % 2) + m][:, 0:N1], ACT.Sigmoid)
                    ins.then_inc(sig_ready, 1)
                split_at(C0["ple_gate"] + j + 2, (0, 1) if j < 3 else (0,))
                for m in range(2):
                    k = 2 * j + m
                    act.wait_ge(h_ready, KD + k + 1)
                    A(xrh[:, k, 0:N2], h[:, k, :], ACT.Copy).then_inc(xh_ready, 1)
            split_at(C0["ple_gate"] + 5, (1,))
            def qk_high(c, turn, chunk):
                act.wait_ge(mm_done, CHUNK_END[chunk])
                for m in range(2):
                    s0 = 8 * turn + 2 * (2 * (c % 2) + m)
                    for half in range(2):
                        r = slice(64 * half, 64 * half + 64)
                        ins = A((qs if c % 4 < 2 else ks)[r, s0 + half, :], ps[2 * (c % 2) + m][r, 0:N2], ACT.Copy)
                    ins.then_inc(qk_hi, 1)

            for c in range(4):
                qk_high(c, 0, C0["even_dqk"] + c)
                split_at(C0["even_dqk"] + c + 2)
            nc.scalar.preload_act_table_set("natural_log_exp_and_others")
            act.wait_ge(fz_ready, 1)
            link(A(fg[:, 1, :], fg[:, 0, :], ACT.Abs))
            link(A(fg[:, 2, :], fg[:, 1, :], ACT.Exp, scale=-1.0))
            A(fg[:, 3, :], fg[:, 2, :], ACT.Ln, bias=eps[0:8, 2:3]).then_inc(fl_ready, 1)
            act.wait_ge(cum_ready, 1)
            act.wait_ge(sel_ready, 3)
            for r0 in (0, 64):
                A(fgs[r0:r0 + 8, :], fg[:, 0, :], ACT.Copy).then_inc(cum_hi, 1)

            def even_unit(i):
                diff_norm(i - NORM)
                if i < len(UNITS):
                    t, diff, hd, m = UNITS[i]
                    n, w = TOK[t][1], SEEN[t]
                    act.wait_ge(u_max, i + 1)
                    if i >= P2:
                        if i - P2 in ORDER:
                            act.wait_ge(u_t_done, ORDER[i - P2] + 1)
                        else:
                            act.wait_ge(u_pn, ORDER[i - P2 + 1] + 1)
                    A(p2[0:n, i % P2, 0:w], s2[0:n, i % 2, 0:w], ACT.Exp, bias=small[0:n, i, 1:2], scale=-1.0,
                      accum_out=small[0:n, i, 2:3]).then_inc(u_exp, 1)
                if i >= T_LAG and i - T_LAG in ORDER:
                    t, diff, hd, m = UNITS[i - T_LAG]
                    o = ORDER[i - T_LAG]
                    nq = TOK[t][1]
                    act.wait_ge(u_t_done, o + 1)
                    wait(act, u_pv, o + 1 - PT2)
                    for b in range(t + 1):
                        kn = TOK[b][1]
                        ins = A(pt2[o % PT2][0:kn, b, 0:nq], ps[6 + o % 2][0:kn, P * b:P * b + nq], ACT.Copy)
                    ins.then_inc(u_pT, 1)
                if i >= V_LAG and i - V_LAG in ORDER:
                    t, diff, hd, m = UNITS[i - V_LAG]
                    o = ORDER[i - V_LAG]
                    q0, nq = TOK[t]
                    r = slice(0, P) if diff else slice(64 * (hd % 2), 64 * (hd % 2) + 64)
                    bank, c0 = out_bank(o)
                    act.wait_ge(u_pv, o + 1)
                    A((oa if diff else of)[r, hd if diff else hd // 2, q0:q0 + nq], ps[bank][r, c0:c0 + nq], ACT.Copy).then_inc(u_out, 1)
                if i == FORGET:
                    forget_high(0)

            def forget_high(j):
                act.wait_ge(u_out, 24 + 12 * j)
                for k in (2 * j, 2 * j + 1):
                    A(xh[:, 4 + k, :], of[:, k, :], ACT.Copy).then_inc(u_fhi, 1)

            def diff_norm(n):
                if 0 <= n - 2 < 4:
                    hd = n - 2
                    act.wait_ge(oastat, hd + 1)
                    wait(act, oarstd, hd)
                    link(A(lnv[:, :], ps[1][:, 0:N2], ACT.Ln, bias=eps[:, 0:1], scale=1.0 / P))
                    A(oasq[:, hd, :], lnv[:, :], ACT.Exp, scale=-0.5).then_inc(oarstd, 1)
                if 0 <= n - 4 < 4:
                    hd = n - 4
                    act.wait_ge(oan, hd + 1)
                    A(xh[:, hd, :], oa[:, hd, :], ACT.Copy).then_inc(oa_hi, 1)

            for c in range(8):
                for k, i in enumerate(WITH[c]):
                    even_unit(i)
                    if c >= 1 and k == EVAC_AT and 2 <= c - 1 < 6:
                        qk_high(c + 1, 1, C0["even_v0"] + c - 1)
                    for half in range(2):
                        if c >= 1 and k == HI_AT[half]:
                            split_at(C0["even_v0"] + c + 1, (half,))
            for i in range(ALONE, len(UNITS) + V_LAG):
                even_unit(i)
            forget_high(1)
            split_at(C0["even_out"] + 1)

            def residual(n, name, per, j, cols):
                for i in range(4):
                    for q in range(per - 1):
                        split_at(C0[name] + per * i + q + 2)
                    if i == 0 and j < 3:
                        raw_columns(j)
                    if j < 3:
                        for k in (2 * i, 2 * i + 1):
                            act.wait_ge(tile_ready, TILES[n] + k + 1)
                            A(xrh[:, k, cols], y[:, k, cols], ACT.Copy, scale=c1("ln_g_2", KD * j + k)).then_inc(xh_ready, 1)
                    for k in (2 * i, 2 * i + 1):
                        squares(n, k, y[:, k, cols], cols)
                    split_at(C0[name] + per * i + per - 1 + 2)

            def ffn_up(name, base, j, cols):
                def turn(i):
                    for u in range(2):
                        if u == 0 and is_first(i):
                            layer_stats(S_LN + j, j, cols, lambda: split_at(C0[name] + 2, (0,)))
                            split_at(C0[name] + 2, (1,))
                        else:
                            split_in(name, i, 2, u)
                        for m in range(2):
                            t = 4 * i + 2 * u + m
                            act.wait_ge(raw_ready, base - FT + (16 if j else 0) + t + 1)
                            A(ra[:, 2 * u + m, cols], rw[:, 2 * u + m, cols], ACT.Relu, bias=b_col[:, 2 * u + m:2 * u + m + 1]).then_inc(relu_ready, 1)
                        if not (is_first(i) and u == 0):
                            for m in range(2):
                                high(4 * i + 2 * u + m - 2, 2 - 2 * u + m)
                    layer_apply(j, i, cols)

                def high(t, slot):
                    act.wait_ge(f_mul, base + t + 1)
                    A(fh[:, at(t), cols], fa[:, slot, cols], ACT.Copy).then_inc(f_hi, 1)

                repeat(act, 8, turn)
                for t in (FT2 - 2, FT2 - 1):
                    high(t, t % 4)

            residual(S_LN, "even_out", 1, 0, ALL)
            ffn_up("ffn_up0", FT, 0, ALL)
            residual(S_LN + 1, "ffn_down0", 4, 1, ALL)
            for c in range(8):
                if c == 0:
                    layer_stats(S_LN + 1, 1, ALL, lambda: split_at(C0["ret_qk"] + 2, (0,)))
                split_at(C0["ret_qk"] + c + 2, (0, 1) if c else (1,))
                cols = LAST if c < 4 else ALL
                for m in range(2):
                    slot = 2 * (c % 2) + m
                    act.wait_ge(raw_ready, FT2 + 2 * c + m + 1)
                    A(rqk[:, c % 4, 2 * (c // 4) + m, cols], rw[:, slot, cols], ACT.Identity, bias=b_col[:, slot:slot + 1]).then_inc(rqk_ready, 1)
                for k in RET_TILES[c]:
                    layer_apply(1, k, ALL, xh)

            def ret_chunks(i):
                for u in range(2):
                    act.wait_ge(mm_done, E0["ret_v"] + 2 * i + u + 1)
                    if not is_first(i):
                        act.wait_ge(vt_done, 2 * i + u - 1)
                    for m in range(2):
                        A(fa[:, 2 * u + m, :], ps[2 * ((P0["ret_v"] + u) % 2) + m][:, 0:N2], ACT.Copy).then_inc(vt_ready, 1)
                    split_in("ret_v", i, 2, u)

            repeat(act, 4, ret_chunks)
            def ret_rms(hd):
                act.wait_ge(rstat, hd + 1)
                wait(act, ron_ready, hd)
                link(A(lnv[:, LAST], ps[RSTAT[hd]][:, 0:N1], ACT.Ln, bias=eps[:, 0:1], scale=1.0 / RV))
                A(r_rstd[:, LAST], lnv[:, LAST], ACT.Exp, scale=-0.5).then_inc(r_rstd_ready, 1)

            for n in range(4 * RH):
                act.wait_ge(ro_ready, n + 1)
                hd, q = n // 4, n % 4
                if q == 0:
                    wait(act, rstat, hd - 1)
                else:
                    before = n - 2
                    wait(act, rsum_ready, 3 * (before // 4) + before % 4)
                A(rsum[hd % 2][:, LAST] if q == 0 else rsq[:, n % 2, LAST], rqk[:, hd, q, LAST], ACT.Square).then_inc(rsq_ready, 1)
                if n % 4 == 2 and n >= 4:
                    ret_rms(n // 4 - 1)
            ret_rms(RH - 1)
            nc.scalar.preload_act_table(ACT.Silu)

            def ret_gate(i):
                for u in range(2):
                    act.wait_ge(mm_done, E0["ret_g"] + 2 * i + u + 1)
                    for m in range(2):
                        A(ra[:, 2 * u + m, LAST], ps[2 * ((P0["ret_g"] + u) % 2) + m][:, 0:N1], ACT.Silu).then_inc(silu2_ready, 1)
                    split_in("ret_g", i, 2, u)
                    for m in range(2):
                        t = 4 * i + 2 * u + m
                        act.wait_ge(y_mul, t + 1)
                        A(gh[:, at(t), LAST], fa[:, 2 * u + m, LAST], ACT.Copy).then_inc(y_hi, 1)

            repeat(act, 4, ret_gate)
            nc.scalar.preload_act_table_set("natural_log_exp_and_others")
            residual(S_LN + 2, "ret_out", 2, 2, LAST)
            ffn_up("ffn_up1", FT + FT2, 2, LAST)
            residual(S_LN + 3, "ffn_down1", 4, 3, LAST)
            layer_stats(S_LN + 3, 3, LAST)
            for k in range(KD):
                layer_apply(3, k, LAST)

        @block.vector
        def _(dve):
            V = nc.vector
            chain = Count()

            def link(ins):
                ins.then_inc(dve_chain, 1)
                dve.wait_ge(dve_chain, chain.up())

            def split_lo(c, slot, halves=(0, 1)):
                for s in halves:
                    dve.wait_ge(w_hi_ready, 2 * c + s + 1)
                    V.tensor_tensor(wlo[:, slot, s * 1024:s * 1024 + 1024], raw[:, slot, s * 1024:s * 1024 + 1024],
                                    f32(whi[:, slot, s * 1024:s * 1024 + 1024]), ALU.subtract).then_inc(w_lo_ready, 1)

            def split_at(c, halves=(0, 1)):
                if c < CHUNKS:
                    split_lo(c, c % 2, halves)

            def split_in(name, i, per, k):
                c = C0[name] + 2 + k
                split_lo(c + per * i, c % 2)

            def x_low(done, k, src, gain=None, dst=(xh, xl), cols=None):
                hi, lo = (v[:, at(k), cols or slice(0, src.shape[-1])] for v in dst)
                dve.wait_ge(xh_ready, done + k + 1)
                if gain is None:
                    V.tensor_tensor(lo, src, f32(hi), ALU.subtract).then_inc(x_ready, 1)
                else:
                    V.scalar_tensor_tensor(lo, src, gain, f32(hi), ALU.mult, ALU.subtract).then_inc(x_ready, 1)

            dve.wait_ge(cols_t, 1)
            V.tensor_copy(g_col[:, :], ps[0][:, 0:KD]).then_inc(cols_ready, 1)
            for k in range(KD):
                dve.wait_ge(xt_done, k + 1)
                V.tensor_copy(h[:, k, META:], ps[4 + k % 4][:, 0:N1]).then_inc(tile_ready, 1)
                if k >= 1:
                    x_low(X_A, k - 1, h[:, k - 1, META:], g_col[:, k - 1:k])
                if k in (4, 6):
                    split_at(0, (k // 2 - 2,))
            x_low(X_A, KD - 1, h[:, KD - 1, META:], g_col[:, KD - 1:KD])
            split_at(1)
            dve.wait_ge(cols_t, 2)
            V.tensor_copy(col1[:, :], ps[7][:, 2 * P:2 * P + R1N])
            V.tensor_copy(col2[:, :], ps[7][:, 0:R2N]).then_inc(cols_ready, 1)
            V.tensor_copy(cw[:, :, :], ps[7][:, P:P + CT * TAPS].rearrange("p (m n) -> p m n", m=CT)).then_inc(cols_ready, 1)
            for j in range(2):
                V.tensor_tensor_reduce(var[0:1, 64 * j:64 * j + 64], lam_rows[:, 128 * j:128 * j + 64], lam_rows[:, 128 * j + 64:128 * j + 128],
                                       1.0, 0.0, ALU.mult, ALU.add, lam_s[:, j:j + 1]).then_inc(lam_sum, 1)
            dve.wait_ge(meta_done, 1)
            V.tensor_copy(h[:, :, 0:META], ps[5][:, 0:KD * META].rearrange("p (k n) -> p k n", k=KD)).then_inc(meta_ready, 1)
            dve.wait_ge(p_hi, 1)
            V.tensor_tensor(pl[:, :, :], ps[6][:, :].rearrange("p (k n) -> p k n", k=2), f32(ph[:, :, :]), ALU.subtract).then_inc(p_ready, 1)
            R = slice(NOPE, QHEAD)
            cos, sin = ang[R, 4, :], ang[R, 5, :]

            two_pi = 2 * np.pi
            p_1 = 6.28125
            p_2 = float(np.float32(np.floor((two_pi - p_1) * 2 ** 21) / 2 ** 21))
            p_3 = float(np.float32(two_pi - p_1 - p_2))
            magic = 1.5 * 2 ** 23

            def angle():
                dve.wait_ge(pos_in, 48)
                link(V.tensor_copy(ang[R, 0, :], pos_i[R, :]))
                link(V.tensor_scalar(ang[R, 0, :], ang[R, 0, :], freq[R, 0:1], None, ALU.mult))

            def angle_turns(turn):
                link(V.tensor_scalar(ang[R, 1, :], ang[R, 0, :], float(1 / two_pi), turn, ALU.mult, ALU.add))
                link(V.tensor_scalar(ang[R, 1, :], ang[R, 1, :], magic, None, ALU.add))
                link(V.tensor_scalar(ang[R, 1, :], ang[R, 1, :], magic, None, ALU.subtract))

            def angle_rest(j, shift):
                link(V.scalar_tensor_tensor(ang[R, 2 + j, :], ang[R, 1, :], -p_1, ang[R, 0, :], ALU.mult, ALU.add))
                link(V.scalar_tensor_tensor(ang[R, 2 + j, :], ang[R, 1, :], -p_2, ang[R, 2 + j, :], ALU.mult, ALU.add))
                link(V.scalar_tensor_tensor(ang[R, 2 + j, :], ang[R, 1, :], -p_3, ang[R, 2 + j, :], ALU.mult, ALU.add))
                link(V.tensor_scalar(ang[R, 2 + j, :], ang[R, 2 + j, :], float(shift), 3.1415925, ALU.add, ALU.min))
                V.tensor_scalar(ang[R, 2 + j, :], ang[R, 2 + j, :], -3.1415925, None, ALU.max).then_inc(ang_ready, 1)

            def conv_taps(first, last):
                for n, (m, tap) in list(enumerate(DVE_TAPS))[first:last]:
                    if tap == 0:
                        dve.wait_ge(conv_in_ready, m + 1)
                        V.tensor_scalar(cv[:, m, :], conv_in[:, m, 0:N1], cw[:, m, 0:1], c2("conv_b", m), ALU.mult, ALU.add).then_inc(conv_step, 1)
                    else:
                        dve.wait_ge(conv_step, DVE_TAPS.index((m, tap - 1)) + 1)
                        V.scalar_tensor_tensor(cv[:, m, :], conv_in[:, m, tap:tap + N1], cw[:, m, tap:tap + 1], cv[:, m, :],
                                               ALU.mult, ALU.add).then_inc(conv_step, 1)

            r_x = rstd[:, S_X % 3, 0:N1]
            dve.wait_ge(rstd_ready, 1)
            for j in range(3):
                p = P0["qkv_in"] + j
                dve.wait_ge(mm_done, E0["qkv_in"] + j + 1)
                for m in range(2):
                    n = QHEAD if 2 * j + m == 5 else P
                    V.tensor_tensor(qkv[0:n, 2 * j + m, :], ps[2 * (p % 2) + m][0:n, 0:N1], r_x[0:n], ALU.mult).then_inc(qkv_ready, 1)
                if j == 0:
                    angle()
                    angle_turns(0.25)
                elif j == 1:
                    angle_rest(0, np.pi / 2)
                else:
                    angle_turns(0.0)
                split_at(C0["qkv_in"] + j + 2)
            angle_rest(1, 0.0)

            def conv_input(m):
                p = P0["conv_in"] + m
                dve.wait_ge(mm_done, E0["conv_in"] + m + 1)
                wait(dve, conv_in_ready, m - 1)
                V.tensor_tensor(ta[:, m % 2, 0:N1], ps[2 * (p % 2)][:, 0:N1], r_x, ALU.mult)
                V.tensor_tensor(tb[:, m % 2, 0:N1], ps[2 * (p % 2) + 1][:, 0:N1], r_x, ALU.mult).then_inc(g_scaled, 1)
                split_at(C0["conv_in"] + m + 2)

            conv_input(0)
            for t in range(5):
                j = 0 if t < 3 else 1
                dve.wait_ge(lrstd_ready, j + 1)
                V.scalar_tensor_tensor(qkv[:, t, :], qkv[:, t, :], c2("g_q_a", t) if t < 3 else c2("g_kv_a", t - 3), lr[:, j, :],
                                       ALU.mult, ALU.mult).then_inc(ln_ready, 1)
                if t >= 1:
                    x_low(X_QKV, t - 1, qkv[:, t - 1, :], dst=(qxh, qxl))
            x_low(X_QKV, 4, qkv[:, 4, :], dst=(qxh, qxl))
            conv_input(1)
            conv_input(2)
            dve.wait_ge(krot_done, 1)
            dve.wait_ge(trig_ready, 2)
            V.tensor_tensor(rope_t[R, 0, 0:N1], ps[5][R, 0:N1], sin, ALU.mult).then_inc(krope_mul, 1)
            V.tensor_tensor(rope_t[R, 1, 0:N1], qkv[R, 5, :], cos, ALU.mult).then_inc(krope_mul, 1)
            conv_input(3)
            conv_taps(0, 5)
            split_at(C0["q"] + 2)
            conv_taps(5, 14)
            dve.wait_ge(lam_exp, 1)
            link(V.tensor_tensor(lam_s[:, 5:6], lam_s[:, 2:3], lam_s[:, 3:4], ALU.subtract))
            V.tensor_scalar(lam_s[:, 4:5], lam_s[:, 5:6], LAM_INIT, None, ALU.add).then_inc(lam_one, 1)
            pair = [ROPE, 2, N1]

            def query_rope(j):
                dve.wait_ge(qrot_done, j + 1)
                wait(dve, qrope_ready, j)
                t1, t2 = (rope_t[R, n, :].rearrange("p (h n) -> p h n", h=2) for n in range(2))
                V.tensor_tensor(t1, ps[QROT[j]][R, :].rearrange("p (h n) -> p h n", h=2), sin.unsqueeze(1).broadcast_to(pair), ALU.mult)
                link(V.tensor_tensor(t2, qt[R, 2 * j:2 * j + 2, :], cos.unsqueeze(1).broadcast_to(pair), ALU.mult))
                V.tensor_tensor(qt[R, 2 * j:2 * j + 2, :], t1, t2, ALU.add).then_inc(qrope_ready, 1)

            dve.wait_ge(krope_ready, 1)
            for j in range(4):
                query_rope(j)
                if j == 2:
                    split_at(C0["q"] + 3)
                conv_taps(14 + j, 15 + j)
            dve.wait_ge(const_in, 32)
            for i in range(16 + 4):
                if i < 16:
                    w = P * (i // 8 + 1)
                    dve.wait_ge(s_done, i + 1)
                    wait(dve, p_exp, i - 1)
                    V.tensor_tensor_reduce(s1[:, i % 2, 0:w], ps[SCORES[i % 3]][:, 0:w], mask1[:, N1 - w:N1], -SC1, 3.0e38,
                                           ALU.add, ALU.min, small[:, i, 1:2]).then_inc(max_ready, 1)
                if 1 <= i < 17:
                    u = i - 1
                    w = P * (u // 8 + 1)
                    dve.wait_ge(p_exp, u + 1)
                    V.reciprocal(small[:, u, 3:4], small[:, u, 2:3]).then_inc(dve_chain, 1)
                    inverse = chain.up()
                    conv_taps(18 + 2 * i, 19 + 2 * i)
                    dve.wait_ge(dve_chain, inverse)
                    V.tensor_scalar(p1[:, u % 4, 0:w], p1[:, u % 4, 0:w], small[:, u, 3:4], None, ALU.mult).then_inc(pn_ready, 1)
                if i >= 5 and i % 2 == 1:
                    g = (i - 5) // 2
                    dve.wait_ge(o_hi, g + 1)
                    lo, hi = (x[:, g % 4, P * (g // 4):P * (g // 4) + P] for x in (xl, xh))
                    V.tensor_tensor(lo, ps[2 + g % 2][:, 0:P], f32(hi), ALU.subtract).then_inc(o_ready, 1)
                conv_taps((19 if 1 <= i < 17 else 18) + 2 * i, 20 + 2 * i)
                if i in (8, 10):
                    split_at(C0["kv"] + 2, (i // 2 - 4,))
                if i == 16:
                    dve.wait_ge(conv_pe, 1)
                    V.tensor_scalar(cv[:, 3, :], ps[7][:, 0:N1], c2("conv_b", 3), None, ALU.add).then_inc(conv_pe, 1)
            dve.wait_ge(conv_step2, len(POOL_TAPS))
            dve.wait_ge(conv_step, len(DVE_TAPS))
            V.tensor_tensor(cv[:, 1, :], cv[:, 1, :], cv_part[:, :], ALU.add).then_inc(conv_step, 1)
            dve.wait_ge(cstat_ready, 1)
            dve.wait_ge(cmu_ready, 1)
            V.scalar_tensor_tensor(var[:, 0:N1], ps[5][:, 0:N1], 1.0 / CONV_C, musq[:, 0:N1], ALU.mult, ALU.subtract).then_inc(cvar_ready, 1)
            for m in range(CT):
                ins = V.tensor_tensor(cv[:, m, :], cv[:, m, :], mu[:, 0:N1], ALU.subtract)
            link(ins)
            dve.wait_ge(crstd_ready, 1)
            for m in range(CT):
                V.tensor_tensor(cv[:, m, :], cv[:, m, :], musq[:, 0:N1], ALU.mult).then_inc(cn_ready, 1)
            for m in range(CT):
                dve.wait_ge(c_hi, m + 1)
                V.tensor_tensor(xl[:, 4 + m, 0:N1], sq6[:, m, :], f32(xh[:, 4 + m, 0:N1]), ALU.subtract).then_inc(c_ready, 1)

            dve.wait_ge(lam_done, 1)
            V.tensor_scalar(neg_lam[:, :], ps[6][:, 0:1], -1.0, None, ALU.mult).then_inc(lam_ready, 1)

            def post_norm(n, gain, done, signal, posts, add=True):
                base, gain_in, x0 = done
                dve.wait_ge(rstd_ready, n + 1)
                for k in range(KD + 2):
                    if k < KD:
                        if k >= 2:
                            dve.wait_ge(signal, base + k - 1)
                        V.scalar_tensor_tensor(ta[:, k % 2, 0:N1], y[:, k, 0:N1], c1(gain, k), rstd[:, n % 3, 0:N1],
                                               ALU.mult, ALU.mult).then_inc(post_ready, 1)
                    if 1 <= k <= KD and add:
                        dve.wait_ge(post_ready, posts + k)
                        V.tensor_tensor(h[:, k - 1, META:], h[:, k - 1, META:], ta[:, (k - 1) % 2, 0:N1], ALU.add).then_inc(signal, 1)
                    if k >= 2:
                        x_low(x0, k - 2, h[:, k - 2, META:], gain_in and c1(gain_in, k - 2))

            for j in range(4):
                dve.wait_ge(mm_done, E0["mix_out"] + j + 1)
                for m in range(2):
                    V.tensor_copy(y[:, 2 * j + m, 0:N1], ps[2 * ((P0["mix_out"] + j) % 2) + m][:, 0:N1]).then_inc(tile_ready, 1)
                if j < 3:
                    split_at(C0["mix_out"] + j + 2)
            V.memset(gt[:, :, 0:2], 0.0)
            for j in range(2):
                dve.wait_ge(mm_done, E0["ple"] + j + 1)
                b = 2 * ((P0["ple"] + j) % 2)
                for m in range(2):
                    ins = V.tensor_copy(e[:, 2 * j + m, :], ps[b + m][:, 0:N1])
                ins.then_inc(e_copied, 1)
            split_at(C0["mix_out"] + 3 + 2)
            post_norm(S_MIX, "g_mix_post", (TILES[S_PRE], "g_ffn_pre", X_FFN), tile_ready, 0)
            split_at(C0["ple"] + 2)
            r_pre = rstd[:, S_PRE % 3, 0:N1]
            dve.wait_ge(rstd_ready, S_PRE + 1)

            def gate_up(i):
                for u in range(2):
                    m = 2 * i + u
                    b = 2 * ((P0["gate_up"] + u) % 2)
                    dve.wait_ge(mm_done, E0["gate_up"] + m + 1)
                    wait(dve, f_mul, m - 1)
                    V.tensor_tensor(ta[:, u, 0:N1], ps[b + 1][:, 0:N1], r_pre, ALU.mult)
                    V.tensor_tensor(gt[:, u, 2:2 + N1], ps[b][:, 0:N1], r_pre, ALU.mult).then_inc(gv_scaled, 1)
                    split_in("gate_up", i, 2, u)
                    dve.wait_ge(t0_ready, m + 1)
                    V.scalar_tensor_tensor(fa[:, 2 + u, 0:N1], gt[:, u, 1:1 + N1], col2[:, at(FT + m)], ra[:, u, 0:N1],
                                           ALU.mult, ALU.add).then_inc(t1_ready, 1)
                    dve.wait_ge(t1_ready, m + 1)
                    V.scalar_tensor_tensor(tb[:, u, 0:N1], gt[:, u, 2:2 + N1], col2[:, at(2 * FT + m)], fa[:, 2 + u, 0:N1],
                                           ALU.mult, ALU.add).then_inc(taps_ready, 1)

            repeat(dve, FT // 2, gate_up)

            def branch(name, per, put, low=None, aside=None):
                for j in range(4):
                    if aside is not None and j == 3:
                        aside(j)
                    for q in range(per - 1):
                        split_at(C0[name] + per * j + q + 2)
                    if aside is not None and j < 3:
                        aside(j)
                    dve.wait_ge(mm_done, E0[name] + per * (j + 1))
                    for m in range(2):
                        put(2 * j + m, ps[2 * ((P0[name] + j) % 2) + m])
                    if low is not None:
                        for m in range(2):
                            low(2 * j + m)
                    if name != "down" or j < 3:
                        split_at(C0[name] + per * j + per - 1 + 2)

            def plain(k, bank):
                V.tensor_copy(y[:, k, 0:N1], bank[:, 0:N1]).then_inc(tile_ready, 1)

            def finish_e(j):
                if j >= 2:
                    dve.wait_ge(rstd_ready, S_E + 1)
                    for k in range(4 * (j - 2), 4 * (j - 1)):
                        V.scalar_tensor_tensor(e[:, k, :], e[:, k, :], c1("g_ple", k), rstd[:, S_E % 3, 0:N1], ALU.mult, ALU.mult).then_inc(e_ready, 1)

            def residual(n, name, per, j, x0, cols):
                def columns(i):
                    if i > 0:
                        return
                    if j < 3:
                        dve.wait_ge(gb_hi, j + 1)
                        for c, gain in enumerate(("ln_g_2", "ln_b_2")):
                            r0 = R1AT[gain] + KD * j
                            V.tensor_tensor(xrl[:, :, N2 + c], col1[:, r0:r0 + KD], f32(xrh[:, :, N2 + c]), ALU.subtract)
                    if j > 0:
                        dve.wait_ge(hn_ready, KD * j)

                def put(k, bank):
                    V.scalar_tensor_tensor(y[:, k, cols], h[:, k, cols], ALPHA, bank[:, 0:size(cols)], ALU.mult, ALU.add).then_inc(tile_ready, 1)

                def low(k):
                    x_low(x0, k, y[:, k, cols], c1("ln_g_2", KD * j + k), (xrh, xrl), cols)

                branch(name, per, put, low if j < 3 else None, columns)

            branch("down", 3, plain, aside=finish_e)
            post_norm(S_FFN, "g_ffn_post", (0, None, X_PLE), h_ready, KD, add=False)
            split_at(C0["ple_gate"] + 1)
            dve.wait_ge(e_ready, KD)
            for j in range(4):
                for k in (2 * j, 2 * j + 1):
                    dve.wait_ge(sig_ready, k + 1)
                    V.tensor_tensor(ta[:, k % 2, 0:N1], ra[:, k % 4, 0:N1], e[:, k, :], ALU.mult).then_inc(post_ready, 1)
                    dve.wait_ge(post_ready, 2 * KD + k + 1)
                    V.tensor_tensor(h[:, k, META:], h[:, k, META:], ta[:, k % 2, 0:N1], ALU.add).then_inc(h_ready, 1)
                split_at(C0["ple_gate"] + j + 2, (0, 1) if j < 3 else (0,))
                for k in (2 * j, 2 * j + 1):
                    x_low(X_B, k, h[:, k, :], dst=(xrh, xrl))
            split_at(C0["ple_gate"] + 5, (1,))
            def qk_low(c, turn):
                for m in range(2):
                    n = 2 * (c % 2) + m
                    s0 = 8 * turn + 2 * n
                    bank = ps[2 * (c % 2) + m]
                    dve.wait_ge(qk_hi, 8 * turn + 2 * (c % 4) + m + 1)
                    for half in range(2):
                        r, other = (slice(64 * k, 64 * k + 64) for k in (half, 1 - half))
                        if c % 4 < 2:
                            ins = V.tensor_tensor(ql[r, 4 * turn + n, :], bank[r, 0:N2], f32(qs[r, s0 + half, :]), ALU.subtract)
                        else:
                            ins = V.tensor_tensor(ks[other, s0 + half, :], bank[r, 0:N2], f32(ks[r, s0 + half, :]), ALU.subtract)
                    ins.then_inc(qk_ready, 1)

            def value_tiles(dst, b, j, ready):
                for t, (r0, bank, c) in enumerate([(0, b, 0), (0, b, 256), (64, b + 1, 0)]):
                    n = TOK[t][1]
                    V.tensor_copy(dst[0:n, t, at(256 * j, 256)], ps[bank][r0:r0 + n, c:c + 256]).then_inc(ready, 1)

            for c in range(4):
                qk_low(c, 0)
                split_at(C0["even_dqk"] + c + 2)
            dve.wait_ge(fb_done, 1)
            V.tensor_scalar(fg[:, 0, :], ps[7][0:8, 0:N2], f_bias[:, 0:1], None, ALU.add).then_inc(fz_ready, 1)
            dve.wait_ge(fl_ready, 1)
            link(V.scalar_tensor_tensor(fg[:, 1, :], fg[:, 0, :], 0.0, fg[:, 3, :], ALU.min, ALU.subtract))
            link(V.tensor_tensor_scan(fg[:, 2, :], ones_row[:, :], fg[:, 1, :], 0.0, ALU.mult, ALU.add))
            V.tensor_scalar(fg[:, 0, :], fg[:, 2, :], -1.0 / SC2, None, ALU.mult).then_inc(cum_ready, 1)
            dve.wait_ge(cum_hi, 2)
            for r0 in (0, 64):
                V.tensor_tensor(fgs[r0 + 32:r0 + 40, :], fg[:, 0, :], f32(fgs[0:8, :]), ALU.subtract).then_inc(cum_lo, 1)
            dve.wait_ge(table_in, 32)

            def even_unit(i):
                diff_norm(i - NORM)
                if i < len(UNITS):
                    t, diff, hd, m = UNITS[i]
                    n, w = TOK[t][1], SEEN[t]
                    dve.wait_ge(u_s_done, i + 1)
                    wait(dve, u_exp, i - 1)
                    mask = alibi[0:n, hd, t, 0:w] if diff else mask2[0:n, t, 0:w]
                    V.tensor_tensor_reduce(s2[0:n, i % 2, 0:w], ps[score_bank(i)][0:n, 0:w], mask, -SC2, 3.0e38,
                                           ALU.add, ALU.min, small[0:n, i, 1:2]).then_inc(u_max, 1)
                if 1 <= i <= len(UNITS):
                    u = i - 1
                    t, diff, hd, m = UNITS[u]
                    n, w = TOK[t][1], SEEN[t]
                    pu, inv = p2[0:n, u % P2, 0:w], small[0:n, u, 3:4]
                    dve.wait_ge(u_exp, u + 1)
                    link(V.reciprocal(inv, small[0:n, u, 2:3]))
                    if diff and m == 1:
                        link(V.tensor_tensor(inv, inv, neg_lam[0:n, :], ALU.mult))
                        dve.wait_ge(u_alone, ORDER[u] + 1)
                        V.scalar_tensor_tensor(pu, pu, inv, p2[0:n, (u - 1) % P2, 0:w], ALU.mult, ALU.add).then_inc(u_pn, 1)
                    else:
                        V.tensor_scalar(pu, pu, inv, None, ALU.mult).then_inc(u_alone if diff else u_pn, 1)

            sub_gain = small[:, 63, 0:1]
            V.tensor_scalar(sub_gain, c2("diff_subln_g_2", 0), 1.0 - LAM_INIT, None, ALU.mult).then_inc(gain_ready, 1)

            def diff_norm(n):
                if 0 <= n - 3 < 4:
                    hd = n - 3
                    dve.wait_ge(gain_ready, 1)
                    dve.wait_ge(oarstd, hd + 1)
                    V.scalar_tensor_tensor(oa[:, hd, :], oa[:, hd, :], sub_gain, oasq[:, hd, :], ALU.mult, ALU.mult).then_inc(oan, 1)

            def evacuate(c):
                if 2 <= c < 6:
                    qk_low(c + 2, 1)
                else:
                    dve.wait_ge(mm_done, CHUNK_END[C0["even_v0"] + c])
                    value_tiles(ve, 2 * (c % 2), c if c < 2 else c - 4, ve_ready)

            for c in range(8):
                for k, i in enumerate(WITH[c]):
                    even_unit(i)
                    if c >= 1 and k == EVAC_AT:
                        evacuate(c - 1)
                    for half in range(2):
                        if c >= 1 and k == LO_AT[half]:
                            split_at(C0["even_v0"] + c + 1, (half,))
            evacuate(7)
            for i in range(ALONE, len(UNITS) + V_LAG):
                even_unit(i)
            split_at(C0["even_out"] + 1)

            def layer_var(n, j, cols, between=None):
                dve.wait_ge(mu_ready, j + 1)
                V.scalar_tensor_tensor(var[:, cols], ps[4][:, 0:size(cols)], 1.0 / D, musq[:, cols], ALU.mult, ALU.subtract).then_inc(var_ready, 1)
                if between is not None:
                    between()
                dve.wait_ge(rstd_ready, n + 1)

            def layer_apply(n, j, k, cols):
                V.tensor_tensor(y[:, at(k), cols], y[:, at(k), cols], mu[:, cols], ALU.add).then_inc(sub_ready, 1)
                dve.wait_ge(sub_ready, KD * j + k + 1)
                V.tensor_tensor(y[:, at(k), cols], y[:, at(k), cols], rstd[:, n % 3, cols], ALU.mult).then_inc(norm_ready, 1)

            def raw_tiles(event, bank, slot, n, done, used, cols):
                w = size(cols)
                dve.wait_ge(mm_done, event)
                wait(dve, raw_ready, done)
                for m in range(2):
                    V.scalar_tensor_tensor(ta[:, m, cols], mu[:, cols], ps[bank + m][:, w:w + 1], ps[bank + m][:, 0:w], ALU.mult, ALU.add).then_inc(raw_sub, 1)
                wait(dve, *used)
                for m in range(2):
                    ins = V.tensor_copy(b_col[:, slot + m:slot + m + 1], ps[bank + m][:, w + 1:w + 2])
                ins.then_inc(raw_out, 1)
                for m in range(2):
                    dve.wait_ge(raw_sub, done + m + 1)
                    V.tensor_tensor(rw[:, slot + m, cols], ta[:, m, cols], rstd[:, n % 3, cols], ALU.mult).then_inc(raw_ready, 1)

            def ffn_up(name, base, j, cols):
                raw0 = base + (16 if j else 0)

                def turn(i):
                    for u in range(2):
                        start = u == 0 and is_first(i)
                        if start:
                            layer_var(S_LN + j, j, cols, lambda: split_at(C0[name] + 2, (0,)))
                        t = 4 * i + 2 * u
                        raw_tiles(E0[name] + 2 * i + u + 1, 2 * ((P0[name] + u) % 2), 2 * u, S_LN + j, raw0 + t, (relu_ready, base + t - 2), cols)
                        if start:
                            split_at(C0[name] + 2, (1,))
                        else:
                            split_in(name, i, 2, u)
                    layer_apply(S_LN + j, j, i, cols)

                repeat(dve, 8, turn)

            residual(S_LN, "even_out", 1, 0, X_LN0, ALL)
            ffn_up("ffn_up0", 0, 0, ALL)
            residual(S_LN + 1, "ffn_down0", 4, 1, X_LN1, ALL)
            low = 0
            for c in range(8):
                if c == 0:
                    layer_var(S_LN + 1, 1, ALL, lambda: split_at(C0["ret_qk"] + 2, (0,)))
                raw_tiles(E0["ret_qk"] + c + 1, 2 * ((P0["ret_qk"] + c) % 2), 2 * (c % 2), S_LN + 1, FT2 + 2 * c, (rqk_ready, 2 * c - 2),
                          LAST if c < 4 else ALL)
                split_at(C0["ret_qk"] + c + 2, (0, 1) if c else (1,))
                for k in RET_TILES[c]:
                    layer_apply(S_LN + 1, 1, k, ALL)
                for k in RET_TILES[c - 1] if c else ():
                    x_low(X_RET, k, h[:, k, :], cols=ALL)

            def ret_value_tiles(j, u):
                dve.wait_ge(vt_done, j + 1)
                for t in range(3):
                    n = TOK[t][1]
                    V.tensor_copy(rv[0:n, t, at(256 * j, 256)], ps[4 + 2 * u + t // 2][0:n, 256 * (t % 2):256 * (t % 2) + 256]).then_inc(rv_ready, 1)

            def ret_values(i):
                for u in range(2):
                    if u == 1 or not is_first(i):
                        ret_value_tiles(2 * i + u - 1, 1 - u)
                    if u == 0 or not is_last(i):
                        split_in("ret_v", i, 2, u)

            is_last = lambda i: isinstance(i, int) and i == 3
            repeat(dve, 3, ret_values)
            ret_values(3)
            dve.wait_ge(decay_in, 16)
            def ret_decay(hd):
                for st in range(3):
                    t0, sn = TOK[st]
                    u = 3 * hd + st
                    dve.wait_ge(rs_done, u + 1)
                    if st == 0 and hd >= 2:
                        dve.wait_ge(ro_done, 4 * (hd - 1))
                    t0 = max(t0, META)
                    V.tensor_tensor(rs[0:sn, hd % 2, st, t0:N2], ps[4 + u % 2][0:sn, t0:N2], decay[0:sn, hd, st, t0:N2], ALU.mult).then_inc(rs_ready, 1)

            def ret_norm(hd):
                dve.wait_ge(r_rstd_ready, hd + 1)
                for q in range(4):
                    ins = V.tensor_tensor(rqk[:, hd, q, LAST], rqk[:, hd, q, LAST], r_rstd[:, LAST], ALU.mult)
                ins.then_inc(ron_ready, 1)

            ret_decay(0)
            ret_value_tiles(7, 1)
            ret_decay(1)
            split_in("ret_v", 3, 2, 1)
            for hd in range(RH):
                for q in range(4):
                    n = 4 * hd + q
                    dve.wait_ge(ro_done, n + 1)
                    V.tensor_copy(rqk[:, hd, q, LAST], ps[6 + n % 2][:, 0:N1]).then_inc(ro_ready, 1)
                if hd + 2 < RH:
                    ret_decay(hd + 2)
                if hd >= 1:
                    ret_norm(hd - 1)
            ret_norm(RH - 1)
            dve.wait_ge(ron_ready, RH)
            o_tiles = rqk[:, :, :, :].rearrange("p h q n -> p (h q) n")

            def ret_gate(i):
                for u in range(2):
                    for m in range(2):
                        t = 4 * i + 2 * u + m
                        dve.wait_ge(silu2_ready, t + 1)
                        if not is_first(i):
                            dve.wait_ge(y_ready, t - 3)
                        V.tensor_tensor(fa[:, 2 * u + m, LAST], ra[:, 2 * u + m, LAST], o_tiles[:, at(t), LAST], ALU.mult).then_inc(y_mul, 1)
                    split_in("ret_g", i, 2, u)

            repeat(dve, 4, ret_gate)
            residual(S_LN + 2, "ret_out", 2, 2, X_LN2, LAST)
            ffn_up("ffn_up1", FT2, 2, LAST)
            residual(S_LN + 3, "ffn_down1", 4, 3, 0, LAST)
            layer_var(S_LN + 3, 3, LAST)
            for k in range(KD + 1):
                if k < KD:
                    V.tensor_tensor(y[:, k, LAST], y[:, k, LAST], mu[:, LAST], ALU.add).then_inc(sub_ready, 1)
                if k >= 1:
                    dve.wait_ge(sub_ready, KD * 3 + k)
                    V.tensor_tensor(y[:, k - 1, LAST], y[:, k - 1, LAST], rstd[:, (S_LN + 3) % 3, LAST], ALU.mult).then_inc(norm_ready, 1)
            for n in range(4):
                half, t = n // 2, n % 2
                dve.wait_ge(ot_done, n + 1)
                V.tensor_copy(otok[:, t, 512 * half:512 * half + 512], ps[2 * t + half][:, :]).then_inc(ot_ready, 1)

        @block.tensor
        def _(pe):
            T = nc.tensor
            rows_x, rows_q, rows_r, rows_f, rows_g = (xh, xl), (qxh, qxl), (xrh, xrl), (fh, fl), (gh, gl)

            def three(dst, w, x, first, last):
                T.matmul(dst, w[0], x[0], start=first, stop=False)
                T.matmul(dst, w[0], x[1], start=False, stop=False)
                return T.matmul(dst, w[1], x[0], start=False, stop=last)

            def tile(slot, at0, n):
                return whi[:, slot, at0:at0 + n], wlo[:, slot, at0:at0 + n]

            def product(c, slot, outs, x, at_x, cols, kt=KD, k0=0, first=True, last=True, ready=None, order=None):
                order = order or range(kt)
                halves = 0
                for n, k in enumerate(order):
                    half = 1 if (k + 1) * cols <= CH // 2 else 2
                    if half > halves:
                        pe.wait_ge(w_lo_ready, 2 * c + half)
                        halves = half
                    if ready is not None:
                        ready(k0 + k)
                    for dst, col, m in outs:
                        ins = three(dst, tile(slot, k * cols + col, m), [v[:, k0 + k, at_x] for v in x],
                                    first and n == 0, last and n == kt - 1)
                return ins

            def pair(name, u, width):
                b = 2 * ((P0[name] + u) % 2)
                return [(ps[b + m][:, 0:width], P * m, P) for m in range(2)]

            def x_from(base):
                return lambda k: pe.wait_ge(x_ready, base + k + 1)

            def f_from(base):
                return lambda k: pe.wait_ge(f_ready, base + k + 1)

            def outputs(name, turns, at_x, x, ready, free, per_pair, behind=None, first=0):
                def turn(i):
                    for u in range(2):
                        j = first + 2 * i + u
                        wait(pe, free, per_pair(j - 2))
                        start = u == 0 and is_first(i)
                        product(C0[name] + j, (C0[name] + u) % 2, pair(name, u, size(at_x)), x, at_x, 256,
                                ready=ready if start else None).then_inc(mm_done, 1)
                        if start and behind is not None:
                            behind()
                repeat(pe, turns, turn)

            def outputs_deep(name, n, at_x, x, depth, ready, behind=None):
                kts = [min(8, depth - 8 * j) for j in range((depth + 7) // 8)]
                with pe.Fori(0, 2) as i:
                    for u in range(2):
                        pe.wait_ge(tile_ready, TILES[n] + 4 * i + 2 * u - 2)
                        for q, kt in enumerate(kts):
                            k = len(kts) * u + q
                            product(C0[name] + 2 * len(kts) * i + k, (C0[name] + k) % 2, pair(name, u, size(at_x)), x, at_x, 256, kt=kt,
                                    k0=8 * q, first=q == 0, last=q == len(kts) - 1, ready=ready if u == 0 else None).then_inc(mm_done, 1)
                        if u == 0 and behind is not None:
                            behind()

            def stat(n, cols=None):
                pe.wait_ge(acc_ready, ACC0[n] + SUMMED[n])
                rest = range(SUMMED[n], KD)
                at_x = cols or TOK1
                sums = [(ps[5], acc1, lambda k: y[:, k, cols])] if cols is not None else []
                sums.append((ps[4], acc2, lambda k: sq[:, k % 2, at_x]))
                for bank, total, _ in sums:
                    ins = T.matmul(bank[:, 0:size(at_x)], ones[:, :], total[:, at_x], start=True, stop=not rest)
                for k in rest:
                    pe.wait_ge(sq_ready, KD * n + k + 1)
                    for bank, _, tiles in sums:
                        ins = T.matmul(bank[:, 0:size(at_x)], ones[:, :], tiles(k), start=False, stop=k == KD - 1)
                ins.then_inc(stat_ready, 1)

            TOK1 = slice(0, N1)
            pe.wait_ge(ident_in, 16)
            pe.wait_ge(x_in, 32)
            for k in range(KD):
                if k == 1:
                    pe.wait_ge(g_in, 16)
                    T.transpose(ps[0][:, 0:KD], g_rows[:, :], ident[0:KD, 0:KD]).then_inc(cols_t, 1)
                wait(pe, tile_ready, k - 3)
                for t in range(2):
                    ins = T.transpose(ps[4 + k % 4][:, P * t:P * t + P], xt[:, t, P * k:P * k + P], ident[:, :])
                ins.then_inc(xt_done, 1)
            pe.wait_ge(cols_ready, 1)

            def others():
                pe.wait_ge(small_in, 16 * (len(ROWS2) + 3))
                T.transpose(ps[7][:, 0:R2N], rows2[:, :], ident[0:R2N, 0:R2N])
                pe.wait_ge(rows1_in, 16 * len(ROWS1))
                T.transpose(ps[7][:, 2 * P:2 * P + R1N], rows1[:, :], ident[0:R1N, 0:R1N])
                for m in range(CT):
                    ins = T.transpose(ps[7][:, P + TAPS * m:P + TAPS * m + TAPS], cw_rows[:, P * m:P * m + P], ident[0:TAPS, 0:TAPS])
                ins.then_inc(cols_t, 1)
                for k in range(KD):
                    ins = T.transpose(ps[5][:, META * k:META * k + META], meta_rows[:, P * k:P * k + P], ident[0:META, 0:META])
                ins.then_inc(meta_done, 1)
                pe.wait_ge(pos_in, 48)
                for kt in range(2):
                    for t in range(2):
                        ins = T.transpose(ps[6][:, N1 * kt + P * t:N1 * kt + P * t + P], pt[:, t, P * kt:P * kt + P], ident[:, :])
                ins.then_inc(pt_done, 1)

            for j in range(3):
                if j == 2:
                    pe.wait_ge(qkv_ready, 2)
                outs = pair("qkv_in", j, N1)
                if j == 2:
                    outs[1] = (outs[1][0][0:QHEAD], NOPE, QHEAD)
                product(C0["qkv_in"] + j, (C0["qkv_in"] + j) % 2, outs, rows_x, TOK1, 256 if j < 2 else P + ROPE,
                        ready=x_from(X_A) if j == 0 else None).then_inc(mm_done, 1)
                if j == 0:
                    pe.wait_ge(tile_ready, KD)
                    stat(S_X)
                    others()
            for m in range(CT):
                pe.wait_ge(qkv_ready, 4 + 2 * m) if m < 2 else pe.wait_ge(g_scaled, m - 1)
                product(C0["conv_in"] + m, (C0["conv_in"] + m) % 2, pair("conv_in", m, N1), rows_x, TOK1, 256).then_inc(mm_done, 1)
                if m == 0:
                    pe.wait_ge(qkv_ready, 6)
                    pe.wait_ge(meta_ready, 1)
                    pe.wait_ge(const_in, 32)
                    T.matmul(ps[5][0:QHEAD, 0:N1], rot[:, :], qkv[0:QHEAD, 5, :], start=True, stop=True).then_inc(krot_done, 1)
                    pe.wait_ge(p_ready, 1)
                    pe.wait_ge(cols_ready, 3)
                    for t in range(5):
                        j, n = (0, t) if t < 3 else (1, t - 3)
                        pe.wait_ge(sq6_ready, t + 1)
                        ins = T.matmul(ps[6 + j][:, 0:N1], ones[:, :], sq6[:, t, :], start=n == 0, stop=n == (2, 1)[j])
                        if n == (2, 1)[j]:
                            ins.then_inc(lstat_ready, 1)
            for j in range(4):
                c = C0["q"] + j // 2
                pe.wait_ge(g_scaled, 3 + j) if j < 2 else pe.wait_ge(q_ready, j - 1)
                outs = [(ps[2 * ((P0["q"] + j) % 2) + m][0:QHEAD, 0:N1], QHEAD * (2 * (j % 2) + m), QHEAD) for m in range(2)]
                product(c, c % 2, outs, rows_q, TOK1, 4 * QHEAD, kt=3, ready=x_from(X_QKV) if j == 0 else None).then_inc(mm_done, 1)
            pe.wait_ge(lrstd_ready, 2)
            pe.wait_ge(krope_mul, 1)

            def conv_taps(first, last):
                for tap in range(first, min(TAPS, last)):
                    if tap == 0:
                        pe.wait_ge(conv_in_ready, CT)
                    pe.wait_ge(diag_ready, tap + 1)
                    ins = T.matmul(ps[7][:, 0:N1], diag[tap], conv_in[:, CT - 1, tap:tap + N1], start=tap == 0, stop=tap == TAPS - 1)
                    if tap == TAPS - 1:
                        ins.then_inc(conv_pe, 1)

            conv_taps(0, 6)
            c = C0["kv"]
            for j in range(4):
                pe.wait_ge(q_ready, 3 + j) if j < 2 else pe.wait_ge(k_ready, j - 1)
                outs = [(ps[2 * ((P0["kv"] + j) % 2) + m][:, 0:N1], P * (2 * j + m), P) for m in range(2)]
                product(c, c % 2, outs, rows_q, TOK1, D, kt=2, k0=3, ready=x_from(X_QKV)).then_inc(mm_done, 1)
                pe.wait_ge(q_ready, j + 1)
                if j == 3:
                    pe.wait_ge(qrope_ready, 1)
                T.matmul(ps[QROT[j]][0:QHEAD, :], rot[:, :], qt[0:QHEAD, 2 * j:2 * j + 2, :], start=True, stop=True).then_inc(qrot_done, 1)
            pe.wait_ge(k_ready, 3)
            b = 2 * ((P0["kv"] + 4) % 2)
            for t in range(2):
                for k in range(2):
                    wv = [v[:, c % 2, D * k:D * k + D].rearrange("p (h c) -> p h c", c=P)[:, :, NOPE:] for v in (whi, wlo)]
                    xv = [v[:, 3 + k, P * t:P * t + P] for v in rows_q]
                    ins = three(ps[b + t][:, :], xv, wv, k == 0, k == 1)
            ins.then_inc(mm_done, 1)
            pe.wait_ge(k_ready, 4)
            pe.wait_ge(v_ready, 2)
            pe.wait_ge(krope_ready, 1)
            def scores(i):
                t, hd = i // 8, i % 8
                wait(pe, max_ready, i - 2)
                if i < 8:
                    pe.wait_ge(qrope_ready, max(min(2 + i, 4), i // 2 + 1))
                T.matmul(ps[SCORES[i % 3]][:, 0:P * (t + 1)], qt[0:QHEAD, hd, P * t:P * t + P], kt_[0:QHEAD, hd, 0:P * (t + 1)],
                         start=True, stop=True).then_inc(s_done, 1)

            def conv_sums(n):
                m = STAT_ORDER[n]
                pe.wait_ge(max_ready, 16)
                pe.wait_ge(csq_ready, n + 1)
                T.matmul(ps[4][:, 0:N1], ones[:, :], cv[:, m, :], start=n == 0, stop=n == CT - 1)
                ins = T.matmul(ps[5][:, 0:N1], ones[:, :], sq6[:, m, :], start=n == 0, stop=n == CT - 1)
                if n == CT - 1:
                    ins.then_inc(cstat_ready, 1)

            scores(0)
            for i in range(16 + 4):
                if i + 1 < 16:
                    scores(i + 1)
                if 3 <= i < 19:
                    u = i - 3
                    pe.wait_ge(pn_ready, u + 1)
                    wait(pe, pT_ready, u - 1)
                    for b in range(u // 8 + 1):
                        ins = T.transpose(ps[u % 2][:, P * b:P * b + P], p1[:, u % 4, P * b:P * b + P], ident[:, :])
                    ins.then_inc(t_done, 1)
                if i >= 4:
                    u = i - 4
                    t, hd, g, s = u // 8, u % 8, u // 2, u % 2
                    pe.wait_ge(pT_ready, u + 1)
                    wait(pe, o_ready, g - 1)
                    for b in range(t + 1):
                        ins = T.matmul(ps[2 + g % 2][64 * s:64 * s + 64, 0:P], v1[:, b, VDIM * hd:VDIM * hd + VDIM], pt1[:, u % 2, b, :],
                                       start=b == 0, stop=b == t)
                    ins.then_inc(pv_done, 1)
                conv_taps(6 + 2 * i, 8 + 2 * i)
            for n in range(2):
                conv_sums(n)
            for n in range(2, CT):
                conv_sums(n)
            def mixed(k):
                pe.wait_ge(o_ready, 4 + k + 1) if k < 4 else pe.wait_ge(c_ready, k - 3)

            pe.wait_ge(lam_one, 1)
            pe.wait_ge(pT_ready, 16)
            T.matmul(ps[6][:, 0:1], ones[0:1, :], lam_s[:, 4:5], start=True, stop=True).then_inc(lam_done, 1)
            c = C0["mix_out"]
            for tiles in (range(4), range(4, KD)):
                for j in range(2):
                    ins = product(c + j, (c + j) % 2, pair("mix_out", j, N1), rows_x, TOK1, 256, kt=4, order=tiles,
                                  first=tiles[0] == 0, last=tiles[0] == 4, ready=mixed)
                    if tiles[0] == 4:
                        ins.then_inc(mm_done, 1)
            for j in (2, 3):
                pe.wait_ge(tile_ready, TILES[S_MIX] + 2 * j - 2)
                product(c + j, (c + j) % 2, pair("mix_out", j, N1), rows_x, TOK1, 256).then_inc(mm_done, 1)
            pe.wait_ge(p_ready, 1)
            pe.wait_ge(w_lo_ready, 2 * (C0["ple"] + 1))
            for j in range(4):
                pe.wait_ge(tile_ready, TILES[S_MIX] + 6 + 2 * j) if j < 2 else pe.wait_ge(e_copied, j - 1)
                b = 2 * ((P0["ple"] + j) % 2)
                for k in range(2):
                    for m in range(2):
                        ins = three(ps[b + m][:, 0:N1], tile(C0["ple"] % 2, D * k + N1 * j + P * m, P), (ph[:, k, :], pl[:, k, :]), k == 0, k == 1)
                ins.then_inc(mm_done, 1)
                if j == 1:
                    stat(S_MIX)
            pe.wait_ge(e_late, 2)
            outputs("gate_up", FT // 2, TOK1, rows_x, x_from(X_FFN), gv_scaled, lambda j: j + 1, behind=lambda: stat(S_PRE))
            kts = (8, 8, 6)
            for j in range(4):
                pe.wait_ge(gv_scaled, FT - 1 + j) if j < 2 else pe.wait_ge(tile_ready, TILES[S_FFN] + 2 * j - 2)
                for q, kt in enumerate(kts):
                    c = C0["down"] + 3 * j + q
                    product(c, c % 2, pair("down", j, N1), rows_f, TOK1, 256, kt=kt, k0=8 * q, first=q == 0, last=q == 2,
                            ready=f_from(0) if j == 0 else None).then_inc(mm_done, 1)
                if j == 1:
                    stat(S_E)
            stat(S_FFN)
            outputs("ple_gate", 2, TOK1, rows_x, x_from(X_PLE), sig_ready, lambda j: 2 * j + 2)
            outputs("even_dqk", 2, ALL, rows_r, x_from(X_B), qk_ready, lambda j: 2 * j + 2)

            def value_products(c, slot, b, x):
                for q0, bank, c0 in ((0, b, 0), (TOK[1][0], b, 256), (N2 - P, b + 1, 0)):
                    for k in range(KD):
                        if q0 == 0 and k % 4 == 0:
                            pe.wait_ge(w_lo_ready, 2 * c + 1 + k // 4)
                        yield three(ps[bank][:, c0:c0 + 256], [v[:, k, q0:q0 + P] for v in x], tile(slot, 256 * k, 256), k == 0, k == KD - 1)

            def qk_products(c, slot, b, x):
                for k in range(KD):
                    if k % 4 == 0:
                        pe.wait_ge(w_lo_ready, 2 * c + 1 + k // 4)
                    for m in range(2):
                        yield three(ps[b + m][:, 0:N2], tile(slot, 256 * k + P * m, P), [v[:, k, ALL] for v in x], k == 0, k == KD - 1)

            pe.wait_ge(gates_in, 32)
            for k in range(KD):
                ins = T.matmul(ps[7][0:8, 0:N2], wf[:, k, :], h[:, k, :], start=k == 0, stop=k == KD - 1)
            ins.then_inc(fb_done, 1)
            def scores(i):
                t, diff, hd, m = UNITS[i]
                (q0, n), w = TOK[t], SEEN[t]
                if i == DIFF:
                    pe.wait_ge(qk_ready, 14)
                    pe.wait_ge(q_twice, 12)
                    pe.wait_ge(cum_lo, 2)
                if i == DIFF + 12:
                    pe.wait_ge(qk_ready, 16)
                    pe.wait_ge(q_twice, 16)
                if i == ALONE + 2:
                    pe.wait_ge(ve_ready, 12)
                wait(pe, u_max, i - 1 if i < ALONE + 2 else i - 2)
                s = ps[score_bank(i)][0:n, 0:w]
                unit = 2 * hd + m if diff else 8 + hd
                r = slice(64 * (unit % 2), 64 * (unit % 2) + 64)
                T.matmul(s, qs[:, unit, q0:q0 + n], ks[:, unit, 0:w], start=True, stop=False)
                ins = T.matmul(s, ql[r, unit // 2, q0:q0 + n], ks[r, unit, 0:w], start=False, stop=diff)
                if not diff:
                    rows = slice(r.start, r.start + 40)
                    ins = T.matmul(s, sel[rows, hd:hd + 1].broadcast_to([40, n]), fgs[rows, 0:w], start=False, stop=True)
                ins.then_inc(u_s_done, 1)

            def even_unit(i):
                ahead = LEAD[i >= ALONE]
                if i == 0:
                    scores(0)
                if i == ALONE:
                    scores(i + 1)
                if i + ahead < len(UNITS):
                    scores(i + ahead)
                if i >= T_LAG and i - T_LAG in ORDER:
                    t, o = UNITS[i - T_LAG][0], ORDER[i - T_LAG]
                    nq = TOK[t][1]
                    pe.wait_ge(u_pn, o + 1)
                    wait(pe, u_out if out_bank(o - 2)[0] == 6 + o % 2 else u_pT, o - 1)
                    for b in range(t + 1):
                        k0, kn = TOK[b]
                        ins = T.transpose(ps[6 + o % 2][0:kn, P * b:P * b + nq], p2[0:nq, (i - T_LAG) % P2, k0:k0 + kn], ident[0:nq, 0:nq])
                    ins.then_inc(u_t_done, 1)
                if i >= V_LAG and i - V_LAG in ORDER:
                    t, diff, hd, m = UNITS[i - V_LAG]
                    o, nq = ORDER[i - V_LAG], TOK[UNITS[i - V_LAG][0]][1]
                    pe.wait_ge(u_pT, o + 1)
                    if o in VALUES:
                        pe.wait_ge(ve_ready, VALUES[o])
                    if diff:
                        r, v0, vn = slice(0, P), P * hd, P
                    else:
                        r, v0, vn = slice(64 * (hd % 2), 64 * (hd % 2) + 64), 512 + 64 * hd, 64
                    bank, c0 = out_bank(o)
                    if bank < 4:
                        pe.wait_ge(u_out, o - 1)
                    dst = ps[bank][r, c0:c0 + nq]
                    for b in range(t + 1):
                        kn = TOK[b][1]
                        ins = T.matmul(dst, ve[0:kn, b, v0:v0 + vn], pt2[o % PT2][0:kn, b, 0:nq], start=b == 0, stop=b == t)
                    ins.then_inc(u_pv, 1)
                hd = i - NORM - 1
                if 0 <= hd < 4:
                    pe.wait_ge(oasq_ready, hd + 1)
                    wait(pe, oarstd, hd)
                    T.matmul(ps[1][:, 0:N2], ones[:, :], oasq[:, hd, :], start=True, stop=True).then_inc(oastat, 1)

            VALUES = {0: 3, 2: 6, 12: 9, 24: 12}
            freed = [(qk_ready, 6), (qk_ready, 8), (ve_ready, 3), (ve_ready, 6), (qk_ready, 10), (qk_ready, 12), (qk_ready, 14), (qk_ready, 16)]
            pe.wait_ge(fz_ready, 1)
            pe.wait_ge(q_twice, 8)
            pe.wait_ge(qk_ready, 8)
            for c in range(8):
                chunk = C0["even_v0"] + c
                pe.wait_ge(*freed[c])
                steps, products = (2 * KD, qk_products) if 2 <= c < 6 else (3 * KD, value_products)
                for n, ins in enumerate(products(chunk, chunk % 2, 2 * (c % 2), rows_r)):
                    if n + 1 == steps:
                        ins.then_inc(mm_done, 1)
                    for k, i in enumerate(WITH[c]):
                        if n + 1 == steps * (k + 1) // len(WITH[c]):
                            even_unit(i)
            for i in range(ALONE, len(UNITS) + V_LAG):
                even_unit(i)
            pe.wait_ge(u_max, len(UNITS))
            pe.wait_ge(oarstd, 4)

            def even_mix(k):
                pe.wait_ge(oa_lo, k + 1) if k < 4 else pe.wait_ge(u_flo, k - 3)

            for j in range(4):
                wait(pe, tile_ready, TILES[S_LN] + 2 * (j - 1) if j >= 2 else 0)
                product(C0["even_out"] + j, (C0["even_out"] + j) % 2, pair("even_out", j, N2), rows_x, ALL, 256,
                        ready=even_mix if j == 0 else None).then_inc(mm_done, 1)

            def raw(cols):
                return slice(cols.start, N2 + 2)

            def mlp(j, layer, x0, raw0, hidden0, cols):
                outputs(f"ffn_up{layer}", FT2 // 4, raw(cols), rows_r, x_from(x0), raw_out,
                        lambda t: raw0 + t + 1 if not isinstance(t, int) or t >= 0 else 0, behind=lambda: stat(S_LN + j, cols))
                pe.wait_ge(raw_out, raw0 + FT2 // 2 - 1)
                outputs_deep(f"ffn_down{layer}", S_LN + j + 1, cols, rows_f, FT2, f_from(hidden0),
                             behind=lambda: pe.wait_ge(raw_out, raw0 + FT2 // 2))

            mlp(0, 0, X_LN0, 0, FT, ALL)
            raw_from = lambda j: FT2 // 2 + j + 1
            outputs("ret_qk", 2, raw(LAST), rows_r, x_from(X_LN1), raw_out, raw_from, behind=lambda: stat(S_LN + 1, ALL))
            outputs("ret_qk", 2, raw(ALL), rows_r, None, raw_out, raw_from, first=4)
            def value_turn(j, u):
                pe.wait_ge(vt_ready, 2 * j + 2)
                wait(pe, rv_ready, 3 * (j - 1))
                for m in range(2):
                    for t, (q0, n) in enumerate(TOK):
                        ins = T.transpose(ps[4 + 2 * u + t // 2][0:n, 256 * (t % 2) + P * m:256 * (t % 2) + P * m + P],
                                          fa[:, 2 * u + m, q0:q0 + n], ident[:, :])
                ins.then_inc(vt_done, 1)

            def ret_values(i):
                for u in range(2):
                    j = 2 * i + u
                    if is_first(i):
                        pe.wait_ge(raw_out, FT2 // 2 + 7 + u)
                    else:
                        pe.wait_ge(vt_ready, 2 * j - 2)
                    for tiles in (range(4), range(4, KD)):
                        ins = product(C0["ret_v"] + j, (C0["ret_v"] + u) % 2, pair("ret_v", u, N2), rows_x, ALL, 256, kt=4, order=tiles,
                                      first=tiles[0] == 0, last=tiles[0] == 4, ready=x_from(X_RET) if u == 0 and is_first(i) else None)
                        if tiles[0] == 4:
                            ins.then_inc(mm_done, 1)
                        elif u == 1 or not is_first(i):
                            value_turn(j - 1, 1 - u)

            repeat(pe, 4, ret_values)
            pe.wait_ge(rv_ready, 21)
            pe.wait_ge(rqk_ready, 16)

            def ret_scores(hd):
                for st in range(3):
                    u = 3 * hd + st
                    t0, sn = TOK[st]
                    wait(pe, rs_ready, u - 1)
                    tq = max(t0, META)
                    for kt in range(2):
                        ins = T.matmul(ps[4 + u % 2][0:sn, tq:N2], rqk[:, hd, 2 + kt, t0:t0 + sn], rqk[:, hd, kt, tq:N2], start=kt == 0, stop=kt == 1)
                    ins.then_inc(rs_done, 1)

            def ret_stat(hd):
                pe.wait_ge(rsum_ready, 3 * hd + 3)
                wait(pe, r_rstd_ready, hd - 1)
                T.matmul(ps[RSTAT[hd]][:, 0:N1], ones[:, :], rsum[hd % 2][:, LAST], start=True, stop=True).then_inc(rstat, 1)

            ret_scores(0)
            value_turn(7, 1)
            for hd in range(RH):
                if hd + 1 < RH:
                    ret_scores(hd + 1)
                if hd == 0:
                    pe.wait_ge(rv_ready, 24)
                pe.wait_ge(rs_ready, 3 * hd + 3)
                for q in range(4):
                    n = 4 * hd + q
                    wait(pe, ro_ready, n - 1)
                    for st in range(3):
                        t0, sn = max(TOK[st][0], META), TOK[st][1]
                        ins = T.matmul(ps[6 + n % 2][:, t0 - META:N1], rv[0:sn, st, RV * hd + P * q:RV * hd + P * q + P], rs[0:sn, hd % 2, st, t0:N2],
                                       start=st == 0, stop=st == 2)
                    ins.then_inc(ro_done, 1)
                    if q == 1 and hd >= 1:
                        ret_stat(hd - 1)
            def last_stat():
                ret_stat(RH - 1)
                pe.wait_ge(r_rstd_ready, RH - 1)

            outputs("ret_g", 4, LAST, rows_x, None, silu2_ready, lambda j: 2 * j + 2, behind=last_stat)
            pe.wait_ge(silu2_ready, 14)
            outputs_deep("ret_out", S_LN + 2, LAST, rows_g, 16, lambda k: pe.wait_ge(y_ready, k + 1), behind=lambda: pe.wait_ge(silu2_ready, 16))
            mlp(2, 1, X_LN2, FT2 // 2 + 8, FT + FT2, LAST)
            stat(S_LN + 3, LAST)
            for k in range(KD):
                pe.wait_ge(hn_ready, 3 * KD + k + 1)
                for t in range(2):
                    ins = T.transpose(ps[2 * t + k // 4][:, P * (k % 4):P * (k % 4) + P], h[:, k, META + P * t:META + P * t + P], ident[:, :])
                    if k % 4 == 3:
                        ins.then_inc(ot_done, 1)


INPUTS = ["x", "p", "positions", "g_mix_pre", "w_in", "g_q_a", "w_q_b", "g_kv_a", "w_kv_b", "conv_w", "conv_b", "conv_ln_g",
          "conv_ln_b", "w_o", "g_mix_post", "g_ffn_pre", "w_ffn_gate", "w_ffn_up", "ffn_dw_w", "ffn_dw_b", "w_ffn_down",
          "g_ffn_post", "w_ple_proj", "g_ple", "w_ple_gate", "meta_tokens_2", "even_w_in_2", "even_f_bias_2", "diff_lambda_2",
          "diff_subln_g_2", "even_w_out_2", "ret_w_in_2", "ret_w_out_2", "ln_g_2", "ln_b_2", "ffn_w1_2", "ffn_w2_2"]


def constants():
    c = {"c_ident": np.eye(P)}
    rot = np.zeros((QHEAD, QHEAD))
    half = ROPE // 2
    for m in range(half):
        rot[NOPE + half + m, NOPE + m] = -1.0
        rot[NOPE + m, NOPE + half + m] = 1.0
    c["c_rot"] = rot
    row, col = np.arange(P)[:, None], np.arange(P)[None, :]
    c["c_mask1"] = np.concatenate([np.zeros((P, P)), np.where(col <= row, 0.0, NEG)], axis=1)
    pos = np.arange(N2)
    chunk = (pos + CHUNK - META) // CHUNK
    mask2, alibi, decay = np.zeros((P, 3, N2)), np.zeros((P, 4, 3, N2)), np.zeros((P, 4, 3, N2))
    for t, (q0, n) in enumerate(TOK):
        q = pos[q0:q0 + n]
        mask2[0:n, t] = np.where(pos[None, :] <= q[:, None], 0.0, NEG)
        dist = np.abs(q[:, None] - pos[None, :])
        for hd in range(4):
            slope = 2.0 ** (-8.0 * (hd + 1) / 4)
            alibi[0:n, hd, t] = np.where(chunk[None, :] <= chunk[q][:, None], -slope * dist / SC2, NEG)
            gamma = 1.0 - 2.0 ** (-5.0 - hd)
            decay[0:n, hd, t] = np.where(chunk[q][:, None] <= chunk[None, :], gamma ** dist * RQK ** -0.5, 0.0)
    c["c_mask2"], c["c_alibi"], c["c_decay"] = mask2, alibi, decay
    c["c_freq"] = np.tile(10000.0 ** (-np.arange(0, ROPE, 2) / ROPE), 2)[:, None]
    return {name: np.ascontiguousarray(v.astype(np.float32)) for name, v in c.items()}


def kernel(**inputs):
    import concourse.bacc as bacc
    from concourse.bass_utils import run_bass_kernel_spmd

    nc = bacc.Bacc("TRN2", target_bir_lowering=False, num_devices=1)
    arrays = {name: np.ascontiguousarray(inputs[name]) for name in INPUTS}
    arrays.update(constants())
    a = {name: nc.dram_tensor(name, v.shape, mybir.dt.from_np(v.dtype), kind="ExternalInput").ap() for name, v in arrays.items()}
    out = nc.dram_tensor("result", (1, N1, D), F32, kind="ExternalOutput").ap()
    build(nc, a, out)
    r = run_bass_kernel_spmd(nc, [arrays], core_ids=[0])
    return r.results[0]["result"]
```
